# Optimizing a Trainium2 kernel written in Bass

```python
import math
import jax, jax.numpy as jnp
from jax import lax
import numpy as np

D_MODEL = 1024
BATCH = 1
SEQ = 256
DEPTH = 2

PLE_DIM = 256
NSA_HEADS = 8
NSA_HEAD_DIM = 64
NSA_GROUPS = 2
NSA_Q_PER_GROUP = NSA_HEADS // NSA_GROUPS
CMP_BLOCK = 32
CMP_STRIDE = 16
CMP_HIDDEN = 4 * NSA_HEAD_DIM
SLC_BLOCK = 64
N_SELECT = 16
WINDOW = 512
Q_BLOCK = 128
RET_HEADS = 4
RET_HEAD_DIM = 128
RET_CHUNK = 128
ROPE_BASE = 10000.0
D_FF = 4 * D_MODEL
EPS = 1e-6
MASK_VALUE = -1e30
FORCE_SCORE = 1e4

NSA_Q_W = NSA_HEADS * NSA_HEAD_DIM
NSA_KV_W = NSA_GROUPS * NSA_HEAD_DIM
NSA_GATE_W = 3 * NSA_HEADS
RET_W = RET_HEADS * RET_HEAD_DIM
IN_SPLITS = (NSA_Q_W, NSA_KV_W, NSA_KV_W, NSA_KV_W, NSA_KV_W, NSA_KV_W, NSA_KV_W, NSA_GATE_W,
             RET_W, RET_W, RET_W, RET_W, D_MODEL, D_MODEL)
D_IN = sum(IN_SPLITS)


def split_cols(z, sizes):
    out = []
    off = 0
    for s in sizes:
        out.append(z[..., off:off + s])
        off += s
    return out

def rmsnorm(x, g):
    xf = x.astype(jnp.float32)
    y = xf * lax.rsqrt(jnp.mean(xf * xf, axis=-1, keepdims=True) + EPS)
    return (y * g.astype(jnp.float32)).astype(x.dtype)

def rms_noaffine(x):
    xf = x.astype(jnp.float32)
    return xf * lax.rsqrt(jnp.mean(xf * xf, axis=-1, keepdims=True) + EPS)

def masked_softmax(s, mask):
    s = jnp.where(mask, s, MASK_VALUE)
    m = jnp.max(s, axis=-1, keepdims=True)
    e = jnp.exp(s - m) * mask
    return e / jnp.maximum(jnp.sum(e, axis=-1, keepdims=True), 1e-30)

def rope(x, pos):
    half = x.shape[-1] // 2
    inv = ROPE_BASE ** (-jnp.arange(half, dtype=jnp.float32) / half)
    ang = pos[:, None] * inv[None, :]
    cos = jnp.cos(ang)[:, None, :]
    sin = jnp.sin(ang)[:, None, :]
    x1 = x[..., :half].astype(jnp.float32)
    x2 = x[..., half:].astype(jnp.float32)
    return jnp.concatenate([x1 * cos - x2 * sin, x1 * sin + x2 * cos], axis=-1)

def nsa_mixer(q_in, kc_in, vc_in, ks_in, vs_in, kw_in, vw_in, gate_logits,
              qn_g, kn_g, pos_k, pos_v, w1_k, w2_k, w1_v, w2_v):
    B, S = q_in.shape[:2]
    G, Hg, dh = NSA_GROUPS, NSA_Q_PER_GROUP, NSA_HEAD_DIM
    dtype = q_in.dtype
    scale = dh ** -0.5
    q = rmsnorm(q_in.reshape(B, S, G, Hg, dh).transpose(0, 2, 3, 1, 4), qn_g)

    def kv_heads(z):
        return z.reshape(B, S, G, dh).transpose(0, 2, 1, 3)

    k_c, v_c = kv_heads(kc_in), kv_heads(vc_in)
    k_s, v_s = rmsnorm(kv_heads(ks_in), kn_g), kv_heads(vs_in)
    k_w, v_w = rmsnorm(kv_heads(kw_in), kn_g), kv_heads(vw_in)
    gates = jax.nn.sigmoid(gate_logits.astype(jnp.float32)).reshape(B, S, 3, G, Hg).transpose(0, 3, 4, 1, 2)

    nc = S // CMP_STRIDE
    starts = jnp.arange(nc) * CMP_STRIDE
    idx = jnp.minimum(starts[:, None] + jnp.arange(CMP_BLOCK)[None, :], S - 1)
    cmp_end = starts + CMP_BLOCK - 1

    def compress(z, pos, w1, w2):
        zb = (z[:, :, idx] + pos).reshape(B, G, nc, CMP_BLOCK * dh)
        return jax.nn.gelu(zb @ w1) @ w2

    k_cmp = rmsnorm(compress(k_c, pos_k, w1_k, w2_k), kn_g)
    v_cmp = compress(v_c, pos_v, w1_v, w2_v)

    ns = S // SLC_BLOCK
    n_sel = min(N_SELECT, ns)
    ratio = SLC_BLOCK // CMP_STRIDE
    k_blk = k_s.reshape(B, G, ns, SLC_BLOCK, dh)
    v_blk = v_s.reshape(B, G, ns, SLC_BLOCK, dh)
    b_ix = jnp.arange(B)[:, None, None, None]
    g_ix = jnp.arange(G)[None, :, None, None]

    pad = ((0, 0), (0, 0), (WINDOW, 0), (0, 0))
    k_w_pad = jnp.pad(k_w, pad)
    v_w_pad = jnp.pad(v_w, pad)

    def query_block(c):
        q0 = c * Q_BLOCK
        qc = lax.dynamic_slice_in_dim(q, q0, Q_BLOCK, axis=3)
        gc = lax.dynamic_slice_in_dim(gates, q0, Q_BLOCK, axis=3)
        t = q0 + jnp.arange(Q_BLOCK)

        s = jnp.einsum('bghqd,bgnd->bghqn', qc, k_cmp).astype(jnp.float32) * scale
        p_cmp = masked_softmax(s, cmp_end[None, :] <= t[:, None])
        o_cmp = jnp.einsum('bghqn,bgnd->bghqd', p_cmp.astype(dtype), v_cmp)

        imp = jnp.sum(p_cmp, axis=2).reshape(B, G, Q_BLOCK, ns, ratio)
        imp_blk = jnp.sum(imp, axis=-1) + jnp.pad(imp[..., :-1, -1], ((0, 0), (0, 0), (0, 0), (1, 0)))
        blk = jnp.arange(ns)[None, :]
        cur = (t // SLC_BLOCK)[:, None]
        forced = (blk == 0) | (blk == cur) | (blk == cur - 1)
        score = jnp.where(forced, FORCE_SCORE, imp_blk)
        score = jnp.where(blk > cur, MASK_VALUE, score)
        _, sel = lax.top_k(score, n_sel)
        ks = k_blk[b_ix, g_ix, sel]
        vs = v_blk[b_ix, g_ix, sel]
        kpos = sel[..., None] * SLC_BLOCK + jnp.arange(SLC_BLOCK)
        smask = (kpos <= t[:, None, None]).reshape(B, G, Q_BLOCK, n_sel * SLC_BLOCK)[:, :, None]
        s = jnp.einsum('bghqd,bgqnkd->bghqnk', qc, ks).astype(jnp.float32) * scale
        p_slc = masked_softmax(s.reshape(B, G, Hg, Q_BLOCK, n_sel * SLC_BLOCK), smask)
        o_slc = jnp.einsum('bghqnk,bgqnkd->bghqd',
                           p_slc.reshape(B, G, Hg, Q_BLOCK, n_sel, SLC_BLOCK).astype(dtype), vs)

        kw = lax.dynamic_slice_in_dim(k_w_pad, q0, Q_BLOCK + WINDOW, axis=2)
        vw = lax.dynamic_slice_in_dim(v_w_pad, q0, Q_BLOCK + WINDOW, axis=2)
        wpos = q0 - WINDOW + jnp.arange(Q_BLOCK + WINDOW)
        dist = t[:, None] - wpos[None, :]
        wmask = (dist >= 0) & (dist < WINDOW) & (wpos[None, :] >= 0)
        s = jnp.einsum('bghqd,bgkd->bghqk', qc, kw).astype(jnp.float32) * scale
        p_win = masked_softmax(s, wmask)
        o_win = jnp.einsum('bghqk,bgkd->bghqd', p_win.astype(dtype), vw)

        return gc[..., 0:1] * o_cmp + gc[..., 1:2] * o_slc + gc[..., 2:3] * o_win

    out = lax.map(query_block, jnp.arange(S // Q_BLOCK))
    return out.transpose(1, 0, 4, 2, 3, 5).reshape(B, S, NSA_Q_W).astype(dtype)

def retention(q_in, k_in, v_in, g_in):
    B, S = q_in.shape[:2]
    H, dk, C = RET_HEADS, RET_HEAD_DIM, RET_CHUNK
    dtype = q_in.dtype
    pos = jnp.arange(S, dtype=jnp.float32)
    q = rope(q_in.reshape(B, S, H, dk), pos)
    k = rope(k_in.reshape(B, S, H, dk), pos) * (dk ** -0.5)
    v = v_in.reshape(B, S, H, dk).astype(jnp.float32)
    nch = S // C

    def chunks(z):
        return z.reshape(B, nch, C, H, dk).transpose(0, 3, 1, 2, 4)

    qc, kc, vc = chunks(q), chunks(k), chunks(v)
    gamma = 1.0 - 2.0 ** (-5.0 - jnp.arange(H, dtype=jnp.float32))
    lg = jnp.log(gamma)
    n = jnp.arange(C, dtype=jnp.float32)
    diff = n[:, None] - n[None, :]
    decay = jnp.where(diff >= 0, jnp.exp(lg[:, None, None] * jnp.maximum(diff, 0.0)), 0.0)
    xi = jnp.exp(lg[:, None] * (n + 1.0))[None, :, None, :, None]
    zeta = jnp.exp(lg[:, None] * (C - 1.0 - n))[None, :, None, :, None]
    g_chunk = jnp.exp(lg * C)[None, :, None, None]

    inner = jnp.einsum('bhcnd,bhcmd->bhcnm', qc, kc) * decay[None, :, None]
    inner = jnp.einsum('bhcnm,bhcme->bhcne', inner, vc)
    kv = jnp.einsum('bhcmd,bhcme->cbhde', kc * zeta, vc)

    def step(R, kv_c):
        return g_chunk * R + kv_c, R

    _, R_prev = lax.scan(step, jnp.zeros((B, H, dk, dk), jnp.float32), kv)
    cross = jnp.einsum('bhcnd,cbhde->bhcne', qc * xi, R_prev)
    y = rms_noaffine(inner + cross)
    y = y.transpose(0, 2, 3, 1, 4).reshape(B, S, RET_W)
    return (jax.nn.silu(g_in.astype(jnp.float32)) * y).astype(dtype)

def first_inputs(seed: int = 0) -> dict:
    key = jax.random.key(seed)
    ks = jax.random.split(key, 21)
    f32 = jnp.float32

    def nrm(k, shape, scale):
        return jax.random.normal(k, shape, f32) * scale

    def gain(k, shape):
        return 1.0 + 0.1 * jax.random.normal(k, shape, f32)

    dh = NSA_HEAD_DIM
    return {
        "x": nrm(ks[0], (BATCH, SEQ, D_MODEL), 1.0),
        "p": nrm(ks[1], (DEPTH, BATCH, SEQ, PLE_DIM), 1.0),
        "norm_mix": gain(ks[2], (DEPTH, D_MODEL)),
        "w_in": nrm(ks[3], (DEPTH, D_MODEL, D_IN), D_MODEL ** -0.5),
        "nsa_q_norm": gain(ks[4], (DEPTH, dh)),
        "nsa_k_norm": gain(ks[5], (DEPTH, dh)),
        "cmp_pos_k": nrm(ks[6], (DEPTH, CMP_BLOCK, dh), 0.1),
        "cmp_pos_v": nrm(ks[7], (DEPTH, CMP_BLOCK, dh), 0.1),
        "cmp_w1_k": nrm(ks[8], (DEPTH, CMP_BLOCK * dh, CMP_HIDDEN), (CMP_BLOCK * dh) ** -0.5),
        "cmp_w2_k": nrm(ks[9], (DEPTH, CMP_HIDDEN, dh), CMP_HIDDEN ** -0.5),
        "cmp_w1_v": nrm(ks[10], (DEPTH, CMP_BLOCK * dh, CMP_HIDDEN), (CMP_BLOCK * dh) ** -0.5),
        "cmp_w2_v": nrm(ks[11], (DEPTH, CMP_HIDDEN, dh), CMP_HIDDEN ** -0.5),
        "w_up_nsa": nrm(ks[12], (DEPTH, NSA_Q_W, D_MODEL), NSA_Q_W ** -0.5),
        "w_up_ret": nrm(ks[13], (DEPTH, RET_W, D_MODEL), RET_W ** -0.5),
        "w_out": nrm(ks[14], (DEPTH, D_MODEL, D_MODEL), D_MODEL ** -0.5),
        "norm_mlp": gain(ks[15], (DEPTH, D_MODEL)),
        "w_ff1": nrm(ks[16], (DEPTH, D_MODEL, D_FF), D_MODEL ** -0.5),
        "w_ff2": nrm(ks[17], (DEPTH, D_FF, D_MODEL), D_FF ** -0.5),
        "norm_ple": gain(ks[18], (DEPTH, D_MODEL)),
        "w_ple": nrm(ks[19], (DEPTH, PLE_DIM, D_MODEL), PLE_DIM ** -0.5),
        "w_ple_gate": nrm(ks[20], (DEPTH, D_MODEL, D_MODEL), D_MODEL ** -0.5),
    }

def first_block(x, p, norm_mix, w_in, nsa_q_norm, nsa_k_norm, cmp_pos_k, cmp_pos_v,
              cmp_w1_k, cmp_w2_k, cmp_w1_v, cmp_w2_v, w_up_nsa, w_up_ret, w_out,
              norm_mlp, w_ff1, w_ff2, norm_ple, w_ple, w_ple_gate):
    for i in range(DEPTH):
        h = rmsnorm(x, norm_mix[i])
        z = h @ w_in[i]
        (q_a, kc, vc, ks_, vs_, kw, vw, g_nsa, rq, rk, rv, rg, merge_a, merge_b) = split_cols(z, IN_SPLITS)
        y_a = nsa_mixer(q_a, kc, vc, ks_, vs_, kw, vw, g_nsa, nsa_q_norm[i], nsa_k_norm[i],
                        cmp_pos_k[i], cmp_pos_v[i], cmp_w1_k[i], cmp_w2_k[i], cmp_w1_v[i], cmp_w2_v[i]) @ w_up_nsa[i]
        y_b = retention(rq, rk, rv, rg) @ w_up_ret[i]
        mix = jax.nn.sigmoid(merge_a) * y_a + jax.nn.sigmoid(merge_b) * y_b
        x = x + mix @ w_out[i]
        h = rmsnorm(x, norm_mlp[i])
        x = x + jnp.square(jax.nn.relu(h @ w_ff1[i])) @ w_ff2[i]
        gate = jax.nn.sigmoid(rmsnorm(x, norm_ple[i]) @ w_ple_gate[i])
        x = x + gate * (p[i] @ w_ple[i])
    return x


HEAD_DIM = 64
MIX_WIDTH = D_MODEL
SB_WIDTH = MIX_WIDTH // 2
SB_HEADS = SB_WIDTH // HEAD_DIM
SSM_WIDTH = MIX_WIDTH - SB_WIDTH
SSM_GROUP = 16
SSM_GROUPS = SSM_WIDTH // SSM_GROUP
SSM_STATE = 64
DSA_HEADS = MIX_WIDTH // HEAD_DIM
DSA_KV_HEADS = 4
DSA_REP = DSA_HEADS // DSA_KV_HEADS
DSA_WIDTH = DSA_HEADS * HEAD_DIM
IDX_HEADS = 8
IDX_DIM = 32
TOPK_MAX = 256
D_FF_2 = 4 * D_MODEL
N_EVEN = (DEPTH + 1) // 2
N_ODD = DEPTH // 2
ALPHA = (2 * DEPTH) ** 0.25
BETA = (8 * DEPTH) ** -0.25
LN_EPS = 1e-5
SB_IN = 3 * SB_WIDTH + SSM_WIDTH
DSA_SIZES = (DSA_WIDTH, DSA_KV_HEADS * HEAD_DIM, DSA_KV_HEADS * HEAD_DIM, IDX_HEADS * IDX_DIM, IDX_DIM, IDX_HEADS)
DSA_IN = sum(DSA_SIZES)
DSA_SPLITS = tuple(int(v) for v in np.cumsum(DSA_SIZES)[:-1])


def layer_norm(x, g, b):
    xf = x.astype(jnp.float32)
    mu = jnp.mean(xf, axis=-1, keepdims=True)
    var = jnp.mean(jnp.square(xf - mu), axis=-1, keepdims=True)
    y = (xf - mu) * lax.rsqrt(var + LN_EPS) * g.astype(jnp.float32) + b.astype(jnp.float32)
    return y.astype(x.dtype)

def to_blocks(a, nb):
    return jnp.moveaxis(a.reshape((a.shape[0], nb, Q_BLOCK) + a.shape[2:]), 1, 0)

def stick_breaking_attention(q, k, v):
    Bn, S, H, dh = q.shape
    nb = S // Q_BLOCK
    spos = jnp.arange(S)
    scale = dh ** -0.5

    def block(args):
        q_b, bid = args
        tpos = bid * Q_BLOCK + jnp.arange(Q_BLOCK)
        z = jnp.einsum('bqhd,bshd->bhqs', q_b, k).astype(jnp.float32) * scale
        causal = (spos[None, :] < tpos[:, None])[None, None]
        log_beta = jax.nn.log_sigmoid(z)
        log_1mb = jnp.where(causal, jax.nn.log_sigmoid(-z), 0.0)
        csum = jnp.cumsum(log_1mb, axis=-1)
        log_w = log_beta + csum[..., -1:] - csum
        w = jnp.where(causal, jnp.exp(log_w), 0.0).astype(v.dtype)
        return jnp.einsum('bhqs,bshd->bqhd', w, v)

    out = lax.map(block, (to_blocks(q, nb), jnp.arange(nb)))
    return jnp.moveaxis(out, 0, 1).reshape(Bn, S, H * dh)

def _complex_scan_op(e_i, e_j):
    air, aii, bir, bii = e_i
    ajr, aji, bjr, bji = e_j
    ar = ajr * air - aji * aii
    ai = ajr * aii + aji * air
    br = ajr * bir - aji * bii + bjr
    bi = ajr * bii + aji * bir + bji
    return (ar, ai, br, bi)

def s5_ssm(u, log_dt, lam_re, lam_im, b_re, b_im, c_re, c_im, d):
    f32 = jnp.float32
    S = u.shape[1]
    dt = jnp.exp(log_dt.astype(f32))[:, None]
    lr = lam_re.astype(f32)
    li = lam_im.astype(f32)
    mag = jnp.exp(lr * dt)
    abar_r = mag * jnp.cos(li * dt)
    abar_i = mag * jnp.sin(li * dt)
    den = lr * lr + li * li
    nr = abar_r - 1.0
    coef_r = ((nr * lr + abar_i * li) / den)[..., None]
    coef_i = ((abar_i * lr - nr * li) / den)[..., None]
    br = b_re.astype(f32)
    bi = b_im.astype(f32)
    bbar_r = coef_r * br - coef_i * bi
    bbar_i = coef_r * bi + coef_i * br
    uf = u.astype(f32)
    bu_r = jnp.einsum('bsgc,gnc->bsgn', uf, bbar_r)
    bu_i = jnp.einsum('bsgc,gnc->bsgn', uf, bbar_i)
    a_r = jnp.broadcast_to(abar_r, (1, S) + abar_r.shape)
    a_i = jnp.broadcast_to(abar_i, (1, S) + abar_i.shape)
    _, _, x_r, x_i = lax.associative_scan(_complex_scan_op, (a_r, a_i, bu_r, bu_i), axis=1)
    y = (jnp.einsum('gcn,bsgn->bsgc', c_re.astype(f32), x_r)
         - jnp.einsum('gcn,bsgn->bsgc', c_im.astype(f32), x_i)
         + d.astype(f32) * uf)
    return y.astype(u.dtype)

def mixer_sb_ssm(x, w_in, log_dt, lam_re, lam_im, b_re, b_im, c_re, c_im, d, w_glu, b_glu, w_out):
    Bn, S, _ = x.shape
    proj = x @ w_in
    q, k, v, u = jnp.split(proj, [SB_WIDTH, 2 * SB_WIDTH, 3 * SB_WIDTH], axis=-1)
    hs = (Bn, S, SB_HEADS, HEAD_DIM)
    a_out = stick_breaking_attention(q.reshape(hs), k.reshape(hs), v.reshape(hs))
    y = s5_ssm(u.reshape(Bn, S, SSM_GROUPS, SSM_GROUP), log_dt, lam_re, lam_im,
               b_re, b_im, c_re, c_im, d).reshape(Bn, S, SSM_WIDTH)
    y = jax.nn.gelu(y)
    y = y * jax.nn.sigmoid(y @ w_glu + b_glu)
    return jnp.concatenate([a_out, y], axis=-1) @ w_out

def alibi_slopes(n_heads):
    return jnp.asarray(2.0 ** (-8.0 * np.arange(1, n_heads + 1) / n_heads), dtype=jnp.float32)

def mixer_dsa(x, w_in, w_out):
    Bn, S, _ = x.shape
    proj = x @ w_in
    q, k, v, qi, ki, wi = jnp.split(proj, DSA_SPLITS, axis=-1)
    q = q.reshape(Bn, S, DSA_KV_HEADS, DSA_REP, HEAD_DIM)
    k = k.reshape(Bn, S, DSA_KV_HEADS, HEAD_DIM)
    v = v.reshape(Bn, S, DSA_KV_HEADS, HEAD_DIM)
    qi = qi.reshape(Bn, S, IDX_HEADS, IDX_DIM)
    topk = min(TOPK_MAX, S // 4)
    nb = S // Q_BLOCK
    spos = jnp.arange(S)
    slopes = alibi_slopes(DSA_HEADS).reshape(DSA_KV_HEADS, DSA_REP)
    idx_scale = (IDX_DIM ** -0.5) * (IDX_HEADS ** -0.5)

    def block(args):
        q_b, qi_b, wi_b, bid = args
        tpos = bid * Q_BLOCK + jnp.arange(Q_BLOCK)
        rel = jax.nn.relu(jnp.einsum('bqhd,bsd->bqsh', qi_b, ki).astype(jnp.float32))
        score = jnp.einsum('bqsh,bqh->bqs', rel, wi_b.astype(jnp.float32)) * idx_scale
        causal = (spos[None, :] <= tpos[:, None])[None]
        score = jnp.where(causal, score, -jnp.inf)
        _, idx = lax.top_k(score, topk)
        k_sel = jax.vmap(lambda kb, ib: kb[ib])(k, idx)
        v_sel = jax.vmap(lambda vb, ib: vb[ib])(v, idx)
        logits = jnp.einsum('bqgrd,bqkgd->bqgrk', q_b, k_sel).astype(jnp.float32) * (HEAD_DIM ** -0.5)
        dist = (tpos[None, :, None] - idx).astype(jnp.float32)
        logits = logits - slopes[None, None, :, :, None] * dist[:, :, None, None, :]
        valid = (idx <= tpos[None, :, None])[:, :, None, None, :]
        logits = jnp.where(valid, logits, -jnp.inf)
        p = jax.nn.softmax(logits, axis=-1).astype(v.dtype)
        o = jnp.einsum('bqgrk,bqkgd->bqgrd', p, v_sel)
        return o.reshape(Bn, Q_BLOCK, DSA_WIDTH)

    out = lax.map(block, (to_blocks(q, nb), to_blocks(qi, nb), to_blocks(wi, nb), jnp.arange(nb)))
    out = jnp.moveaxis(out, 0, 1).reshape(Bn, S, DSA_WIDTH)
    return out @ w_out

def sq_relu_mlp(x, w1, w2):
    return jnp.square(jax.nn.relu(x @ w1)) @ w2

def second_inputs(seed: int = 0) -> dict:
    key = jax.random.key(seed)
    ks = jax.random.split(key, 32)
    f32 = jnp.float32

    def nrm(k, shape, scale):
        return jax.random.normal(k, shape, f32) * scale

    ws = D_MODEL ** -0.5
    x = nrm(ks[0], (BATCH, SEQ, D_MODEL), 1.0)
    sb_ssm_w_in = jnp.concatenate([
        nrm(ks[1], (N_EVEN, D_MODEL, 2 * SB_WIDTH), ws),
        nrm(ks[2], (N_EVEN, D_MODEL, SB_WIDTH), ws * BETA),
        nrm(ks[3], (N_EVEN, D_MODEL, SSM_WIDTH), ws)], axis=-1)
    ssm_log_dt = jax.random.uniform(ks[4], (N_EVEN, SSM_GROUPS), f32,
                                    minval=math.log(1e-3), maxval=math.log(1e-1))
    n = jnp.arange(SSM_STATE, dtype=f32)
    ssm_lam_re = -0.5 + nrm(ks[5], (N_EVEN, SSM_GROUPS, SSM_STATE), 0.01)
    ssm_lam_im = math.pi * n + nrm(ks[6], (N_EVEN, SSM_GROUPS, SSM_STATE), 0.01)
    bsc = (2 * SSM_GROUP) ** -0.5
    ssm_b_re = nrm(ks[7], (N_EVEN, SSM_GROUPS, SSM_STATE, SSM_GROUP), bsc)
    ssm_b_im = nrm(ks[8], (N_EVEN, SSM_GROUPS, SSM_STATE, SSM_GROUP), bsc)
    csc = (2 * SSM_STATE) ** -0.5
    ssm_c_re = nrm(ks[9], (N_EVEN, SSM_GROUPS, SSM_GROUP, SSM_STATE), csc)
    ssm_c_im = nrm(ks[10], (N_EVEN, SSM_GROUPS, SSM_GROUP, SSM_STATE), csc)
    ssm_d = nrm(ks[11], (N_EVEN, SSM_GROUPS, SSM_GROUP), 1.0)
    ssm_w_glu = nrm(ks[12], (N_EVEN, SSM_WIDTH, SSM_WIDTH), SSM_WIDTH ** -0.5)
    ssm_b_glu = nrm(ks[13], (N_EVEN, SSM_WIDTH), 0.02)
    sb_ssm_w_out = nrm(ks[14], (N_EVEN, MIX_WIDTH, D_MODEL), (MIX_WIDTH ** -0.5) * BETA)
    kvw = DSA_KV_HEADS * HEAD_DIM
    dsa_w_in = jnp.concatenate([
        nrm(ks[15], (N_ODD, D_MODEL, DSA_WIDTH + kvw), ws),
        nrm(ks[16], (N_ODD, D_MODEL, kvw), ws * BETA),
        nrm(ks[17], (N_ODD, D_MODEL, IDX_HEADS * IDX_DIM + IDX_DIM + IDX_HEADS), ws)], axis=-1)
    dsa_w_out = nrm(ks[18], (N_ODD, DSA_WIDTH, D_MODEL), (DSA_WIDTH ** -0.5) * BETA)
    ln_mix_g = 1.0 + nrm(ks[19], (DEPTH, D_MODEL), 0.02)
    ln_mix_b = nrm(ks[20], (DEPTH, D_MODEL), 0.02)
    ln_ffn_g = 1.0 + nrm(ks[21], (DEPTH, D_MODEL), 0.02)
    ln_ffn_b = nrm(ks[22], (DEPTH, D_MODEL), 0.02)
    mlp_w1 = nrm(ks[23], (DEPTH, D_MODEL, D_FF_2), ws * BETA)
    mlp_w2 = nrm(ks[24], (DEPTH, D_FF_2, D_MODEL), (D_FF_2 ** -0.5) * BETA)
    return {"x": x, "sb_ssm_w_in": sb_ssm_w_in, "ssm_log_dt": ssm_log_dt,
            "ssm_lam_re": ssm_lam_re, "ssm_lam_im": ssm_lam_im,
            "ssm_b_re": ssm_b_re, "ssm_b_im": ssm_b_im,
            "ssm_c_re": ssm_c_re, "ssm_c_im": ssm_c_im, "ssm_d": ssm_d,
            "ssm_w_glu": ssm_w_glu, "ssm_b_glu": ssm_b_glu, "sb_ssm_w_out": sb_ssm_w_out,
            "dsa_w_in": dsa_w_in, "dsa_w_out": dsa_w_out,
            "ln_mix_g": ln_mix_g, "ln_mix_b": ln_mix_b,
            "ln_ffn_g": ln_ffn_g, "ln_ffn_b": ln_ffn_b,
            "mlp_w1": mlp_w1, "mlp_w2": mlp_w2}

def second_block(x, sb_ssm_w_in, ssm_log_dt, ssm_lam_re, ssm_lam_im, ssm_b_re, ssm_b_im,
              ssm_c_re, ssm_c_im, ssm_d, ssm_w_glu, ssm_b_glu, sb_ssm_w_out,
              dsa_w_in, dsa_w_out, ln_mix_g, ln_mix_b, ln_ffn_g, ln_ffn_b, mlp_w1, mlp_w2):
    for i in range(DEPTH):
        j = i // 2
        if i % 2 == 0:
            h = mixer_sb_ssm(x, sb_ssm_w_in[j], ssm_log_dt[j], ssm_lam_re[j], ssm_lam_im[j],
                             ssm_b_re[j], ssm_b_im[j], ssm_c_re[j], ssm_c_im[j], ssm_d[j],
                             ssm_w_glu[j], ssm_b_glu[j], sb_ssm_w_out[j])
        else:
            h = mixer_dsa(x, dsa_w_in[j], dsa_w_out[j])
        x = layer_norm(ALPHA * x + h, ln_mix_g[i], ln_mix_b[i])
        x = layer_norm(ALPHA * x + sq_relu_mlp(x, mlp_w1[i], mlp_w2[i]), ln_ffn_g[i], ln_ffn_b[i])
    return x


def setup_inputs(seed=0):
    out = dict(first_inputs(seed))
    for name, value in second_inputs(seed + 1).items():
        if name != "x":
            out[name + "_2"] = value
    return out


def reference(
    x, p, norm_mix, w_in, nsa_q_norm, nsa_k_norm, cmp_pos_k, cmp_pos_v, cmp_w1_k, cmp_w2_k,
    cmp_w1_v, cmp_w2_v, w_up_nsa, w_up_ret, w_out, norm_mlp, w_ff1, w_ff2, norm_ple, w_ple,
    w_ple_gate, sb_ssm_w_in_2, ssm_log_dt_2, ssm_lam_re_2, ssm_lam_im_2, ssm_b_re_2, ssm_b_im_2,
    ssm_c_re_2, ssm_c_im_2, ssm_d_2, ssm_w_glu_2, ssm_b_glu_2, sb_ssm_w_out_2, dsa_w_in_2,
    dsa_w_out_2, ln_mix_g_2, ln_mix_b_2, ln_ffn_g_2, ln_ffn_b_2, mlp_w1_2, mlp_w2_2,
):
    x = first_block(
        x, p, norm_mix, w_in, nsa_q_norm, nsa_k_norm, cmp_pos_k, cmp_pos_v, cmp_w1_k, cmp_w2_k,
        cmp_w1_v, cmp_w2_v, w_up_nsa, w_up_ret, w_out, norm_mlp, w_ff1, w_ff2, norm_ple, w_ple,
        w_ple_gate,
    )
    return second_block(
        x, sb_ssm_w_in_2, ssm_log_dt_2, ssm_lam_re_2, ssm_lam_im_2, ssm_b_re_2, ssm_b_im_2,
        ssm_c_re_2, ssm_c_im_2, ssm_d_2, ssm_w_glu_2, ssm_b_glu_2, sb_ssm_w_out_2, dsa_w_in_2,
        dsa_w_out_2, ln_mix_g_2, ln_mix_b_2, ln_ffn_g_2, ln_ffn_b_2, mlp_w1_2, mlp_w2_2,
    )


_drawn_inputs = setup_inputs


def setup_inputs(seed=0):
    import zlib

    import numpy as np

    out = dict(_drawn_inputs(seed))
    spreads = {}
    factors = {'nsa_q_norm': 3.943,
     'nsa_k_norm': 3.636,
     'cmp_pos_k': 6.391,
     'cmp_pos_v': 2.844,
     'norm_ple': 3.099,
     'ssm_log_dt_2': 45.424,
     'ssm_lam_re_2': 64.0,
     'ssm_lam_im_2': 41.56,
     'ssm_b_re_2': 58.056,
     'ssm_b_im_2': 51.784,
     'ssm_c_re_2': 50.904,
     'ssm_c_im_2': 56.312,
     'ssm_b_glu_2': 53.031}
    for name, (base, spread) in spreads.items():
        noise = np.random.default_rng([zlib.crc32(name.encode()), seed]).standard_normal(out[name].shape)
        drawn = base * np.exp(spread * noise) if base else spread * noise
        out[name] = __import__('jax').numpy.asarray(drawn.astype(out[name].dtype))
    for name, factor in factors.items():
        out[name] = (out[name] * factor).astype(out[name].dtype)
    return out
```

```python
from contextlib import ExitStack

import numpy as np

import concourse.bass as bass
from concourse import mybir

F32 = mybir.dt.float32
F32R = mybir.dt.float32r
ALU = mybir.AluOpType
ACT = mybir.ActivationFunctionType
AX_X = mybir.AxisListType.X

P = 128
S = 256
TT = S // P
D = 1024
KT = D // P
DEPTH = 2
DFF = 4 * D
FB = DFF // P
BANK = 512
SLOT = 4096
RING = 3
EPS = 1e-6
MASKED = -1e30

HEADS, DH, GROUPS = 8, 64, 2
NCMP, CMP_STRIDE, CMP_LEN, CMP_HID = 16, 16, 32, 256
Z_Q, Z_KC, Z_VC, Z_KS, Z_VS, Z_KW, Z_VW, Z_GATE = 0, 512, 640, 768, 896, 1024, 1152, 1280
Z_RQ, Z_RK, Z_RV, Z_RG, Z_MA, Z_MB, D_IN = 1304, 1816, 2328, 2840, 3352, 4376, 5400
N_IN = -(-D_IN // BANK)
RH, RD = 4, 128
PLE = 256

ALPHA = (2 * DEPTH) ** 0.25
LN_EPS = 1e-5
SB_W, SB_HEADS = 512, 8
SSM_G, SSM_C, SSM_N = 32, 16, 64
SJ = SSM_G * SSM_N // P
DSA_HEADS, DSA_KV = 16, 4
IDX_HEADS, IDX_DIM, TOPK = 8, 32, min(256, S // 4)
I_Q, I_K, I_V, I_QI, I_KI, I_WI, DSA_IN = 0, 1024, 1280, 1536, 1792, 1824, 1832
TAKEN = -3e38
TWO_PI = 2 * np.pi
TURN = [6.28125]
TURN.append(np.floor((TWO_PI - TURN[0]) * 2.0 ** 21) / 2.0 ** 21)
TURN.append(TWO_PI - TURN[0] - TURN[1])
ROUND = 1.5 * 2.0 ** 23

CONST_PARTS = [("ident", P), ("causal", P), ("cmp_add", 128), ("cmp_keep", 128), ("decay", RH * 384),
               ("cos", TT * 64), ("sin", TT * 64), ("own_rows", 4), ("suffix", P), ("ones", P),
               ("strict_keep", P), ("strict_add", P), ("rel", S)]
CONST_AT = {}
_n = 0
for _name, _w in CONST_PARTS:
    CONST_AT[_name] = (_n, _n + _w)
    _n += _w
CONST_W = _n


def constants():
    f = np.float32
    c = np.zeros((P, CONST_W), f)

    def put(name, a):
        lo, hi = CONST_AT[name]
        c[:, lo:hi] = np.asarray(a, f).reshape(P, hi - lo)

    i = np.arange(P)
    put("ident", np.eye(P))
    put("causal", np.where(i[None, :] <= i[:, None], 0.0, MASKED))
    t = np.arange(S).reshape(TT, P).T[:, :, None, None]
    own = np.arange(GROUPS)[:, None] == np.arange(GROUPS * NCMP)[None, :] // NCMP
    ends = (np.arange(GROUPS * NCMP) % NCMP) * CMP_STRIDE + CMP_LEN - 1
    keep = (ends[None, None, None, :] <= t) & own[None, None]
    put("cmp_add", np.where(keep, 0.0, MASKED))
    put("cmp_keep", keep)
    gamma = (f(1.0) - f(2.0) ** (f(-5.0) - np.arange(RH, dtype=f))).astype(f)
    lg = np.log(gamma).astype(np.float64)
    diff = (i[None, :] - i[:, None]).astype(np.float64)
    near = np.where(diff[:, None] >= 0, np.exp(lg[None, :, None] * np.maximum(diff[:, None], 0)), 0.0)
    far = np.exp(lg[None, :, None] * (diff[:, None] + P))
    put("decay", np.concatenate([near, far, near], -1) * RD ** -0.5)
    inv = (f(10000.0) ** (-np.arange(64, dtype=f) / f(64))).astype(f)
    ang = (np.arange(S, dtype=f)[:, None] * inv[None]).astype(f).reshape(TT, P, 64).transpose(1, 0, 2)
    put("cos", np.cos(ang.astype(np.float64)))
    put("sin", np.sin(ang.astype(np.float64)))
    put("own_rows", i[:, None] // 32 == np.arange(4)[None])
    put("suffix", i[:, None] >= i[None, :])
    put("ones", np.ones((P, P)))
    put("strict_keep", i[:, None] < i[None, :])
    put("strict_add", np.where(i[:, None] < i[None, :], 0.0, MASKED))
    put("rel", np.arange(S)[None, :] - P - i[:, None])
    return c


WIDE = [f"c{c}t{t}" for c in range(5) for t in range(TT)] + ["hk", "hv"]
WIDE += [f"c{c}t{t}" for c in (5, 6, 7) for t in range(TT)] + ["o0"]
WIDE += [f"c8t{t}" for t in range(TT)] + ["o1"] + [f"c9t{t}" for t in range(TT)] + ["yr0", "yr1"]
WIDE += [f"c10t{t}" for t in range(TT)] + [f"f{n}" for n in range(FB // 2)] + [f"g{n}" for n in range(4)]
AUX = ["cols"] + [f"n{n}" for n in range(4)] + ["q0", "q1", "k", "zc", "hidT", "w2", "kcT", "cmp0", "cmp1"]
AUX += [f"pt0.{n}" for n in range(4)] + ["pcT"] + [f"pt1.{n}" for n in range(4)] + [f"pt2.{n}" for n in range(4)]
AUX += [f"rot{n}" for n in range(4)] + ["pT", "ya0", "ya1", "yr0", "yr1"]
AUX += [f"upa{n}" for n in range(4)] + [f"upb{n}" for n in range(4)] + [f"m{n}" for n in range(4)]
AUX += [f"out{n}" for n in range(4)] + [f"nm{n}" for n in range(4)] + [f"np{n}" for n in range(4)]
AUX += [f"ple{n}" for n in range(4)]
assert len(WIDE) % 2 == 0 and len(AUX) % 2 == 0, (len(WIDE), len(AUX))

TILES = [f"in{c}" for c in range(5)] + ["w1k", "w1v"] + [f"in{c}" for c in range(5, N_IN)]
TILES += ["up_nsa", "up_ret", "out0", "out1"] + [f"ff1.{n}" for n in range(8)] + [f"ff2.{n}" for n in range(8)]
TILES += ["gate0", "gate1", "ple"]
assert len(TILES) % RING == 0
MLP_TILES = 16


def _mlp_names(pre, n, kind):
    return [f"{pre}{kind}{i}" for i in range(n)]


WIDE2 = ["u0", "u1", "sq0", "sq1", "sk0", "sk1", "sv0", "sv1", "y0", "sA0", "sA1", "y1", "sB0", "sB1", "y2", "y3"]
WIDE2 += ["glu0", "glu1"] + _mlp_names("A.", FB // 2, "f")
WIDE2 += ["qi", "kiw", "dk", "dv", "dq0", "dq1", "dq2", "dq3", "do0", "do1", "do2", "do3"] + _mlp_names("B.", FB // 2, "f")
AUX2 = _mlp_names("A.", 4, "x") + ["ct0", "ct1", "par", "bt0", "bt1", "bu0", "bu1"] + [f"cs{h}" for h in range(4)]
AUX2 += [f"bu{j}" for j in range(2, 9)] + [f"cs{h}" for h in range(4, 8)] + [f"bu{j}" for j in range(9, 16)]
AUX2 += ["ao0", "ao1"] + _mlp_names("A.", 4, "out") + _mlp_names("A.", 4, "n")
AUX2 += _mlp_names("B.", 4, "x") + [f"pt{b}.{n}" for b in range(3) for n in range(4)] + [f"do{n}" for n in range(4)]
AUX2 += _mlp_names("B.", 4, "out") + _mlp_names("B.", 4, "n")
TILES2 = ["sb3", "sb0", "sb1", "sb2", "glu", "sbo0", "sbo1"]
TILES2 += [f"A.ff1.{n}" for n in range(8)] + [f"A.ff2.{n}" for n in range(8)]
TILES2 += ["ds3", "ds2", "ds0", "ds1", "dso0", "dso1"]
TILES2 += [f"B.ff1.{n}" for n in range(8)] + [f"B.ff2.{n}" for n in range(8)]


class Signal:

    def __init__(self, sem, per_layer, start=0):
        self.sem, self.per_layer, self.start = sem, per_layer, start


class Where:

    def __init__(self, layer=None):
        self.layer = layer

    def value(self, signal, n):
        if self.layer is None:
            return DEPTH * signal.per_layer + n
        return self.layer * signal.per_layer + n


class Steps:

    def __init__(self, where):
        self.where, self.count, self.last = where, {}, None

    def up(self, signal, by=1):
        self.count[signal] = self.count.get(signal, 0) + by
        self.last = signal
        return signal.sem

    def at(self, signal, n):
        return self.where.value(signal, n)

    def reached(self):
        return self.at(self.last, self.last.start + self.count[self.last])

    def check(self):
        bad = {s.sem.name: (n, s.per_layer) for s, n in self.count.items() if n != s.per_layer}
        assert not bad, bad


class Line:

    def __init__(self, banks, names, ready, saved):
        self.banks, self.names, self.ready, self.saved, self.at = banks, names, ready, saved, 0

    def next(self, name):
        assert self.names[self.at] == name, (self.names[self.at], name)
        self.at += 1
        return self.banks[(self.at - 1) % 2], self.at

    def nth_save(self, name):
        return self.names.index(name) + 3

    def again(self, names):
        return Line(self.banks, names, self.ready, self.saved)


class Kit:

    def __init__(self, mm, tp, next_tile, tile_done, turn_rows, rows_by_tile, units_by_tile, mlp, finish):
        self.mm, self.tp, self.next_tile, self.tile_done = mm, tp, next_tile, tile_done
        self.turn_rows, self.rows_by_tile, self.units_by_tile = turn_rows, rows_by_tile, units_by_tile
        self.mlp, self.finish = mlp, finish


def bc(ap, axis, n):
    ap = ap.unsqueeze(axis)
    shape = list(ap.shape)
    shape[axis] = n
    return ap.broadcast_to(shape)


def build(nc, I, out):
    with ExitStack() as ctx:
        program(nc, ctx, I, out)


def program(nc, ctx, I, out):
    address = {}

    def sb(name, shape):
        address[name] = -(-nc.sbuf_base // 32) * 32
        return ctx.enter_context(nc.sbuf_tensor(name, shape, F32))

    def digits(name, buffer, lo, width):
        return nc.alloc_sbuf_tensor_at(name, [P, width], F32R, offset=address[buffer] + 4 * lo)

    def sig(name, per_layer=0, start=0):
        return Signal(ctx.enter_context(nc.semaphore(name)), per_layer, start)

    ring = [sb(f"ring{i}", [P, SLOT]) for i in range(RING)]
    x = sb("x", [P, TT, D])
    hT = sb("hT", [P, KT, S])
    big = sb("big", [P, TT * D_IN])
    scr = sb("scr", [P, 2304])
    rows = sb("rows", [P, 2048])
    tmp = sb("tmp", [P, 2048])
    const = sb("const", [P, CONST_W])
    work = sb("work", [P, 10848])
    tiny = sb("tiny", [P, 512])
    pT = sb("pT", [P, 2, S])
    psum = ctx.enter_context(nc.psum_tensor("psum", [P, 8 * BANK], F32))
    bank = [psum[:, b * BANK:(b + 1) * BANK] for b in range(8)]
    scores = psum[:, 4 * BANK:8 * BANK]

    K = {name: const[:, lo:hi] for name, (lo, hi) in CONST_AT.items()}
    ident = K["ident"]
    z = big[:, :].rearrange("p (t n) -> p t n", t=TT)
    hid_f = work[:, 0:FB * S].rearrange("p (f t) -> p f t", t=S)
    hid_hi = digits("hid_hi", "big", 0, FB * S)[:, :].rearrange("p (f t) -> p f t", t=S)
    hid_lo = digits("hid_lo", "work", 0, FB * S)[:, :].rearrange("p (f t) -> p f t", t=S)
    ht_f = scr[:, 0:KT * S].rearrange("p (k t) -> p k t", t=S)
    ht_hi = digits("ht_hi", "hT", 0, KT * S)[:, :].rearrange("p (k t) -> p k t", t=S)
    ht_lo = digits("ht_lo", "scr", 0, KT * S)[:, :].rearrange("p (k t) -> p k t", t=S)
    HALF = SLOT // 2
    w_hi = [[digits("w_hi00", "big", FB * S, HALF), digits("w_hi01", "work", FB * S, HALF)],
            [digits("w_hi10", "tmp", 0, HALF), digits("w_hi11", "rows", 0, HALF)]]
    w_lo = [digits(f"w_lo{i}", f"ring{i}", 0, SLOT) for i in range(RING)]
    rows_t = rows[:, :].rearrange("p (t n) -> p t n", t=TT)

    qn = tmp[:, 0:1024].rearrange("p (t n) -> p t n", t=TT)

    def part(lo, width, pattern=None, **sizes):
        ap = work[:, lo:lo + width]
        return ap.rearrange(pattern, **sizes) if pattern else ap

    qT = part(0, 1024, "p (b t) -> p b t", t=S)
    yaT = qT
    kT = part(1024, 512, "p (k t) -> p k t", t=S)
    zT2 = part(1536, 1088, "p (k g t) -> p k g t", k=2, g=2)
    zb2 = part(2624, 1024, "p (k j g n) -> p k j g n", k=2, j=16, g=2)
    hc, hu, he = (work[0:32, lo:lo + 512] for lo in (3648, 4160, 4672))
    hidT = part(5184, 512, "p (k h m) -> p k h m", k=2, h=2)
    kvc = part(5696, 128)
    kcd = part(5824, 128, "p (u d) -> p u d", u=2)
    vz = part(5952, 256, "p (h d) -> p h d", d=DH)
    kcT = part(10784, 64, "p (g n) -> p g n", g=GROUPS)
    pc = part(6240, 512, "p (t h n) -> p t h n", t=2, n=32)
    pcT = part(6752, 512, "p (b t) -> p b t", t=P)
    qkT = part(7264, 2048, "p (a h t) -> p a h t", a=2, t=S)
    yrT = part(7264, 1024, "p (b t) -> p b t", t=S)
    p_sb = part(9312, 512, "p (t n) -> p t n", t=TT)
    w2 = part(10336, 256, "p (k h d) -> p k h d", k=2, h=2)
    vec_rows = work[0:64, 10592:10720]
    cols = part(10720, 64)
    inner = scr[:, 0:RH * 384].rearrange("p (h n) -> p h n", h=RH)
    ptb = scr[:, 0:2048].rearrange("p (b t) -> p b t", t=P)
    sq = scr[:, :].rearrange("p (t n) -> p t n", t=TT)
    C_MIX, C_MLP, C_PLE, C_Q, C_K, C_POS = 0, 8, 16, 24, 25, 32
    ss36, rr36 = tiny[:, 0:36], tiny[:, 36:72]
    gates = tiny[:, 72:120].rearrange("p (t n) -> p t n", t=TT)
    mx, sums, wts = tiny[:, 120:136], tiny[:, 136:152], tiny[:, 152:168]
    nss, nrr = tiny[:, 168:170], tiny[:, 170:172]
    kss, krr = tiny[:, 172:173], tiny[:, 173:174]
    cmx, csum = tiny[:, 176:192], tiny[:, 192:208]
    yss, yrr = tiny[:, 208:216], tiny[:, 216:224]

    const_in, x_in = sig("const_in"), sig("x_in")
    small_in = sig("small_in", 16 * 9)
    late_in = sig("late_in", 16 * 3)
    small_used = sig("small_used", 1, 1)
    tile_in = [sig(f"tile_in{r}", 16 * len(TILES) // RING) for r in range(RING)]
    tile_used = sig("tile_used", len(TILES))
    wide = Line(bank[0:2], WIDE, sig("wide_ready", len(WIDE)), sig("wide_saved", len(WIDE), 2))
    aux = Line(bank[2:4], AUX, sig("aux_ready", len(AUX)), sig("aux_saved", len(AUX), 2))
    act_step, dve_step, pool_step = sig("act_step", 60), sig("dve_step", 58), sig("pool_step", 23)
    h_ready = sig("h_ready", 3 * TT)
    sq_ready, ss_ready, rr_ready = sig("sq_ready", 1), sig("ss_ready", 1), sig("rr_ready", 1)
    heads_ready = sig("heads_ready", 1)
    gate_exp = sig("gate_exp", 1)
    zb_ready = sig("zb_ready", 1)
    gelu_arg, gelu_exp, gelu_ready = sig("gelu_arg", 1), sig("gelu_exp", 1), sig("gelu_ready", 1)
    kc_ss, kc_rr, kc_ready = sig("kc_ss", 1), sig("kc_rr", 1), sig("kc_ready", 1)
    cmp_arg, cmp_exp, cmp_ready = sig("cmp_arg", 1), sig("cmp_exp", 1), sig("cmp_ready", 1)
    scores_ready = sig("scores_ready", 4)
    max_ready, exp_ready, probs_ready = sig("max_ready", 3), sig("exp_ready", 3), sig("probs_ready", 3)
    inner_saved = sig("inner_saved", 1)
    rope_ready = sig("rope_ready", 1)
    silu_exp = sig("silu_exp", 1)
    yr_sq, yr_ss, yr_rr, yr_ready = sig("yr_sq", 1), sig("yr_ss", 1), sig("yr_rr", 1), sig("yr_ready", 1)
    merge_exp, merge_inc = sig("merge_exp", 2), sig("merge_inc", 2)
    mix_ready = sig("mix_ready", 4)
    ht_split = sig("ht_split", 4)
    w_hi_ready = sig("w_hi_ready", 2 * MLP_TILES)
    w_lo_ready = sig("w_lo_ready", 2 * MLP_TILES)
    hid_hi_ready, hid_lo_ready = sig("hid_hi_ready", FB // 2), sig("hid_lo_ready", FB // 2)
    ff2_ready, ff2_saved = sig("ff2_ready", 4), sig("ff2_saved", 4)
    stored = sig("stored")
    zero_set = sig("zero_set")

    BATCHES = [(0, 0, 8), (1, 0, 4), (1, 4, 4)]

    def batch_view(b):
        keys = (BATCHES[b][0] + 1) * P
        return scores.rearrange("p (i n) -> p i n", n=keys), keys

    def mlp_nth(pre):
        return 1 if pre == "B." else 0

    def split_nth(name):
        pre, kind, num = name.rpartition("ff")[0], name[-3], int(name[-1])
        return MLP_TILES * mlp_nth(pre) + (8 if kind == "2" else 0) + num

    def w_tile(n, shape):
        k, m = shape
        return ring[n % RING][:, 0:k * m].rearrange("p (k n) -> p k n", k=k)

    block = ctx.enter_context(nc.Block())

    def pe_kit(pe, st, wide_, aux_, tiles):
        tile = {"at": 0, "owed": 0}

        def mm(o, lhsT, rhs, start, stop, signal=None):
            ins = pe.matmul(o, lhsT, rhs, start=start, stop=stop)
            if signal:
                ins.then_inc(st.up(signal), 1)
            elif tile["owed"]:
                ins.then_inc(st.up(tile_used, tile["owed"]), tile["owed"])
                tile["owed"] = 0

        def tp(o, in_, n=P, signal=None):
            ins = pe.transpose(o, in_, ident[0:n, 0:n])
            if signal:
                ins.then_inc(st.up(signal), 1)
            elif tile["owed"]:
                ins.then_inc(st.up(tile_used, tile["owed"]), tile["owed"])
                tile["owed"] = 0

        def next_tile(name, k, m):
            n = tile["at"]
            assert tiles[n] == name
            pe.wait_ge(tile_in[n % RING].sem, st.at(tile_in[n % RING], 16 * (n // RING + 1)))
            tile["at"] += 1
            return w_tile(n, (k, m))

        def tile_done():
            tile["owed"] += 1

        def turn_rows(names, source, ready, first):
            for n, name in enumerate(names):
                t, half = divmod(n, 2)
                if half == 0 and ready:
                    pe.wait_ge(ready.sem, st.at(ready, first + t))
                b, nth = aux_.next(name)
                pe.wait_ge(aux_.saved.sem, st.at(aux_.saved, nth))
                for k in range(4):
                    lo = (4 * half + k) * P
                    tp(b[:, k * P:(k + 1) * P], source[:, t, lo:lo + P],
                       signal=aux_.ready if k == 3 else None)

        def rows_by_tile(line, names, xT, w, k, c0=0, m=BANK):
            for t, name in enumerate(names):
                b, nth = line.next(name)
                pe.wait_ge(line.saved.sem, st.at(line.saved, nth))
                for j in range(k):
                    mm(b[:, 0:m], xT[:, j, t * P:(t + 1) * P], w[:, j, c0:c0 + m], j == 0, j == k - 1,
                       line.ready if j == k - 1 else None)

        def units_by_tile(line, names, w, col=0):
            for n, name in enumerate(names):
                b, nth = line.next(name)
                pe.wait_ge(line.saved.sem, st.at(line.saved, nth))
                for u in range(2):
                    lo = col + (2 * n + u) * P
                    for k in range(KT):
                        mm(b[:, u * S:(u + 1) * S], w[:, k, lo:lo + P], hT[:, k, :], k == 0, k == KT - 1,
                           line.ready if u == 1 and k == KT - 1 else None)

        def next_split(name, k, m):
            nth = split_nth(name)
            next_tile(name, k, m)
            pe.wait_ge(w_lo_ready.sem, st.at(w_lo_ready, 2 * nth + 2))
            halves = [h[:, :].rearrange("p (k n) -> p k n", k=k // 2) for h in w_hi[nth % 2]]
            lo = w_lo[(tile["at"] - 1) % RING][:, :].rearrange("p (k n) -> p k n", k=k)
            return lo, lambda kk, cols_: halves[kk // (k // 2)][:, kk % (k // 2), cols_]

        def products(o, a_hi, a_lo, b_hi, b_lo, start, stop, signal):
            mm(o, a_lo, b_hi, start, False)
            mm(o, a_hi, b_lo, False, False)
            mm(o, a_hi, b_hi, False, stop, signal)

        def mlp(pre):
            for n in range(8):
                lo, hi = next_split(f"{pre}ff1.{n}", KT, BANK)
                for q in range(2):
                    b, nth = wide_.next(f"{pre}f{2 * n + q}")
                    pe.wait_ge(wide_.saved.sem, st.at(wide_.saved, nth))
                    for u in range(2):
                        c = slice((2 * q + u) * P, (2 * q + u + 1) * P)
                        for k in range(KT):
                            last = k == KT - 1
                            products(b[:, u * S:(u + 1) * S], hi(k, c), lo[:, k, c], ht_hi[:, k, :], ht_lo[:, k, :],
                                     k == 0, last, wide_.ready if last and u == 1 else None)
                tile_done()
            for n in range(8):
                lo, hi = next_split(f"{pre}ff2.{n}", 4, D)
                pe.wait_ge(hid_lo_ready.sem, st.at(hid_lo_ready, FB // 2 * mlp_nth(pre) + 2 * n + 2))
                for q in range(4):
                    c, t = divmod(q, 2)
                    for k in range(4):
                        last = n == 7 and k == 3
                        tok, col = slice(t * P, (t + 1) * P), slice(c * BANK, (c + 1) * BANK)
                        products(scores[:, q * BANK:(q + 1) * BANK], hid_hi[:, 4 * n + k, tok],
                                 hid_lo[:, 4 * n + k, tok], hi(k, col), lo[:, k, col], n == 0 and k == 0, last,
                                 ff2_ready if last else None)
                tile_done()

        def finish():
            pe.drain().then_inc(st.up(tile_used, tile["owed"]), tile["owed"])
            assert tile["at"] == len(tiles)

        return Kit(mm, tp, next_tile, tile_done, turn_rows, rows_by_tile, units_by_tile, mlp, finish)

    def pe_layer(pe, st):
        wide_, aux_ = wide.again(WIDE), aux.again(AUX)
        kit = pe_kit(pe, st, wide_, aux_, TILES)
        mm, tp, next_tile, tile_done = kit.mm, kit.tp, kit.next_tile, kit.tile_done
        turn_rows, rows_by_tile = kit.turn_rows, kit.rows_by_tile

        def chunk(c):
            m = min(BANK, D_IN - c * BANK)
            w = next_tile(f"in{c}", KT, m)
            rows_by_tile(wide_, [f"c{c}t{t}" for t in range(TT)], hT, w, KT, 0, m)
            tile_done()

        def score_batch(b):
            t, h0, nh = BATCHES[b]
            view, keys = batch_view(b)
            if b:
                pe.wait_ge(exp_ready.sem, st.at(exp_ready, b))
            for h in range(h0, h0 + nh):
                g, hg = divmod(h, 4)
                for kind in range(2):
                    last = h == h0 + nh - 1 and kind == 1
                    mm(view[:, (h - h0) * 2 + kind, :], qT[64 * g:64 * g + 64, hg, t * P:(t + 1) * P],
                       kT[64 * g:64 * g + 64, kind, 0:keys], True, True, scores_ready if last else None)

        def turn_probs(b):
            pe.wait_ge(probs_ready.sem, st.at(probs_ready, b + 1))
            for n in range(4):
                bk, nth = aux_.next(f"pt{b}.{n}")
                pe.wait_ge(aux_.saved.sem, st.at(aux_.saved, nth))
                for k in range(4):
                    lo = (4 * n + k) * P
                    tp(bk[:, k * P:(k + 1) * P], rows[:, lo:lo + P], signal=aux_.ready if k == 3 else None)

        def weigh_values(b, o, last_signal):
            t, h0, nh = BATCHES[b]
            pe.wait_ge(aux_.saved.sem, st.at(aux_.saved, aux_.nth_save(f"pt{b}.3")))
            for h in range(h0, h0 + nh):
                g = h // 4
                terms = [(pcT[:, 2 * t + h // 4, :], vz[:, h % 4, :])]
                for kind, col in enumerate((Z_VS, Z_VW)):
                    for kt in range(t + 1):
                        blk = ((h - h0) * 2 + kind) * (t + 1) + kt
                        terms.append((ptb[:, blk, :], z[:, kt, col + g * DH:col + (g + 1) * DH]))
                for n, (a, v) in enumerate(terms):
                    last = n == len(terms) - 1
                    mm(o[:, h * DH:(h + 1) * DH], a, v, n == 0, last,
                       last_signal if last and h == h0 + nh - 1 else None)

        pe.wait_ge(small_in.sem, st.at(small_in, 16 * 9))
        b, nth = aux_.next("cols")
        pe.wait_ge(aux_.saved.sem, st.at(aux_.saved, nth))
        mm(b[:, 0:64], vec_rows, ident[0:64, 0:64], True, True, aux_.ready)
        turn_rows([f"n{n}" for n in range(4)], rows_t, h_ready, 1)
        pe.wait_ge(aux_.saved.sem, st.at(aux_.saved, aux_.nth_save("n3")))
        for c in range(4):
            chunk(c)
        pe.wait_ge(heads_ready.sem, st.at(heads_ready, 1))
        for t in range(TT):
            b, nth = aux_.next(f"q{t}")
            pe.wait_ge(aux_.saved.sem, st.at(aux_.saved, nth))
            for hg in range(4):
                tp(b[:, hg * P:(hg + 1) * P], qn[:, t, hg * P:(hg + 1) * P], signal=aux_.ready if hg == 3 else None)
        for name, pair in (("k", (Z_KS, Z_KW)), ("zc", (Z_KC, Z_VC))):
            b, nth = aux_.next(name)
            pe.wait_ge(aux_.saved.sem, st.at(aux_.saved, nth))
            for n, col in enumerate(pair):
                for t in range(TT):
                    tp(b[:, n * S + t * P:n * S + (t + 1) * P], z[:, t, col:col + P],
                       signal=aux_.ready if n == t == 1 else None)
        chunk(4)
        pe.wait_ge(zb_ready.sem, st.at(zb_ready, 1))
        for kind, name in enumerate(("hk", "hv")):
            w = next_tile("w1" + name[1], 16, CMP_HID)
            b, nth = wide_.next(name)
            pe.wait_ge(wide_.saved.sem, st.at(wide_.saved, nth))
            for j in range(16):
                mm(b[0:32, 0:CMP_HID], zb2[:, kind, j].rearrange("p g n -> p (g n)"), w[:, j, :], j == 0, j == 15,
                   wide_.ready if j == 15 else None)
            tile_done()
        score_batch(0)
        chunk(5)
        pe.wait_ge(gelu_ready.sem, st.at(gelu_ready, 1))
        b, nth = aux_.next("hidT")
        pe.wait_ge(aux_.saved.sem, st.at(aux_.saved, nth))
        for kind in range(2):
            for half in range(2):
                n = kind * 2 + half
                mm(b[:, n * 32:n * 32 + 32], hc[:, n * P:(n + 1) * P], ident[0:32, 0:32], True, True,
                   aux_.ready if n == 3 else None)
        pe.wait_ge(aux_.saved.sem, st.at(aux_.saved, aux_.nth_save("hidT")))
        pe.wait_ge(late_in.sem, st.at(late_in, 16 * 3))
        b, nth = aux_.next("w2")
        pe.wait_ge(aux_.saved.sem, st.at(aux_.saved, nth))
        for kind in range(2):
            for half in range(2):
                mm(b[:, kind * DH:(kind + 1) * DH], hidT[:, kind, half, :], w2[:, kind, half, :],
                   half == 0, half == 1, aux_.ready if kind == half == 1 else None)
        chunk(6)
        pe.wait_ge(kc_ready.sem, st.at(kc_ready, 1))
        b, nth = aux_.next("kcT")
        pe.wait_ge(aux_.saved.sem, st.at(aux_.saved, nth))
        tp(b[:, 0:P], kcd.rearrange("p u d -> p (u d)"), signal=aux_.ready)
        pe.wait_ge(aux_.saved.sem, st.at(aux_.saved, aux_.nth_save("kcT")))
        for t in range(TT):
            b, nth = aux_.next(f"cmp{t}")
            pe.wait_ge(aux_.saved.sem, st.at(aux_.saved, nth))
            for h in range(HEADS):
                g, hg = divmod(h, 4)
                mm(b[:, h * 32:h * 32 + 32], qT[:, hg, t * P:(t + 1) * P], kcT[:, g, :], True,
                   True, aux_.ready if h == HEADS - 1 else None)
        turn_probs(0)
        score_batch(1)
        chunk(7)
        pe.wait_ge(cmp_ready.sem, st.at(cmp_ready, 1))
        b, nth = aux_.next("pcT")
        pe.wait_ge(aux_.saved.sem, st.at(aux_.saved, nth))
        for n in range(4):
            tp(b[:, n * P:(n + 1) * P], pc[:, n // 2, 4 * (n % 2):4 * (n % 2) + 4, :].rearrange("p h n -> p (h n)"),
               signal=aux_.ready if n == 3 else None)
        pe.wait_ge(aux_.saved.sem, st.at(aux_.saved, aux_.nth_save("pcT")))
        o, nth = wide_.next("o0")
        pe.wait_ge(wide_.saved.sem, st.at(wide_.saved, nth))
        weigh_values(0, o, wide_.ready)
        turn_probs(1)
        score_batch(2)
        chunk(8)
        o, nth = wide_.next("o1")
        pe.wait_ge(wide_.saved.sem, st.at(wide_.saved, nth))
        weigh_values(1, o, None)
        turn_probs(2)
        weigh_values(2, o, wide_.ready)
        pe.wait_ge(rope_ready.sem, st.at(rope_ready, 1))
        for n in range(4):
            a, t = divmod(n, 2)
            b, nth = aux_.next(f"rot{n}")
            pe.wait_ge(aux_.saved.sem, st.at(aux_.saved, nth))
            for h in range(RH):
                lo = (Z_RQ, Z_RK)[a] + h * RD
                tp(b[:, h * P:(h + 1) * P], z[:, t, lo:lo + RD], signal=aux_.ready if h == 3 else None)
        pe.wait_ge(aux_.saved.sem, st.at(aux_.saved, aux_.nth_save("rot3")))
        pe.wait_ge(exp_ready.sem, st.at(exp_ready, 3))
        for h in range(RH):
            o = scores[:, h * BANK:h * BANK + 384]
            mm(o[:, 0:S], qkT[:, 1, h, 0:P], qkT[:, 0, h, :], True, True)
            mm(o[:, S:384], qkT[:, 1, h, P:S], qkT[:, 0, h, P:S], True, True, scores_ready if h == RH - 1 else None)
        chunk(9)
        pe.wait_ge(inner_saved.sem, st.at(inner_saved, 1))
        for t in range(TT):
            o, nth = wide_.next(f"yr{t}")
            pe.wait_ge(wide_.saved.sem, st.at(wide_.saved, nth))
            for h in range(RH):
                v = [z[:, m, Z_RV + h * RD:Z_RV + (h + 1) * RD] for m in range(TT)]
                terms = [(inner[:, h, 0:P], v[0])] if t == 0 else [(inner[:, h, P:S], v[0]), (inner[:, h, S:384], v[1])]
                for n, (a, vv) in enumerate(terms):
                    last = n == len(terms) - 1
                    mm(o[:, h * RD:(h + 1) * RD], a, vv, n == 0, last,
                       wide_.ready if last and h == RH - 1 else None)
        pe.wait_ge(late_in.sem, st.at(late_in, 16 * 3))
        b, nth = aux_.next("pT")
        pe.wait_ge(aux_.saved.sem, st.at(aux_.saved, nth))
        for k in range(2):
            for t in range(TT):
                tp(b[:, k * S + t * P:k * S + (t + 1) * P], p_sb[:, t, k * P:(k + 1) * P],
                   signal=aux_.ready if k == t == 1 else None)
        pe.wait_ge(wide_.saved.sem, st.at(wide_.saved, wide_.nth_save("o1")))
        for t in range(TT):
            b, nth = aux_.next(f"ya{t}")
            pe.wait_ge(aux_.saved.sem, st.at(aux_.saved, nth))
            for k in range(4):
                tp(b[:, k * P:(k + 1) * P], z[:, t, Z_Q + k * P:Z_Q + (k + 1) * P],
                   signal=aux_.ready if k == 3 else None)
        chunk(10)
        pe.wait_ge(yr_ready.sem, st.at(yr_ready, 1))
        for t in range(TT):
            b, nth = aux_.next(f"yr{t}")
            pe.wait_ge(aux_.saved.sem, st.at(aux_.saved, nth))
            for k in range(4):
                tp(b[:, k * P:(k + 1) * P], z[:, t, Z_RQ + k * P:Z_RQ + (k + 1) * P],
                   signal=aux_.ready if k == 3 else None)
        pe.wait_ge(aux_.saved.sem, st.at(aux_.saved, aux_.nth_save("ya1")))
        w = next_tile("up_nsa", 4, D)
        for c in range(2):
            rows_by_tile(aux_, [f"upa{2 * c + t}" for t in range(TT)], yaT, w, 4, c * BANK)
        tile_done()
        pe.wait_ge(aux_.saved.sem, st.at(aux_.saved, aux_.nth_save("yr1")))
        w = next_tile("up_ret", 4, D)
        for c in range(2):
            rows_by_tile(aux_, [f"upb{2 * c + t}" for t in range(TT)], yrT, w, 4, c * BANK)
        tile_done()
        for n in range(4):
            c, t = divmod(n, 2)
            pe.wait_ge(mix_ready.sem, st.at(mix_ready, n + 1))
            b, nth = aux_.next(f"m{n}")
            pe.wait_ge(aux_.saved.sem, st.at(aux_.saved, nth))
            for k in range(4):
                lo = (4 * c + k) * P
                tp(b[:, k * P:(k + 1) * P], rows_t[:, t, lo:lo + P], signal=aux_.ready if k == 3 else None)
        pe.wait_ge(aux_.saved.sem, st.at(aux_.saved, aux_.nth_save("m3")))
        for c in range(2):
            w = next_tile(f"out{c}", KT, BANK)
            rows_by_tile(aux_, [f"out{2 * c + t}" for t in range(TT)], hT, w, KT)
            tile_done()
        turn_rows([f"nm{n}" for n in range(4)], rows_t, h_ready, 3)
        pe.wait_ge(ht_split.sem, st.at(ht_split, 4))
        kit.mlp("")
        turn_rows([f"np{n}" for n in range(4)], rows_t, h_ready, 5)
        pe.wait_ge(aux_.saved.sem, st.at(aux_.saved, aux_.nth_save("np3")))
        for c in range(2):
            w = next_tile(f"gate{c}", KT, BANK)
            rows_by_tile(wide_, [f"g{2 * c + t}" for t in range(TT)], hT, w, KT)
            tile_done()
        w = next_tile("ple", 2, D)
        for c in range(2):
            rows_by_tile(aux_, [f"ple{2 * c + t}" for t in range(TT)], pT, w, 2, c * BANK)
        tile_done()
        kit.finish()

    def act_rsqrt(st, act, dst, src, scale, eps, signal=None):
        act.activation(dst, src, ACT.Ln, bias=eps_col[eps], scale=scale).then_inc(st.up(act_step), 1)
        act.wait_ge(st.last.sem, st.reached())
        act.activation(dst, dst, ACT.Exp, scale=-0.5).then_inc(st.up(signal or act_step), 1)

    eps_tile = sb("eps_tile", [P, 3])
    eps_col = {EPS: eps_tile[:, 0:1], LN_EPS: eps_tile[:, 1:2]}
    half_pi = eps_tile[:, 2:3]
    eps_set = sig("eps_set")

    def act_norm(st, act):
        for t in range(TT):
            act.activation(rows_t[:, t, :], x[:, t, :], ACT.Square, accum_out=nss[:, t:t + 1]) \
                .then_inc(st.up(act_step), 1)
        act.wait_ge(st.last.sem, st.reached())
        act_rsqrt(st, act, nrr, nss, 1.0 / D, EPS)
        act.wait_ge(st.last.sem, st.reached())
        for t in range(TT):
            act.activation(rows_t[:, t, :], x[:, t, :], ACT.Copy, scale=nrr[:, t:t + 1]).then_inc(st.up(h_ready), 1)

    def act_split(st, act, tiles, name):
        n, nth = tiles.index(name), split_nth(name)
        act.wait_ge(tile_in[n % RING].sem, st.at(tile_in[n % RING], 16 * (n // RING + 1)))
        if not name.endswith(("ff1.0", "ff1.1")):
            act.wait_ge(tile_used.sem, st.at(tile_used, n - 2 + 1 + RING))
        for h in range(2):
            act.activation(w_hi[nth % 2][h][:, :], ring[n % RING][:, h * HALF:(h + 1) * HALF], ACT.Copy) \
                .then_inc(st.up(w_hi_ready), 1)

    def dve_split(st, dve, tiles, name):
        n, nth = tiles.index(name), split_nth(name)
        for h in range(2):
            c = slice(h * HALF, (h + 1) * HALF)
            dve.wait_ge(w_hi_ready.sem, st.at(w_hi_ready, 2 * nth + h + 1))
            dve.tensor_tensor(w_lo[n % RING][:, c], ring[n % RING][:, c], w_hi[nth % 2][h][:, :].bitcast(F32), ALU.subtract) \
                .then_inc(st.up(w_lo_ready), 1)

    def mlp_tile(pre, n):
        return f"{pre}ff{n // 8 + 1}.{n % 8}"

    def act_mlp(st, act, wide_, pre, tiles):
        for n in range(1, MLP_TILES):
            act_split(st, act, tiles, mlp_tile(pre, n))
            for f in ((2 * n - 2, 2 * n - 1) if n <= FB // 4 else ()):
                b, nth = wide_.next(f"{pre}f{f}")
                act.wait_ge(wide_.ready.sem, st.at(wide_.ready, nth))
                hi, h = (v[:, 2 * f:2 * f + 2, :].rearrange("p f t -> p (f t)") for v in (hid_hi, hid_f))
                act.activation(h, b, ACT.Relu).then_inc(st.up(wide_.saved), 1)
                act.wait_ge(st.last.sem, st.reached())
                act.activation(h, h, ACT.Square).then_inc(st.up(act_step), 1)
                act.wait_ge(st.last.sem, st.reached())
                act.activation(hi, h, ACT.Copy).then_inc(st.up(hid_hi_ready), 1)

    def dve_mlp(st, dve, pre, tiles):
        for n in range(1, MLP_TILES):
            dve_split(st, dve, tiles, mlp_tile(pre, n))
            for f in ((2 * n - 2, 2 * n - 1) if n <= FB // 4 else ()):
                hi, lo, h = (v[:, 2 * f:2 * f + 2, :] for v in (hid_hi, hid_lo, hid_f))
                dve.wait_ge(hid_hi_ready.sem, st.at(hid_hi_ready, FB // 2 * mlp_nth(pre) + f + 1))
                dve.tensor_tensor(lo, h, hi.bitcast(F32), ALU.subtract).then_inc(st.up(hid_lo_ready), 1)

    def act_layer(act, st):
        wide_, aux_ = wide.again(WIDE), aux.again(AUX)

        def save_chunk(c):
            m = min(BANK, D_IN - c * BANK)
            for t in range(TT):
                b, nth = wide_.next(f"c{c}t{t}")
                act.wait_ge(wide_.ready.sem, st.at(wide_.ready, nth))
                act.activation(z[:, t, c * BANK:c * BANK + m], b[:, 0:m], ACT.Copy).then_inc(st.up(wide_.saved), 1)

        def exps(b):
            _, _, nh = BATCHES[b]
            view, keys = batch_view(b)
            act.wait_ge(max_ready.sem, st.at(max_ready, b + 1))
            e = rows[:, :].rearrange("p (i n) -> p i n", n=keys)
            for n in range(2 * nh):
                act.activation(e[:, n, :], view[:, n, :], ACT.Exp, bias=mx[:, n:n + 1],
                                     accum_out=sums[:, n:n + 1]) \
                    .then_inc(st.up(exp_ready if n == 2 * nh - 1 else act_step), 1)

        act.wait_ge(aux.saved.sem, st.at(aux.saved, 2))
        act_norm(st, act)
        for c in range(3):
            save_chunk(c)
        act.wait_ge(st.last.sem, st.reached())
        act.activation(sq, z[:, :, 0:1152], ACT.Square).then_inc(st.up(sq_ready), 1)
        act.activation(gates, z[:, :, Z_GATE:Z_GATE + 24], ACT.Exp, scale=-1.0).then_inc(st.up(gate_exp), 1)
        act.wait_ge(ss_ready.sem, st.at(ss_ready, 1))
        act_rsqrt(st, act, rr36, ss36, 1.0 / DH, EPS, rr_ready)
        save_chunk(3)
        save_chunk(4)
        for n, name in enumerate(("hk", "hv")):
            b, nth = wide_.next(name)
            act.wait_ge(wide_.ready.sem, st.at(wide_.ready, nth))
            act.activation(hc[:, n * CMP_HID:(n + 1) * CMP_HID], b[0:32, 0:CMP_HID], ACT.Copy) \
                .then_inc(st.up(wide_.saved), 1)
        exps(0)
        act.wait_ge(gelu_arg.sem, st.at(gelu_arg, 1))
        act.activation(he, hu, ACT.Exp, scale=-2.0 * (2.0 / np.pi) ** 0.5).then_inc(st.up(gelu_exp), 1)
        save_chunk(5)
        act.wait_ge(kc_ss.sem, st.at(kc_ss, 1))
        act_rsqrt(st, act, krr, kss, 1.0 / DH, EPS, kc_rr)
        save_chunk(6)
        act.wait_ge(cmp_arg.sem, st.at(cmp_arg, 1))
        act.activation(pc.rearrange("p t h n -> p (t h n)"), pc.rearrange("p t h n -> p (t h n)"), ACT.Exp) \
            .then_inc(st.up(cmp_exp), 1)
        exps(1)
        save_chunk(7)
        b, nth = wide_.next("o0")
        act.wait_ge(wide_.ready.sem, st.at(wide_.ready, nth))
        act.activation(z[:, 0, Z_Q:Z_Q + 512], b, ACT.Copy).then_inc(st.up(wide_.saved), 1)
        exps(2)
        save_chunk(8)
        act.wait_ge(st.last.sem, st.reached())
        act.activation(z[:, :, Z_MA:Z_MB], z[:, :, Z_MA:Z_MB], ACT.Exp, scale=-1.0).then_inc(st.up(merge_exp), 1)
        b, nth = wide_.next("o1")
        act.wait_ge(wide_.ready.sem, st.at(wide_.ready, nth))
        act.activation(z[:, 1, Z_Q:Z_Q + 512], b, ACT.Copy).then_inc(st.up(wide_.saved), 1)
        save_chunk(9)
        for t in range(TT):
            b, nth = wide_.next(f"yr{t}")
            act.wait_ge(wide_.ready.sem, st.at(wide_.ready, nth))
            act.activation(z[:, t, Z_RQ:Z_RQ + 512], b, ACT.Copy).then_inc(st.up(wide_.saved), 1)
        act.wait_ge(st.last.sem, st.reached())
        act.activation(sq[:, :, 0:512], z[:, :, Z_RQ:Z_RQ + 512], ACT.Square).then_inc(st.up(yr_sq), 1)
        act.activation(tmp[:, 0:1024].rearrange("p (t n) -> p t n", t=TT), z[:, :, Z_RG:Z_RG + 512], ACT.Exp,
                             scale=-1.0).then_inc(st.up(silu_exp), 1)
        act.wait_ge(yr_ss.sem, st.at(yr_ss, 1))
        act_rsqrt(st, act, yrr, yss, 1.0 / RD, EPS, yr_rr)
        save_chunk(10)
        act.wait_ge(st.last.sem, st.reached())
        act.activation(z[:, :, Z_MB:D_IN], z[:, :, Z_MB:D_IN], ACT.Exp, scale=-1.0).then_inc(st.up(merge_exp), 1)
        act.wait_ge(mix_ready.sem, st.at(mix_ready, 4))
        act_split(st, act, TILES, "ff1.0")
        act.wait_ge(aux_.saved.sem, st.at(aux_.saved, aux_.nth_save("out3")))
        act_norm(st, act)
        act.wait_ge(ht_split.sem, st.at(ht_split, 4))
        act_mlp(st, act, wide_, "", TILES)
        act.wait_ge(ff2_saved.sem, st.at(ff2_saved, 4))
        act_norm(st, act)
        for n in range(4):
            c, t = divmod(n, 2)
            b, nth = wide_.next(f"g{n}")
            act.wait_ge(wide_.ready.sem, st.at(wide_.ready, nth))
            act.activation(rows_t[:, t, c * BANK:(c + 1) * BANK], b, ACT.Exp, scale=-1.0).then_inc(st.up(wide_.saved), 1)

    def dve_layer(dve, st):
        wide_, aux_ = wide.again(WIDE), aux.again(AUX)

        def tt(o, a, b, op):
            return dve.tensor_tensor(o, a, b, op)

        def tsc(o, a, s1, op0, s2=None, op1=None):
            return dve.tensor_scalar(o, a, s1, s2, op0, op1) if op1 else dve.tensor_scalar(o, a, s1, None, op0)

        def copy(o, a):
            return dve.tensor_copy(o, a)

        def sigmoid_of_exp(ap):
            tsc(ap, ap, 1.0, ALU.add).then_inc(st.up(dve_step), 1)
            dve.wait_ge(st.last.sem, st.reached())
            dve.reciprocal(ap, ap).then_inc(st.up(dve_step), 1)

        def save_turned(names, gain):
            for n, name in enumerate(names):
                t, half = divmod(n, 2)
                b, nth = aux_.next(name)
                dve.wait_ge(aux_.ready.sem, st.at(aux_.ready, nth))
                o = hT[:, 4 * half:4 * half + 4, t * P:(t + 1) * P]
                b4 = b.rearrange("p (k t) -> p k t", t=P)
                tt(o, b4, bc(cols[:, gain + 4 * half:gain + 4 * half + 4], 2, P), ALU.mult).then_inc(st.up(aux_.saved), 1)

        def maxima(b):
            t, _, nh = BATCHES[b]
            view, keys = batch_view(b)
            dve.wait_ge(scores_ready.sem, st.at(scores_ready, b + 1))
            diag = view[:, :, t * P:(t + 1) * P]
            tt(diag, diag, bc(K["causal"], 1, 2 * nh), ALU.add).then_inc(st.up(dve_step), 1)
            dve.wait_ge(st.last.sem, st.reached())
            dve.tensor_reduce(mx[:, 0:2 * nh], view, AX_X, ALU.max, negate=True).then_inc(st.up(max_ready), 1)

        def probabilities(b):
            t, h0, nh = BATCHES[b]
            _, keys = batch_view(b)
            dve.wait_ge(exp_ready.sem, st.at(exp_ready, b + 1))
            dve.reciprocal(wts[:, 0:2 * nh], sums[:, 0:2 * nh]).then_inc(st.up(dve_step), 1)
            dve.wait_ge(st.last.sem, st.reached())
            w = wts[:, 0:2 * nh].rearrange("p (h k) -> p h k", k=2)
            tt(w, w, gates[:, t, 8:24].rearrange("p (k h) -> p h k", k=2)[:, h0:h0 + nh, :], ALU.mult) \
                .then_inc(st.up(dve_step), 1)
            dve.wait_ge(st.last.sem, st.reached())
            e = rows[:, :].rearrange("p (i n) -> p i n", n=keys)
            tt(e, e, bc(wts[:, 0:2 * nh], 2, keys), ALU.mult).then_inc(st.up(probs_ready), 1)

        def save_probs(b):
            for n in range(4):
                bk, nth = aux_.next(f"pt{b}.{n}")
                dve.wait_ge(aux_.ready.sem, st.at(aux_.ready, nth))
                copy(scr[:, n * BANK:(n + 1) * BANK], bk).then_inc(st.up(aux_.saved), 1)

        b, nth = aux_.next("cols")
        dve.wait_ge(aux_.ready.sem, st.at(aux_.ready, nth))
        copy(cols, b[:, 0:64]).then_inc(st.up(aux_.saved), 1)
        dve.wait_ge(st.last.sem, st.reached())
        save_turned([f"n{n}" for n in range(4)], C_MIX)
        dve.wait_ge(sq_ready.sem, st.at(sq_ready, 1))
        dve.tensor_reduce(ss36.rearrange("p (t n) -> p t n", t=TT), sq.rearrange("p t (n d) -> p t n d", d=DH),
                                AX_X, ALU.add).then_inc(st.up(ss_ready), 1)
        dve.wait_ge(gate_exp.sem, st.at(gate_exp, 1))
        sigmoid_of_exp(gates)
        dve.wait_ge(rr_ready.sem, st.at(rr_ready, 1))
        rr = rr36.rearrange("p (t n) -> p t n", t=TT)
        for t in range(TT):
            tt(qn[:, t, :].rearrange("p (h g d) -> p g h d", g=GROUPS, d=DH),
               z[:, t, Z_Q:Z_Q + 512].rearrange("p (g h d) -> p g h d", g=GROUPS, d=DH),
               bc(rr[:, t, 0:8].rearrange("p (g h) -> p g h", g=GROUPS), 3, DH), ALU.mult).then_inc(st.up(dve_step), 1)
        for n, (col, r0, nh) in enumerate(((Z_KS, 12, 2), (Z_KW, 16, 2))):
            v = z[:, :, col:col + nh * DH].rearrange("p t (h d) -> p t h d", d=DH)
            tt(v, v, bc(rr[:, :, r0:r0 + nh], 3, DH), ALU.mult).then_inc(st.up(heads_ready if n == 1 else dve_step), 1)
        for t in range(TT):
            b, nth = aux_.next(f"q{t}")
            dve.wait_ge(aux_.ready.sem, st.at(aux_.ready, nth))
            tsc(qT[:, :, t * P:(t + 1) * P], b.rearrange("p (k t) -> p k t", t=P), cols[:, C_Q:C_Q + 1], ALU.mult,
                DH ** -0.5, ALU.mult).then_inc(st.up(aux_.saved), 1)
        b, nth = aux_.next("k")
        dve.wait_ge(aux_.ready.sem, st.at(aux_.ready, nth))
        tsc(kT.rearrange("p k t -> p (k t)"), b, cols[:, C_K:C_K + 1], ALU.mult).then_inc(st.up(aux_.saved), 1)
        b, nth = aux_.next("zc")
        dve.wait_ge(aux_.ready.sem, st.at(aux_.ready, nth))
        bz = b.rearrange("p (k t) -> p k t", k=2)
        for g in range(GROUPS):
            src = bz[64 * g:64 * g + 64]
            copy(zT2[0:64, :, g, 0:S], src).then_inc(st.up(dve_step), 1)
            copy(zT2[64:128, :, g, 0:S - 1], src[:, :, 1:S]).then_inc(st.up(dve_step), 1)
            copy(zT2[0:64, :, g, S:272], src[:, :, S - 1:S].broadcast_to([64, 2, 16])).then_inc(st.up(dve_step), 1)
            copy(zT2[64:128, :, g, S - 1:272], src[:, :, S - 1:S].broadcast_to([64, 2, 17])) \
                .then_inc(st.up(aux_.saved if g == 1 else dve_step), 1)
        dve.wait_ge(st.last.sem, st.reached())
        for kind in range(2):
            for g in range(GROUPS):
                for jh in range(2):
                    src = zT2[:, kind, g, 16 * jh:16 * jh + S].rearrange("p (n j l) -> p j n l", j=8, l=2)[:, :, :, 0]
                    pos = cols[:, C_POS + 16 * kind + 8 * jh:C_POS + 16 * kind + 8 * jh + 8]
                    tt(zb2[:, kind, 8 * jh:8 * jh + 8, g, :], src, bc(pos, 2, NCMP), ALU.add) \
                        .then_inc(st.up(zb_ready if kind == g == jh == 1 else dve_step), 1)
        maxima(0)
        dve.wait_ge(wide_.saved.sem, st.at(wide_.saved, wide_.nth_save("hv")))
        tt(hu, hc, hc, ALU.mult).then_inc(st.up(dve_step), 1)
        dve.wait_ge(st.last.sem, st.reached())
        tsc(hu, hu, 0.044715, ALU.mult, 1.0, ALU.add).then_inc(st.up(dve_step), 1)
        dve.wait_ge(st.last.sem, st.reached())
        tt(hu, hu, hc, ALU.mult).then_inc(st.up(gelu_arg), 1)
        dve.wait_ge(gelu_exp.sem, st.at(gelu_exp, 1))
        sigmoid_of_exp(he)
        dve.wait_ge(st.last.sem, st.reached())
        tt(hc, hc, he, ALU.mult).then_inc(st.up(gelu_ready), 1)
        probabilities(0)
        b, nth = aux_.next("hidT")
        dve.wait_ge(aux_.ready.sem, st.at(aux_.ready, nth))
        copy(hidT.rearrange("p k h (r m) -> p (k h) r m", r=4),
             bc(b[:, 0:P].rearrange("p (n m) -> p n m", m=32), 2, 4)).then_inc(st.up(aux_.saved), 1)
        b, nth = aux_.next("w2")
        dve.wait_ge(aux_.ready.sem, st.at(aux_.ready, nth))
        copy(kvc, b[:, 0:P]).then_inc(st.up(aux_.saved), 1)
        dve.wait_ge(st.last.sem, st.reached())
        tt(kcd[:, 0, :], kvc[:, 0:DH], kvc[:, 0:DH], ALU.mult).then_inc(st.up(dve_step), 1)
        dve.wait_ge(st.last.sem, st.reached())
        dve.tensor_reduce(kss, kcd[:, 0, :], AX_X, ALU.add).then_inc(st.up(kc_ss), 1)
        dve.wait_ge(kc_rr.sem, st.at(kc_rr, 1))
        for u in range(2):
            tsc(kcd[:, u, :], kvc[:, 0:DH], krr, ALU.mult).then_inc(st.up(dve_step), 1)
        tt(vz, bc(kvc[:, DH:2 * DH], 1, 4), bc(K["own_rows"], 2, DH), ALU.mult).then_inc(st.up(kc_ready), 1)
        b, nth = aux_.next("kcT")
        dve.wait_ge(aux_.ready.sem, st.at(aux_.ready, nth))
        for g in range(GROUPS):
            r = slice(64 * g, 64 * g + 64)
            tsc(kcT[r, g, :], b[r, 0:32], cols[r, C_K:C_K + 1], ALU.mult) \
                .then_inc(st.up(aux_.saved if g else dve_step), 1)
        for t in range(TT):
            b, nth = aux_.next(f"cmp{t}")
            dve.wait_ge(aux_.ready.sem, st.at(aux_.ready, nth))
            m = K["cmp_add"].rearrange("p (t g n) -> p t g n", t=TT, g=GROUPS)[:, t]
            tt(pc[:, t].rearrange("p (g h) n -> p g h n", g=GROUPS),
               b[:, 0:S].rearrange("p (g h n) -> p g h n", g=GROUPS, n=32), bc(m, 2, 4), ALU.add) \
                .then_inc(st.up(aux_.saved), 1)
        dve.wait_ge(st.last.sem, st.reached())
        pc2 = pc.rearrange("p t h n -> p (t h) n")
        dve.tensor_reduce(cmx, pc2, AX_X, ALU.max).then_inc(st.up(dve_step), 1)
        dve.wait_ge(st.last.sem, st.reached())
        tt(pc2, pc2, bc(cmx, 2, 32), ALU.subtract).then_inc(st.up(cmp_arg), 1)
        save_probs(0)
        dve.wait_ge(cmp_exp.sem, st.at(cmp_exp, 1))
        for t in range(TT):
            m = K["cmp_keep"].rearrange("p (t g n) -> p t g n", t=TT, g=GROUPS)[:, t]
            v = pc[:, t].rearrange("p (g h) n -> p g h n", g=GROUPS)
            tt(v, v, bc(m, 2, 4), ALU.mult).then_inc(st.up(dve_step), 1)
        dve.wait_ge(st.last.sem, st.reached())
        dve.tensor_reduce(csum, pc2, AX_X, ALU.add).then_inc(st.up(dve_step), 1)
        dve.wait_ge(st.last.sem, st.reached())
        tsc(csum, csum, 1e-30, ALU.max).then_inc(st.up(dve_step), 1)
        dve.wait_ge(st.last.sem, st.reached())
        dve.reciprocal(csum, csum).then_inc(st.up(dve_step), 1)
        dve.wait_ge(st.last.sem, st.reached())
        cs2 = csum.rearrange("p (t h) -> p t h", t=TT)
        tt(cs2, cs2, gates[:, :, 0:8], ALU.mult).then_inc(st.up(dve_step), 1)
        dve.wait_ge(st.last.sem, st.reached())
        tt(pc2, pc2, bc(csum, 2, 32), ALU.mult).then_inc(st.up(cmp_ready), 1)
        maxima(1)
        b, nth = aux_.next("pcT")
        dve.wait_ge(aux_.ready.sem, st.at(aux_.ready, nth))
        copy(pcT.rearrange("p b t -> p (b t)"), b).then_inc(st.up(aux_.saved), 1)
        probabilities(1)
        dve.wait_ge(wide_.saved.sem, st.at(wide_.saved, wide_.nth_save("o0")))
        save_probs(1)
        maxima(2)
        probabilities(2)
        aux_names = [f"pt2.{n}" for n in range(4)]
        for n in range(4):
            bk, nth = aux_.next(aux_names[n])
            dve.wait_ge(aux_.ready.sem, st.at(aux_.ready, nth))
            copy(scr[:, n * BANK:(n + 1) * BANK], bk).then_inc(st.up(aux_.saved), 1)
        for n in range(4):
            a, t = divmod(n, 2)
            b, nth = aux_.next(f"rot{n}")
            dve.wait_ge(aux_.ready.sem, st.at(aux_.ready, nth))
            copy(qkT[:, a, :, t * P:(t + 1) * P], b.rearrange("p (h t) -> p h t", t=P)).then_inc(st.up(aux_.saved), 1)
        dve.wait_ge(merge_inc.sem, st.at(merge_inc, 1))
        dve.reciprocal(z[:, :, Z_MA:Z_MB], z[:, :, Z_MA:Z_MB]).then_inc(st.up(dve_step), 1)
        dve.wait_ge(scores_ready.sem, st.at(scores_ready, 4))
        tt(inner, scores.rearrange("p (h n) -> p h n", n=BANK)[:, :, 0:384],
           K["decay"].rearrange("p (h n) -> p h n", h=RH), ALU.mult).then_inc(st.up(inner_saved), 1)
        b, nth = aux_.next("pT")
        dve.wait_ge(aux_.ready.sem, st.at(aux_.ready, nth))
        copy(pT.rearrange("p k t -> p (k t)"), b).then_inc(st.up(aux_.saved), 1)
        for t in range(TT):
            b, nth = aux_.next(f"ya{t}")
            dve.wait_ge(aux_.ready.sem, st.at(aux_.ready, nth))
            copy(yaT[:, :, t * P:(t + 1) * P], b.rearrange("p (h t) -> p h t", t=P)).then_inc(st.up(aux_.saved), 1)
        dve.wait_ge(yr_sq.sem, st.at(yr_sq, 1))
        dve.tensor_reduce(yss.rearrange("p (t h) -> p t h", t=TT),
                                sq[:, :, 0:512].rearrange("p t (h d) -> p t h d", d=RD), AX_X, ALU.add) \
            .then_inc(st.up(yr_ss), 1)
        dve.wait_ge(silu_exp.sem, st.at(silu_exp, 1))
        sg = tmp[:, 0:1024].rearrange("p (t n) -> p t n", t=TT)
        sigmoid_of_exp(tmp[:, 0:1024])
        dve.wait_ge(st.last.sem, st.reached())
        tt(sg, sg, z[:, :, Z_RG:Z_RG + 512], ALU.mult).then_inc(st.up(dve_step), 1)
        dve.wait_ge(yr_rr.sem, st.at(yr_rr, 1))
        yv = z[:, :, Z_RQ:Z_RQ + 512].rearrange("p t (h d) -> p t h d", d=RD)
        tt(yv, yv, bc(yrr.rearrange("p (t h) -> p t h", t=TT), 3, RD), ALU.mult).then_inc(st.up(dve_step), 1)
        dve.wait_ge(st.last.sem, st.reached())
        yv = z[:, :, Z_RQ:Z_RQ + 512]
        tt(yv, yv, sg, ALU.mult).then_inc(st.up(yr_ready), 1)
        for t in range(TT):
            b, nth = aux_.next(f"yr{t}")
            dve.wait_ge(aux_.ready.sem, st.at(aux_.ready, nth))
            copy(yrT[:, :, t * P:(t + 1) * P], b.rearrange("p (h t) -> p h t", t=P)).then_inc(st.up(aux_.saved), 1)
        for n in range(4):
            c, t = divmod(n, 2)
            b, nth = aux_.next(f"upa{n}")
            dve.wait_ge(aux_.ready.sem, st.at(aux_.ready, nth))
            tt(rows_t[:, t, c * BANK:(c + 1) * BANK], b, z[:, t, Z_MA + c * BANK:Z_MA + (c + 1) * BANK],
               ALU.mult).then_inc(st.up(aux_.saved), 1)
        dve.wait_ge(merge_inc.sem, st.at(merge_inc, 2))
        dve.reciprocal(z[:, :, Z_MB:D_IN], z[:, :, Z_MB:D_IN]).then_inc(st.up(dve_step), 1)
        dve.wait_ge(st.last.sem, st.reached())
        for n in range(4):
            c, t = divmod(n, 2)
            b, nth = aux_.next(f"upb{n}")
            dve.wait_ge(aux_.ready.sem, st.at(aux_.ready, nth))
            u = tmp[:, n * BANK:(n + 1) * BANK]
            tt(u, b, z[:, t, Z_MB + c * BANK:Z_MB + (c + 1) * BANK], ALU.mult).then_inc(st.up(aux_.saved), 1)
            dve.wait_ge(st.last.sem, st.reached())
            r = rows_t[:, t, c * BANK:(c + 1) * BANK]
            tt(r, r, u, ALU.add).then_inc(st.up(mix_ready), 1)
        for n in range(4):
            c, t = divmod(n, 2)
            b, nth = aux_.next(f"m{n}")
            dve.wait_ge(aux_.ready.sem, st.at(aux_.ready, nth))
            copy(hT[:, 4 * c:4 * c + 4, t * P:(t + 1) * P], b.rearrange("p (k t) -> p k t", t=P)) \
                .then_inc(st.up(aux_.saved), 1)
        dve_split(st, dve, TILES, "ff1.0")
        for n in range(4):
            c, t = divmod(n, 2)
            b, nth = aux_.next(f"out{n}")
            dve.wait_ge(aux_.ready.sem, st.at(aux_.ready, nth))
            xv = x[:, t, c * BANK:(c + 1) * BANK]
            tt(xv, xv, b, ALU.add).then_inc(st.up(aux_.saved), 1)
        for n in range(4):
            t, half = divmod(n, 2)
            b, nth = aux_.next(f"nm{n}")
            dve.wait_ge(aux_.ready.sem, st.at(aux_.ready, nth))
            hi, lo, h = (v[:, 4 * half:4 * half + 4, t * P:(t + 1) * P] for v in (ht_hi, ht_lo, ht_f))
            tt(h, b.rearrange("p (k t) -> p k t", t=P), bc(cols[:, C_MLP + 4 * half:C_MLP + 4 * half + 4], 2, P),
               ALU.mult).then_inc(st.up(aux_.saved), 1)
            dve.wait_ge(st.last.sem, st.reached())
            copy(hi, h).then_inc(st.up(dve_step), 1)
            dve.wait_ge(st.last.sem, st.reached())
            tt(lo, h, hi.bitcast(F32), ALU.subtract).then_inc(st.up(ht_split), 1)
        dve_mlp(st, dve, "", TILES)
        for n in range(4):
            c, t = divmod(n, 2)
            dve.wait_ge(ff2_ready.sem, st.at(ff2_ready, n + 1))
            xv = x[:, t, c * BANK:(c + 1) * BANK]
            tt(xv, xv, scores[:, n * BANK:(n + 1) * BANK], ALU.add).then_inc(st.up(ff2_saved), 1)
        save_turned([f"np{n}" for n in range(4)], C_PLE)
        dve.wait_ge(st.last.sem, st.reached())
        dve.wait_ge(wide_.saved.sem, st.at(wide_.saved, wide_.nth_save("g3")))
        tsc(rows[:, :], rows[:, :], 1.0, ALU.add).then_inc(st.up(dve_step), 1)
        dve.wait_ge(st.last.sem, st.reached())
        dve.reciprocal(rows[:, :], rows[:, :]).then_inc(st.up(small_used), 1)
        dve.wait_ge(st.last.sem, st.reached())
        for n in range(4):
            c, t = divmod(n, 2)
            b, nth = aux_.next(f"ple{n}")
            dve.wait_ge(aux_.ready.sem, st.at(aux_.ready, nth))
            u = tmp[:, n * BANK:(n + 1) * BANK]
            tt(u, b, rows_t[:, t, c * BANK:(c + 1) * BANK], ALU.mult).then_inc(st.up(dve_step), 1)
            dve.wait_ge(st.last.sem, st.reached())
            xv = x[:, t, c * BANK:(c + 1) * BANK]
            tt(xv, xv, u, ALU.add).then_inc(st.up(aux_.saved), 1)

    def pool_layer(pool, st):
        pool.wait_ge(wide.again(WIDE).saved.sem, st.at(wide.again(WIDE).saved, wide.again(WIDE).nth_save("c4t1")))
        t4 = [tmp[:, n * 512:(n + 1) * 512].rearrange("p (t h d) -> p t h d", t=TT, d=64) for n in range(4)]
        cos, sin = (bc(K[n].rearrange("p (t d) -> p t d", t=TT), 2, RH) for n in ("cos", "sin"))
        for a, col in enumerate((Z_RQ, Z_RK)):
            v = z[:, :, col:col + 512].rearrange("p t (h u d) -> p t h u d", u=2, d=64)
            x1, x2 = ([v[:, t, :, u, :] for t in range(TT)] for u in range(2))
            for t in range(TT):
                for n, (xx, tab) in enumerate(((x1, cos), (x2, sin), (x1, sin), (x2, cos))):
                    pool.tensor_tensor(t4[n][:, t], xx[t], tab[:, t], ALU.mult).then_inc(st.up(pool_step), 1)
            pool.wait_ge(st.last.sem, st.reached())
            for t in range(TT):
                pool.tensor_tensor(x1[t], t4[0][:, t], t4[1][:, t], ALU.subtract).then_inc(st.up(pool_step), 1)
                pool.tensor_tensor(x2[t], t4[2][:, t], t4[3][:, t], ALU.add) \
                    .then_inc(st.up(rope_ready if a == t == 1 else pool_step), 1)
            if a == 0:
                pool.wait_ge(st.last.sem, st.reached())
        for n, (lo, hi) in enumerate(((Z_MA, Z_MB), (Z_MB, D_IN))):
            pool.wait_ge(merge_exp.sem, st.at(merge_exp, n + 1))
            one = K["ones"][:, 0:1].unsqueeze(1).broadcast_to([P, TT, hi - lo])
            pool.tensor_tensor(z[:, :, lo:hi], z[:, :, lo:hi], one, ALU.add).then_inc(st.up(merge_inc), 1)

    uT = part(0, 1024, "p (b t) -> p b t", t=S)
    sqT = part(1024, 1024, "p (b t) -> p b t", t=S)
    ao = part(1024, 1024, "p (t n) -> p t n", t=TT)
    skT = part(2048, 1024, "p (b t) -> p b t", t=S)
    sv = part(3072, 1024, "p (t n) -> p t n", t=TT)
    BD = part(4096, 1024, "p (r j u c) -> p r j u c", r=2, j=SJ, u=2)
    BT = part(5120, 1024, "p (r q n) -> p r q n", r=2, q=4)
    CT = part(6144, 1024, "p (r i m) -> p r i m", r=2, i=4)
    cin = part(7168, 1024, "p (r i u n) -> p r i u n", r=2, i=4, u=2)
    bin_ = part(8192, 512, "p (r j c) -> p r j c", r=2, j=SJ)
    t1, t2 = part(8704, 512), part(9216, 512)
    wst = [part(9728 + 512 * n, 512) for n in range(2)]
    pu1, pu2 = part(4096, 512), part(4608, 512)
    xst = [part(7168 + 512 * n, 512) for n in range(2)]
    ctab, stab = (big[:, n * 4096:(n + 1) * 4096].rearrange("p (j t) -> p j t", t=S) for n in range(2))
    ln_lo = CONST_AT["cmp_add"][0]
    assert CONST_AT["sin"][1] - ln_lo == 2 * D
    ln_g, ln_b = const[:, ln_lo:ln_lo + D], const[:, ln_lo + D:ln_lo + 2 * D]
    prow = scr[0:16, :].rearrange("p (r n) -> p r n", n=P)
    log_dt, dt = tiny[0:16, 340:342], tiny[0:16, 342:344]
    pcol = tiny[:, 240:320].rearrange("p (r j) -> p r j", j=SJ)
    cm, sm, cn, sn2 = (tiny[:, 400 + 16 * n:416 + 16 * n] for n in range(4))
    neg_b, d_col = tiny[:, 330:334], tiny[:, 334:338]
    zs = rows[:, 0:1536].rearrange("p (h n) -> p h n", h=4)
    sp_ = tmp[:, 0:1536].rearrange("p (h n) -> p h n", h=4)
    sw = scr[:, 0:1536].rearrange("p (h n) -> p h n", h=4)
    yT = hT[:, 4:8, :]
    ge = part(8704, 1024)
    lsum, lmu, lss, lrr = (tiny[:, 350 + 2 * n:352 + 2 * n] for n in range(4))
    dqT = part(0, 2048, "p (b t) -> p b t", t=S)
    dkT = part(2048, 1024, "p (v t) -> p v t", t=S)
    dv = part(3072, 512, "p (t n) -> p t n", t=TT)
    qiT = part(3584, 512, "p (b t) -> p b t", t=S)
    kiz = part(4096, 1024, "p (h t) -> p h t", t=S)
    relu_ = part(5120, 2048)
    isc, irep, iadd = part(7168, 384), part(7552, 384), part(7936, 384)
    m8 = tiny[:, 470:478]
    wi = tiny[:, 480:496]
    dob = big[:, 0:2048].rearrange("p (t n) -> p t n", t=TT)
    (P_LR, P_LI, P_Y, P_TH, P_W, P_E, P_KQ, P_RED, P_HA, P_SN, P_CS, P_SIN, P_CM1, P_COS, P_MAG, P_NR, P_T1,
     P_T2) = range(18)
    P_CR, P_CI, P_ABI, P_DEN = P_Y, P_W, P_SN, P_KQ

    par_in, b_in, c_in, ln_in = sig("par_in"), sig("b_in"), sig("c_in"), sig("ln_in")
    dt_ready, sin_arg, sin_ready, par_ready = sig("dt_ready"), sig("sin_arg"), sig("sin_ready"), sig("par_ready")
    bd_ready = sig("bd_ready")
    sbz_ready, ln1p_ready, sp_ready, sw_arg, sw_ready = (sig(n) for n in (
        "sbz_ready", "ln1p_ready", "sp_ready", "sw_arg", "sw_ready"))
    scan_ready, state_ready, state_used = sig("scan_ready"), sig("state_ready"), sig("state_used")
    ygelu_arg, ygelu_exp, ygelu_ready, y_ready = (sig(n) for n in ("ygelu_arg", "ygelu_exp", "ygelu_ready", "y_ready"))
    ln_stats, ln_done = sig("ln_stats"), sig("ln_done")
    idx_ready, idx_relu, idx_summed = sig("idx_ready"), sig("idx_relu"), sig("idx_summed")
    kiz_zero = sig("kiz_zero")
    dsc_ready, dsc_read, dmax_ready, dexp_ready, dprobs_ready = (sig(n) for n in (
        "dsc_ready", "dsc_read", "dmax_ready", "dexp_ready", "dprobs_ready"))

    DSA_BATCHES = [(0, 0, 16), (1, 0, 8), (1, 8, 8)]

    def dsa_view(b):
        keys = (DSA_BATCHES[b][0] + 1) * P
        return scores.rearrange("p (i n) -> p i n", n=keys), keys

    def slots(b):
        _, h0, nh = DSA_BATCHES[b]
        return [h0 + 2 * n for n in range(nh // 2)] + [h0 + 2 * n + 1 for n in range(nh // 2)]

    def flat(ap):
        return ap.rearrange("p a b -> p (a b)")

    def sp_tail(sp):
        where = Where()
        sp.wait_ge(ff2_saved.sem, DEPTH * ff2_saved.per_layer)

        def load(dst, src, signal):
            sp.dma_start(dst, src).then_inc(signal.sem, 16)

        def load_ln(which, n):
            for dst, v in ((ln_g, "g"), (ln_b, "b")):
                load(dst, I[f"ln_{which}_{v}_2"][n:n + 1, :].broadcast_to([P, D]), ln_in)

        for r, name in ((P_LR, "ssm_lam_re_2"), (P_LI, "ssm_lam_im_2")):
            load(prow[:, r, :], I[name][0].rearrange("(j u) n -> j (u n)", u=2), par_in)
        load(log_dt, I["ssm_log_dt_2"][0].rearrange("(j u) -> j u", u=2), par_in)
        load(vec_rows[0:4, :], I["ssm_d_2"][0].rearrange("(r g) c -> r (g c)", r=4), par_in)
        load(vec_rows[4:8, :], I["ssm_b_glu_2"][0].rearrange("(r n) -> r n", r=4), par_in)
        for r, name in enumerate(("ssm_c_re_2", "ssm_c_im_2")):
            for u in range(2):
                load(cin[:, r, :, u, :], I[name][0].rearrange("(i g) c n -> (g c) i n", i=4), c_in)
        for r, name in enumerate(("ssm_b_re_2", "ssm_b_im_2")):
            load(bin_[:, r], I[name][0].rearrange("(j u) n c -> (u n) j c", u=2), b_in)
        load_ln("mix", 0)
        for n, name in enumerate(TILES2):
            sp.wait_ge(tile_used.sem, where.value(tile_used, n + 1))
            kind, _, num = name.rpartition(".")
            layer = "AB".find(name[0])
            if kind.endswith("ff1"):
                s, k, m = I["mlp_w1_2"][layer][:, int(num) * BANK:(int(num) + 1) * BANK], KT, BANK
            elif kind.endswith("ff2"):
                s, k, m = I["mlp_w2_2"][layer][int(num) * BANK:(int(num) + 1) * BANK, :], 4, D
            elif name == "glu":
                s, k, m = I["ssm_w_glu_2"][0], 4, SB_W
            else:
                w = I[{"sb": "sb_ssm_w_in_2", "sbo": "sb_ssm_w_out_2", "ds": "dsa_w_in_2",
                       "dso": "dsa_w_out_2"}[name[:-1]]][0]
                c = int(name[-1])
                k, m = KT, min(BANK, w.shape[1] - c * BANK)
                s = w[:, c * BANK:c * BANK + m]
            sp.dma_start(w_tile(n, (k, m)), s.rearrange("(k p) n -> p k n", p=P)) \
                .then_inc(tile_in[n % RING].sem, 16)
            if name in ("A.ff1.0", "ds3", "B.ff1.0"):
                done = {"A.ff1.0": 1, "ds3": 2, "B.ff1.0": 3}[name]
                sp.wait_ge(ln_done.sem, done)
                load_ln(*{1: ("ffn", 0), 2: ("mix", 1), 3: ("ffn", 1)}[done])
        sp.wait_ge(ln_done.sem, 4)
        sp.dma_start(out[0].rearrange("(t p) n -> p t n", p=P), x[:, :, :]).then_inc(stored.sem, 16)
        sp.wait_ge(stored.sem, 16)

    def pe_tail(pe, st):
        wide_, aux_ = wide.again(WIDE2), aux.again(AUX2)
        kit = pe_kit(pe, st, wide_, aux_, TILES2)
        mm, tp, next_tile, tile_done = kit.mm, kit.tp, kit.next_tile, kit.tile_done

        def sb_scores(batch):
            for hl in range(4):
                blk, r = (4 * batch + hl) // 2, slice(64 * (hl % 2), 64 * (hl % 2) + 64)
                o = scores[:, hl * BANK:hl * BANK + 384]
                mm(o[:, 0:S], skT[r, blk, 0:P], sqT[r, blk, :], True, True)
                mm(o[:, S:384], skT[r, blk, P:S], sqT[r, blk, P:S], True, True, sbz_ready if hl == 3 else None)

        def suffix_sums(batch):
            pe.wait_ge(sp_ready.sem, st.at(sp_ready, batch + 1))
            for hl in range(4):
                b, nth = aux_.next(f"cs{4 * batch + hl}")
                pe.wait_ge(aux_.saved.sem, st.at(aux_.saved, nth))
                mm(b[:, 0:384], K["suffix"], sp_[:, hl, :], True, False)
                mm(b[:, P:S], K["ones"], sp_[:, hl, S:384], False, True, aux_.ready)

        def sb_values(batch):
            pe.wait_ge(sw_ready.sem, st.at(sw_ready, batch + 1))
            for t in range(TT):
                o, nth = wide_.next(f"s{'AB'[batch]}{t}")
                pe.wait_ge(wide_.saved.sem, st.at(wide_.saved, nth))
                for hl in range(4):
                    h = 4 * batch + hl
                    v = [sv[:, m, h * DH:(h + 1) * DH] for m in range(TT)]
                    terms = [(sw[:, hl, 0:P], v[0])] if t == 0 else [(sw[:, hl, P:S], v[0]), (sw[:, hl, S:384], v[1])]
                    for n, (a, vv) in enumerate(terms):
                        last = n == len(terms) - 1
                        mm(o[:, hl * DH:(hl + 1) * DH], a, vv, n == 0, last, wide_.ready if last and hl == 3 else None)

        def ssm_in(j):
            q, jl = divmod(j, 4)
            r = slice(32 * jl, 32 * jl + 32)
            b, nth = aux_.next(f"bu{j}")
            pe.wait_ge(aux_.saved.sem, st.at(aux_.saved, nth))
            for ri in range(2):
                mm(b[:, ri * S:(ri + 1) * S], BT[r, ri, q, :], uT[r, q, :], True, True, aux_.ready if ri else None)

        y_bank = [None]

        def ssm_out(j):
            q, jl = divmod(j, 4)
            if jl == 0:
                y_bank[0], nth = wide_.next(f"y{q}")
                pe.wait_ge(wide_.saved.sem, st.at(wide_.saved, nth))
            pe.wait_ge(state_ready.sem, st.at(state_ready, j + 1))
            r = slice(32 * jl, 32 * jl + 32)
            for ri in range(2):
                ins = pe.matmul(y_bank[0][r, 0:S], CT[:, ri, q, r], xst[j % 2][:, ri * S:(ri + 1) * S], start=ri == 0, stop=ri == 1)
            ins.then_inc(st.up(wide_.ready if jl == 3 else state_used), 1)

        pe.wait_ge(aux_.saved.sem, st.at(aux_.saved, 2))
        kit.turn_rows([f"A.x{n}" for n in range(4)], x, None, 0)
        pe.wait_ge(c_in.sem, st.at(c_in, 64))
        for ri in range(2):
            b, nth = aux_.next(f"ct{ri}")
            pe.wait_ge(aux_.saved.sem, st.at(aux_.saved, nth))
            for i in range(4):
                tp(b[:, i * P:(i + 1) * P], cin[:, ri, i].rearrange("p u n -> p (u n)"),
                   signal=aux_.ready if i == 3 else None)
        pe.wait_ge(aux_.saved.sem, st.at(aux_.saved, aux_.nth_save("A.x3")))
        w = next_tile("sb3", KT, BANK)
        kit.units_by_tile(wide_, ["u0", "u1"], w)
        tile_done()
        w = next_tile("sb0", KT, BANK)
        kit.units_by_tile(wide_, ["sq0", "sq1"], w)
        tile_done()
        pe.wait_ge(par_ready.sem, st.at(par_ready, 1))
        b, nth = aux_.next("par")
        pe.wait_ge(aux_.saved.sem, st.at(aux_.saved, nth))
        for n, r in enumerate((P_CR, P_CI, P_MAG, P_COS, P_SIN)):
            tp(b[:, n * SJ:(n + 1) * SJ], prow[:, r, :], 16)
        tp(b[:, 80:144], vec_rows, 64, aux_.ready)
        w = next_tile("sb1", KT, BANK)
        kit.units_by_tile(wide_, ["sk0", "sk1"], w)
        tile_done()
        w = next_tile("sb2", KT, BANK)
        kit.rows_by_tile(wide_, ["sv0", "sv1"], hT, w, KT)
        tile_done()
        pe.wait_ge(bd_ready.sem, st.at(bd_ready, 1))
        for ri in range(2):
            b, nth = aux_.next(f"bt{ri}")
            pe.wait_ge(aux_.saved.sem, st.at(aux_.saved, nth))
            for q in range(4):
                tp(b[:, q * P:(q + 1) * P], BD[:, ri, 4 * q:4 * q + 4].rearrange("p j u c -> p (j u c)"),
                   signal=aux_.ready if q == 3 else None)
        pe.wait_ge(wide_.saved.sem, st.at(wide_.saved, wide_.nth_save("sk1")))
        sb_scores(0)
        pe.wait_ge(aux_.saved.sem, st.at(aux_.saved, aux_.nth_save("bt1")))
        for j in range(SJ + 2):
            if j < SJ:
                ssm_in(j)
            if j == 1:
                suffix_sums(0)
                sb_scores(1)
            if j == 8:
                suffix_sums(1)
            if j >= 2:
                ssm_out(j - 2)
            if j in (5, 9):
                sb_values(j // 8)
        pe.wait_ge(ygelu_ready.sem, st.at(ygelu_ready, 1))
        w = next_tile("glu", 4, SB_W)
        for n in range(2):
            b, nth = wide_.next(f"glu{n}")
            pe.wait_ge(wide_.saved.sem, st.at(wide_.saved, nth))
            for u in range(2):
                lo = (2 * n + u) * P
                for k in range(4):
                    mm(b[:, u * S:(u + 1) * S], w[:, k, lo:lo + P], yT[:, k, :], k == 0, k == 3,
                       wide_.ready if u == 1 and k == 3 else None)
        tile_done()
        pe.wait_ge(wide_.saved.sem, st.at(wide_.saved, wide_.nth_save("sB1")))
        for t in range(TT):
            b, nth = aux_.next(f"ao{t}")
            pe.wait_ge(aux_.saved.sem, st.at(aux_.saved, nth))
            for k in range(4):
                tp(b[:, k * P:(k + 1) * P], ao[:, t, k * P:(k + 1) * P], signal=aux_.ready if k == 3 else None)
        pe.wait_ge(aux_.saved.sem, st.at(aux_.saved, aux_.nth_save("ao1")))
        pe.wait_ge(y_ready.sem, st.at(y_ready, 1))

        def project_and_mlp(pre, name, norm):
            for c in range(2):
                w = next_tile(f"{name}{c}", KT, BANK)
                kit.rows_by_tile(aux_, [f"{pre}out{2 * c + t}" for t in range(TT)], hT, w, KT)
                tile_done()
            pe.wait_ge(ln_done.sem, st.at(ln_done, norm))
            kit.turn_rows([f"{pre}n{n}" for n in range(4)], x, None, 0)
            pe.wait_ge(aux_.saved.sem, st.at(aux_.saved, aux_.nth_save(f"{pre}n3")))
            kit.mlp(pre)

        project_and_mlp("A.", "sbo", 1)
        pe.wait_ge(ln_done.sem, st.at(ln_done, 2))
        kit.turn_rows([f"B.x{n}" for n in range(4)], x, None, 0)
        pe.wait_ge(aux_.saved.sem, st.at(aux_.saved, aux_.nth_save("B.x3")))
        w = next_tile("ds3", KT, DSA_IN - I_QI)
        kit.units_by_tile(wide_, ["qi"], w)
        b, nth = wide_.next("kiw")
        pe.wait_ge(wide_.saved.sem, st.at(wide_.saved, nth))
        for k in range(KT):
            mm(b[0:32, 0:S], w[:, k, I_KI - I_QI:I_WI - I_QI], hT[:, k, :], k == 0, k == KT - 1)
        for t in range(TT):
            for k in range(KT):
                mm(b[:, S + 8 * t:S + 8 * t + 8], hT[:, k, t * P:(t + 1) * P], w[:, k, I_WI - I_QI:DSA_IN - I_QI],
                   k == 0, k == KT - 1, wide_.ready if t == 1 and k == KT - 1 else None)
        tile_done()

        def index_scores(t):
            if t == 0:
                pe.wait_ge(wide_.saved.sem, st.at(wide_.saved, wide_.nth_save("kiw")))
            else:
                pe.wait_ge(idx_relu.sem, st.at(idx_relu, 1))
            keys = (t + 1) * P
            for h in range(IDX_HEADS):
                mm(scores[:, h * keys:(h + 1) * keys], qiT[:, h // 4, t * P:(t + 1) * P], kiz[:, h % 4, 0:keys],
                   True, True, idx_ready if h == IDX_HEADS - 1 else None)

        pe.wait_ge(ff2_saved.sem, st.at(ff2_saved, 4))
        index_scores(0)
        w = next_tile("ds2", KT, BANK)
        kit.units_by_tile(wide_, ["dk"], w)
        b, nth = wide_.next("dv")
        pe.wait_ge(wide_.saved.sem, st.at(wide_.saved, nth))
        for t in range(TT):
            for k in range(KT):
                mm(b[:, t * S:(t + 1) * S], hT[:, k, t * P:(t + 1) * P], w[:, k, S:2 * S], k == 0, k == KT - 1,
                   wide_.ready if t == 1 and k == KT - 1 else None)
        tile_done()
        index_scores(1)
        for c in range(2):
            w = next_tile(f"ds{c}", KT, BANK)
            kit.units_by_tile(wide_, [f"dq{2 * c}", f"dq{2 * c + 1}"], w)
            tile_done()

        def dsa_scores(b):
            t, _, _ = DSA_BATCHES[b]
            view, keys = dsa_view(b)
            if b == 0:
                pe.wait_ge(idx_relu.sem, st.at(idx_relu, 2))
                pe.wait_ge(wide_.saved.sem, st.at(wide_.saved, wide_.nth_save("dq3")))
            else:
                pe.wait_ge(dsc_read.sem, st.at(dsc_read, b))
            hs = slots(b)
            for n, h in enumerate(hs):
                r = slice(64 * (h % 2), 64 * (h % 2) + 64)
                mm(view[:, n, :], dqT[r, h // 2, t * P:(t + 1) * P], dkT[r, h // 4, 0:keys], True, True,
                   dsc_ready if n == len(hs) - 1 else None)

        def dsa_probs(b):
            pe.wait_ge(dprobs_ready.sem, st.at(dprobs_ready, b + 1))
            for n in range(4):
                bk, nth = aux_.next(f"pt{b}.{n}")
                pe.wait_ge(aux_.saved.sem, st.at(aux_.saved, nth))
                for k in range(4):
                    lo = (4 * n + k) * P
                    tp(bk[:, k * P:(k + 1) * P], rows[:, lo:lo + P], signal=aux_.ready if k == 3 else None)

        def dsa_values(b):
            t, h0, nh = DSA_BATCHES[b]
            pe.wait_ge(aux_.saved.sem, st.at(aux_.saved, aux_.nth_save(f"pt{b}.3")))
            place = {h: n for n, h in enumerate(slots(b))}
            for half in range(nh // 8):
                o, nth = wide_.next(f"do{b + 1 if b else half}")
                pe.wait_ge(wide_.saved.sem, st.at(wide_.saved, nth))
                for hl in range(8):
                    h = h0 + 8 * half + hl
                    for kt in range(t + 1):
                        last = kt == t
                        mm(o[:, hl * DH:(hl + 1) * DH], ptb[:, place[h] * (t + 1) + kt, :],
                           dv[:, kt, (h // 4) * DH:(h // 4 + 1) * DH], kt == 0, last,
                           wide_.ready if last and hl == 7 else None)

        dsa_scores(0)
        dsa_scores(1)
        dsa_probs(0)
        dsa_values(0)
        dsa_scores(2)
        dsa_probs(1)
        dsa_values(1)
        dsa_probs(2)
        dsa_values(2)
        pe.wait_ge(wide_.saved.sem, st.at(wide_.saved, wide_.nth_save("do3")))
        kit.turn_rows([f"do{n}" for n in range(4)], dob, None, 0)
        pe.wait_ge(aux_.saved.sem, st.at(aux_.saved, aux_.nth_save("do3")))
        project_and_mlp("B.", "dso", 3)

    def act_tail(act, st):
        wide_, aux_ = wide.again(WIDE2), aux.again(AUX2)
        norm = [0]

        def save(name, dst, lo=0, hi=BANK, scale=1.0, rows_=slice(0, P), last=True):
            b, nth = wide_.next(name)
            act.wait_ge(wide_.ready.sem, st.at(wide_.ready, nth))
            act.activation(dst, b[rows_, lo:hi], ACT.Copy, scale=scale) \
                .then_inc(st.up(wide_.saved if last else act_step), 1)
            return b

        def ln_statistics():
            for t in range(TT):
                act.activation(rows_t[:, t, :], x[:, t, :], ACT.Copy, accum_out=lsum[:, t:t + 1]) \
                    .then_inc(st.up(act_step), 1)
            act.wait_ge(st.last.sem, st.reached())
            act.activation(lmu, lsum, ACT.Copy, scale=-1.0 / D).then_inc(st.up(act_step), 1)
            act.wait_ge(st.last.sem, st.reached())
            for t in range(TT):
                act.activation(rows_t[:, t, :], x[:, t, :], ACT.Square, bias=lmu[:, t:t + 1],
                                     accum_out=lss[:, t:t + 1]).then_inc(st.up(act_step), 1)
            act.wait_ge(st.last.sem, st.reached())
            act_rsqrt(st, act, lrr, lss, 1.0 / D, LN_EPS, ln_stats)

        act.wait_ge(par_in.sem, st.at(par_in, 16 * 5))
        act.activation(dt, log_dt, ACT.Exp).then_inc(st.up(dt_ready), 1)
        act.wait_ge(sin_arg.sem, st.at(sin_arg, 1))
        act.activation(prow[:, P_SN, :], prow[:, P_RED, :], ACT.Sin).then_inc(st.up(act_step), 1)
        act.activation(prow[:, P_CS, :], prow[:, P_HA, :], ACT.Sin, bias=half_pi[0:16, :], scale=-1.0) \
            .then_inc(st.up(sin_ready), 1)
        for n in range(2):
            save(f"u{n}", flat(uT[:, 2 * n:2 * n + 2, :]))
        for n in range(2):
            save(f"sq{n}", flat(sqT[:, 2 * n:2 * n + 2, :]), scale=DH ** -0.5)
        for n in range(2):
            save(f"sk{n}", flat(skT[:, 2 * n:2 * n + 2, :]))
        for t in range(TT):
            save(f"sv{t}", sv[:, t, :])

        def softplus_parts(batch):
            act.wait_ge(sbz_ready.sem, st.at(sbz_ready, batch + 1))
            v = scores.rearrange("p (h n) -> p h n", n=BANK)[:, :, 0:384]
            if batch:
                act.wait_ge(st.last.sem, st.reached())
            act.activation(sp_, v, ACT.Abs).then_inc(st.up(act_step), 1)
            act.activation(zs, v, ACT.Copy).then_inc(st.up(act_step), 1)
            act.wait_ge(st.last.sem, st.reached())
            act.activation(sp_, sp_, ACT.Exp, scale=-1.0).then_inc(st.up(act_step), 1)
            act.wait_ge(st.last.sem, st.reached())
            act.activation(sp_, sp_, ACT.Ln, bias=1.0).then_inc(st.up(ln1p_ready), 1)

        def weights(batch):
            act.wait_ge(sw_arg.sem, st.at(sw_arg, batch + 1))
            act.activation(sw, zs, ACT.Exp).then_inc(st.up(sw_ready), 1)

        def save_sb(batch):
            for t in range(TT):
                save(f"s{'AB'[batch]}{t}", ao[:, t, batch * S:(batch + 1) * S], 0, S)

        softplus_parts(0)
        weights(0)
        softplus_parts(1)
        save("y0", yT[:, 0, :], 0, S)
        save_sb(0)
        weights(1)
        save("y1", yT[:, 1, :], 0, S)
        save_sb(1)
        save("y2", yT[:, 2, :], 0, S)
        save("y3", yT[:, 3, :], 0, S)
        act.wait_ge(ygelu_arg.sem, st.at(ygelu_arg, 1))
        act.activation(ge, ge, ACT.Exp, scale=-2.0 * (2.0 / np.pi) ** 0.5).then_inc(st.up(ygelu_exp), 1)
        for n in range(2):
            b, nth = wide_.next(f"glu{n}")
            act.wait_ge(wide_.ready.sem, st.at(wide_.ready, nth))
            for u in range(2):
                blk = 2 * n + u
                if blk == 0:
                    act.wait_ge(ygelu_ready.sem, st.at(ygelu_ready, 1))
                act.activation(ge[:, blk * S:(blk + 1) * S], b[:, u * S:(u + 1) * S], ACT.Exp,
                                     bias=neg_b[:, blk:blk + 1], scale=-1.0) \
                    .then_inc(st.up(wide_.saved if u else act_step), 1)
        act.wait_ge(y_ready.sem, st.at(y_ready, 1))
        act_split(st, act, TILES2, "A.ff1.0")
        act.wait_ge(aux_.saved.sem, st.at(aux_.saved, aux_.nth_save("A.out3")))
        ln_statistics()
        act_mlp(st, act, wide_, "A.", TILES2)
        act.wait_ge(ff2_saved.sem, st.at(ff2_saved, 4))
        ln_statistics()
        save("qi", flat(qiT))
        b, nth = wide_.next("kiw")
        act.wait_ge(wide_.ready.sem, st.at(wide_.ready, nth))
        act.wait_ge(kiz_zero.sem, st.at(kiz_zero, 1))
        for hl in range(4):
            act.activation(kiz[32 * hl:32 * hl + 32, hl, :], b[0:32, 0:S], ACT.Copy).then_inc(st.up(act_step), 1)
        act.activation(wi, b[:, S:S + 16], ACT.Copy, scale=IDX_DIM ** -0.5 * IDX_HEADS ** -0.5) \
            .then_inc(st.up(wide_.saved), 1)

        def index_relu(t):
            act.wait_ge(idx_ready.sem, st.at(idx_ready, t + 1))
            if t:
                act.wait_ge(idx_summed.sem, st.at(idx_summed, 1))
            n = IDX_HEADS * (t + 1) * P
            act.activation(relu_[:, 0:n], scores[:, 0:n], ACT.Relu).then_inc(st.up(idx_relu), 1)

        index_relu(0)
        b, nth = wide_.next("dk")
        act.wait_ge(wide_.ready.sem, st.at(wide_.ready, nth))
        for f in range(2):
            src = b[64 * f:64 * f + 64, :].rearrange("p (u t) -> p u t", t=S)
            for r in range(2):
                act.activation(dkT[64 * r:64 * r + 64].rearrange("p (u f) t -> p f u t", f=2)[:, f], src, ACT.Copy) \
                    .then_inc(st.up(wide_.saved if f == r == 1 else act_step), 1)
        save("dv", flat(dv))
        index_relu(1)
        for n in range(4):
            save(f"dq{n}", flat(dqT[:, 2 * n:2 * n + 2, :]), scale=DH ** -0.5)

        def dsa_exp(b):
            nh = DSA_BATCHES[b][2]
            act.wait_ge(dmax_ready.sem, st.at(dmax_ready, b + 1))
            e = rows[:, :].rearrange("p (i n) -> p i n", i=nh)
            for n in range(nh):
                act.activation(e[:, n, :], e[:, n, :], ACT.Exp, bias=mx[:, n:n + 1],
                                     accum_out=sums[:, n:n + 1]) \
                    .then_inc(st.up(dexp_ready if n == nh - 1 else act_step), 1)

        dsa_exp(0)
        dsa_o = [dob[:, 0, 0:512], dob[:, 0, 512:1024], dob[:, 1, 0:512], dob[:, 1, 512:1024]]
        save("do0", dsa_o[0])
        save("do1", dsa_o[1])
        dsa_exp(1)
        save("do2", dsa_o[2])
        dsa_exp(2)
        save("do3", dsa_o[3])
        act.wait_ge(dprobs_ready.sem, st.at(dprobs_ready, 3))
        act_split(st, act, TILES2, "B.ff1.0")
        act.wait_ge(aux_.saved.sem, st.at(aux_.saved, aux_.nth_save("B.out3")))
        ln_statistics()
        act_mlp(st, act, wide_, "B.", TILES2)
        act.wait_ge(ff2_saved.sem, st.at(ff2_saved, 8))
        ln_statistics()

    def dve_tail(dve, st):
        wide_, aux_ = wide.again(WIDE2), aux.again(AUX2)

        def tt(o, a, b, op):
            return dve.tensor_tensor(o, a, b, op)

        def tsc(o, a, s1, op0, s2=None, op1=None):
            return dve.tensor_scalar(o, a, s1, s2, op0, op1) if op1 else dve.tensor_scalar(o, a, s1, None, op0)

        def stt(o, a, s1, b, op0, op1):
            return dve.scalar_tensor_tensor(out=o, in0=a, scalar=s1, in1=b, op0=op0, op1=op1)

        def copy(o, a):
            return dve.tensor_copy(o, a)

        def save_turned(names):
            for n, name in enumerate(names):
                t, half = divmod(n, 2)
                b, nth = aux_.next(name)
                dve.wait_ge(aux_.ready.sem, st.at(aux_.ready, nth))
                copy(hT[:, 4 * half:4 * half + 4, t * P:(t + 1) * P], b.rearrange("p (k t) -> p k t", t=P)) \
                    .then_inc(st.up(aux_.saved), 1)

        def split_turned(names):
            for n, name in enumerate(names):
                t, half = divmod(n, 2)
                b, nth = aux_.next(name)
                dve.wait_ge(aux_.ready.sem, st.at(aux_.ready, nth))
                hi, lo = (v[:, 4 * half:4 * half + 4, t * P:(t + 1) * P] for v in (ht_hi, ht_lo))
                b4 = b.rearrange("p (k t) -> p k t", t=P)
                copy(hi, b4).then_inc(st.up(dve_step), 1)
                dve.wait_ge(st.last.sem, st.reached())
                tt(lo, b4, hi.bitcast(F32), ALU.subtract).then_inc(st.up(aux_.saved), 1)

        def add_projected(names):
            for n, name in enumerate(names):
                c, t = divmod(n, 2)
                b, nth = aux_.next(name)
                dve.wait_ge(aux_.ready.sem, st.at(aux_.ready, nth))
                xv = x[:, t, c * BANK:(c + 1) * BANK]
                stt(xv, xv, ALPHA, b, ALU.mult, ALU.add).then_inc(st.up(aux_.saved), 1)

        def add_mlp(first):
            for n in range(4):
                c, t = divmod(n, 2)
                dve.wait_ge(ff2_ready.sem, st.at(ff2_ready, first + n + 1))
                xv = x[:, t, c * BANK:(c + 1) * BANK]
                stt(xv, xv, ALPHA, scores[:, n * BANK:(n + 1) * BANK], ALU.mult, ALU.add).then_inc(st.up(ff2_saved), 1)

        def layer_norm(n):
            dve.wait_ge(ln_stats.sem, st.at(ln_stats, n))
            for t in range(TT):
                tsc(x[:, t, :], x[:, t, :], lmu[:, t:t + 1], ALU.add, lrr[:, t:t + 1], ALU.mult) \
                    .then_inc(st.up(dve_step), 1)
            dve.wait_ge(st.last.sem, st.reached())
            dve.wait_ge(ln_in.sem, st.at(ln_in, 32 * n))
            tt(x[:, :, :], x[:, :, :], bc(ln_g, 1, TT), ALU.mult).then_inc(st.up(dve_step), 1)
            dve.wait_ge(st.last.sem, st.reached())
            tt(x[:, :, :], x[:, :, :], bc(ln_b, 1, TT), ALU.add).then_inc(st.up(ln_done), 1)

        save_turned([f"A.x{n}" for n in range(4)])
        dve.memset(part(4096, 1024), 0.0).then_inc(st.up(dve_step), 1)
        dve.memset(part(6144, 1024), 0.0).then_inc(st.up(dve_step), 1)
        dve.wait_ge(st.last.sem, st.reached())
        for ri in range(2):
            b, nth = aux_.next(f"ct{ri}")
            dve.wait_ge(aux_.ready.sem, st.at(aux_.ready, nth))
            for u in range(2):
                r = slice(64 * u, 64 * u + 64)
                o = CT[r, ri].rearrange("p i (j u c) -> p (i j) u c", u=2, c=SSM_C)[:, :, u, :]
                v = b[r, :].rearrange("p (j u c) -> p j u c", u=2, c=SSM_C)[:, :, u, :]
                tsc(o, v, -1.0 if ri else 1.0, ALU.mult).then_inc(st.up(aux_.saved if u else dve_step), 1)
        R = [prow[:, n, :] for n in range(18)]
        dve.wait_ge(dt_ready.sem, st.at(dt_ready, 1))
        for o, a in ((P_Y, P_LR), (P_TH, P_LI)):
            tt(R[o].rearrange("p (u n) -> p u n", u=2), R[a].rearrange("p (u n) -> p u n", u=2), bc(dt, 2, SSM_N), ALU.mult) \
                .then_inc(st.up(dve_step), 1)
        dve.wait_ge(st.last.sem, st.reached())
        tsc(R[P_Y], R[P_Y], -80.0, ALU.max, 80.0, ALU.min).then_inc(st.up(dve_step), 1)
        dve.wait_ge(st.last.sem, st.reached())
        tsc(R[P_W], R[P_Y], 1.0 / 256, ALU.mult).then_inc(st.up(dve_step), 1)
        dve.wait_ge(st.last.sem, st.reached())
        tsc(R[P_E], R[P_W], 1.0 / 7, ALU.mult, 1.0, ALU.add).then_inc(st.up(dve_step), 1)
        for n in range(6, 1, -1):
            dve.wait_ge(st.last.sem, st.reached())
            tt(R[P_E], R[P_E], R[P_W], ALU.mult).then_inc(st.up(dve_step), 1)
            dve.wait_ge(st.last.sem, st.reached())
            tsc(R[P_E], R[P_E], 1.0 / n, ALU.mult, 1.0, ALU.add).then_inc(st.up(dve_step), 1)
        dve.wait_ge(st.last.sem, st.reached())
        tt(R[P_E], R[P_E], R[P_W], ALU.mult).then_inc(st.up(dve_step), 1)
        for _ in range(8):
            dve.wait_ge(st.last.sem, st.reached())
            stt(R[P_E], R[P_E], 2.0, R[P_E], ALU.add, ALU.mult).then_inc(st.up(dve_step), 1)
        tsc(R[P_KQ], R[P_TH], 1.0 / TWO_PI, ALU.mult, ROUND, ALU.add).then_inc(st.up(dve_step), 1)
        dve.wait_ge(st.last.sem, st.reached())
        tsc(R[P_KQ], R[P_KQ], ROUND, ALU.subtract).then_inc(st.up(dve_step), 1)
        dve.wait_ge(st.last.sem, st.reached())
        stt(R[P_RED], R[P_KQ], -TURN[0], R[P_TH], ALU.mult, ALU.add).then_inc(st.up(dve_step), 1)
        for c in TURN[1:]:
            dve.wait_ge(st.last.sem, st.reached())
            stt(R[P_RED], R[P_KQ], -c, R[P_RED], ALU.mult, ALU.add).then_inc(st.up(dve_step), 1)
        dve.wait_ge(st.last.sem, st.reached())
        tsc(R[P_RED], R[P_RED], 0.5, ALU.mult).then_inc(st.up(dve_step), 1)
        dve.wait_ge(st.last.sem, st.reached())
        stt(R[P_HA], R[P_RED], -1.0, R[P_RED], ALU.mult, ALU.max).then_inc(st.up(sin_arg), 1)
        tsc(R[P_MAG], R[P_E], 1.0, ALU.add).then_inc(st.up(dve_step), 1)
        tt(R[P_DEN], R[P_LR], R[P_LR], ALU.mult).then_inc(st.up(dve_step), 1)
        tt(R[P_T1], R[P_LI], R[P_LI], ALU.mult).then_inc(st.up(dve_step), 1)
        dve.wait_ge(st.last.sem, st.reached())
        tt(R[P_DEN], R[P_DEN], R[P_T1], ALU.add).then_inc(st.up(dve_step), 1)
        dve.wait_ge(st.last.sem, st.reached())
        dve.reciprocal(R[P_DEN], R[P_DEN]).then_inc(st.up(dve_step), 1)
        dve.wait_ge(sin_ready.sem, st.at(sin_ready, 1))
        stt(R[P_SIN], R[P_SN], 2.0, R[P_CS], ALU.mult, ALU.mult).then_inc(st.up(dve_step), 1)
        stt(R[P_CM1], R[P_SN], -2.0, R[P_SN], ALU.mult, ALU.mult).then_inc(st.up(dve_step), 1)
        dve.wait_ge(st.last.sem, st.reached())
        tsc(R[P_COS], R[P_CM1], 1.0, ALU.add).then_inc(st.up(dve_step), 1)
        tt(R[P_ABI], R[P_MAG], R[P_SIN], ALU.mult).then_inc(st.up(dve_step), 1)
        dve.wait_ge(st.last.sem, st.reached())
        tt(R[P_NR], R[P_E], R[P_COS], ALU.mult).then_inc(st.up(dve_step), 1)
        dve.wait_ge(st.last.sem, st.reached())
        tt(R[P_NR], R[P_NR], R[P_CM1], ALU.add).then_inc(st.up(dve_step), 1)
        dve.wait_ge(st.last.sem, st.reached())
        for o, a, c, op in ((P_CR, P_LR, P_LI, ALU.add), (P_CI, P_LI, P_LR, ALU.subtract)):
            dve.wait_ge(st.last.sem, st.reached())
            tt(R[P_T1], R[P_NR], R[a], ALU.mult).then_inc(st.up(dve_step), 1)
            tt(R[P_T2], R[P_ABI], R[c], ALU.mult).then_inc(st.up(dve_step), 1)
            dve.wait_ge(st.last.sem, st.reached())
            if o == P_CR:
                tt(R[P_T1], R[P_T1], R[P_T2], op).then_inc(st.up(dve_step), 1)
            else:
                tt(R[P_T1], R[P_T2], R[P_T1], op).then_inc(st.up(dve_step), 1)
            dve.wait_ge(st.last.sem, st.reached())
            tt(R[o], R[P_T1], R[P_DEN], ALU.mult).then_inc(st.up(par_ready if o == P_CI else dve_step), 1)
        b, nth = aux_.next("par")
        dve.wait_ge(aux_.ready.sem, st.at(aux_.ready, nth))
        copy(tiny[:, 240:320], b[:, 0:80]).then_inc(st.up(dve_step), 1)
        copy(d_col, b[:, 80:84]).then_inc(st.up(dve_step), 1)
        tsc(neg_b, b[:, 84:88], -1.0, ALU.mult).then_inc(st.up(aux_.saved), 1)
        dve.wait_ge(st.last.sem, st.reached())
        cr, ci, mag, cost, sint = (pcol[:, n, :] for n in range(5))
        dve.wait_ge(b_in.sem, st.at(b_in, 32))
        v1, v2 = (v[:, 0:256].rearrange("p (j c) -> p j c", c=SSM_C) for v in (t1, t2))
        for ri, (a, c, op) in enumerate(((cr, ci, ALU.subtract), (ci, cr, ALU.add))):
            dve.wait_ge(st.last.sem, st.reached())
            tt(v1, bin_[:, 0], bc(a, 2, SSM_C), ALU.mult).then_inc(st.up(dve_step), 1)
            tt(v2, bin_[:, 1], bc(c, 2, SSM_C), ALU.mult).then_inc(st.up(dve_step), 1)
            dve.wait_ge(st.last.sem, st.reached())
            for u in range(2):
                r = slice(64 * u, 64 * u + 64)
                tt(BD[r, ri, :, u, :], v1[r], v2[r], op).then_inc(st.up(bd_ready if ri == u == 1 else dve_step), 1)
        dve.memset(ctab[:, :, 0:1], 1.0).then_inc(st.up(dve_step), 1)
        dve.memset(stab[:, :, 0:1], 0.0).then_inc(st.up(dve_step), 1)
        copy(cm, cost).then_inc(st.up(dve_step), 1)
        copy(sm, sint).then_inc(st.up(dve_step), 1)
        m = 1
        while m < S:
            a = scr[:, 0:SJ * m].rearrange("p (j t) -> p j t", t=m)
            c = part(8704, SJ * m, "p (j t) -> p j t", t=m)
            for o, p, q, op in ((ctab, cm, sm, ALU.subtract), (stab, sm, cm, ALU.add)):
                dve.wait_ge(st.last.sem, st.reached())
                tt(a, ctab[:, :, 0:m], bc(p, 2, m), ALU.mult).then_inc(st.up(dve_step), 1)
                tt(c, stab[:, :, 0:m], bc(q, 2, m), ALU.mult).then_inc(st.up(dve_step), 1)
                dve.wait_ge(st.last.sem, st.reached())
                tt(o[:, :, m:2 * m], a, c, op).then_inc(st.up(dve_step), 1)
            tt(cn, cm, cm, ALU.mult).then_inc(st.up(dve_step), 1)
            tt(sn2, sm, sm, ALU.mult).then_inc(st.up(dve_step), 1)
            dve.wait_ge(st.last.sem, st.reached())
            stt(sm, sm, 2.0, cm, ALU.mult, ALU.mult).then_inc(st.up(dve_step), 1)
            dve.wait_ge(st.last.sem, st.reached())
            tt(cm, cn, sn2, ALU.subtract).then_inc(st.up(dve_step), 1)
            m *= 2
        for ri in range(2):
            b, nth = aux_.next(f"bt{ri}")
            dve.wait_ge(aux_.ready.sem, st.at(aux_.ready, nth))
            copy(flat(BT[:, ri]), b).then_inc(st.up(aux_.saved), 1)

        def softplus(batch):
            dve.wait_ge(ln1p_ready.sem, st.at(ln1p_ready, batch + 1))
            v = scores.rearrange("p (h n) -> p h n", n=BANK)[:, :, 0:384]
            stt(sp_, v, 0.0, sp_, ALU.max, ALU.add).then_inc(st.up(dve_step), 1)
            dve.wait_ge(st.last.sem, st.reached())
            d = sp_.rearrange("p h (b t) -> p h b t", t=P)
            for n in (0, 2):
                tt(d[:, :, n, :], d[:, :, n, :], bc(K["strict_keep"], 1, 4), ALU.mult) \
                    .then_inc(st.up(sp_ready if n else dve_step), 1)

        def log_weights(batch):
            for hl in range(4):
                b, nth = aux_.next(f"cs{4 * batch + hl}")
                dve.wait_ge(aux_.ready.sem, st.at(aux_.ready, nth))
                tt(zs[:, hl, :], zs[:, hl, :], b[:, 0:384], ALU.subtract).then_inc(st.up(aux_.saved), 1)
            dve.wait_ge(st.last.sem, st.reached())
            d = zs.rearrange("p h (b t) -> p h b t", t=P)
            for n in (0, 2):
                tt(d[:, :, n, :], d[:, :, n, :], bc(K["strict_add"], 1, 4), ALU.add) \
                    .then_inc(st.up(sw_arg if n else dve_step), 1)

        def scan(j):
            b, nth = aux_.next(f"bu{j}")
            dve.wait_ge(aux_.ready.sem, st.at(aux_.ready, nth))
            b2 = b.rearrange("p (r t) -> p r t", r=2)
            if j >= 2:
                dve.wait_ge(state_ready.sem, st.at(state_ready, j - 1))
            v1, v2 = (v.rearrange("p (r t) -> p r t", r=2) for v in (t1, t2))
            dve.wait_ge(st.last.sem, st.reached())
            tt(v1, b2, bc(ctab[:, j, :], 1, 2), ALU.mult).then_inc(st.up(dve_step), 1)
            tt(v2, b2, bc(stab[:, j, :], 1, 2), ALU.mult).then_inc(st.up(aux_.saved), 1)
            dve.wait_ge(st.last.sem, st.reached())
            tt(v1[:, 0], v1[:, 0], v2[:, 1], ALU.add).then_inc(st.up(dve_step), 1)
            tt(v1[:, 1], v1[:, 1], v2[:, 0], ALU.subtract).then_inc(st.up(dve_step), 1)
            dve.wait_ge(st.last.sem, st.reached())
            for ri in range(2):
                dve.tensor_tensor_scan(wst[j % 2][:, ri * S:(ri + 1) * S], mag[:, j:j + 1].broadcast_to([P, S]),
                                             v1[:, ri], 0.0, ALU.mult, ALU.add) \
                    .then_inc(st.up(scan_ready if ri else dve_step), 1)

        softplus(0)
        for j in range(SJ):
            scan(j)
            if j == 1:
                log_weights(0)
                softplus(1)
            if j == 8:
                log_weights(1)
        dve.wait_ge(wide_.saved.sem, st.at(wide_.saved, wide_.nth_save("y3")))
        for k in range(4):
            stt(yT[:, k, :], uT[:, k, :], d_col[:, k:k + 1], yT[:, k, :], ALU.mult, ALU.add).then_inc(st.up(dve_step), 1)
        dve.wait_ge(st.last.sem, st.reached())
        y1 = yT.rearrange("p b t -> p (b t)")
        tt(ge, y1, y1, ALU.mult).then_inc(st.up(dve_step), 1)
        dve.wait_ge(st.last.sem, st.reached())
        tsc(ge, ge, 0.044715, ALU.mult, 1.0, ALU.add).then_inc(st.up(dve_step), 1)
        dve.wait_ge(st.last.sem, st.reached())
        tt(ge, ge, y1, ALU.mult).then_inc(st.up(dve_step), 1)
        dve.wait_ge(st.last.sem, st.reached())
        tsc(ge, ge, -50.0, ALU.max).then_inc(st.up(ygelu_arg), 1)
        dve.wait_ge(ygelu_exp.sem, st.at(ygelu_exp, 1))
        tsc(ge, ge, 1.0, ALU.add).then_inc(st.up(dve_step), 1)
        dve.wait_ge(st.last.sem, st.reached())
        dve.reciprocal(ge, ge).then_inc(st.up(dve_step), 1)
        dve.wait_ge(st.last.sem, st.reached())
        tt(y1, y1, ge, ALU.mult).then_inc(st.up(ygelu_ready), 1)
        for t in range(TT):
            b, nth = aux_.next(f"ao{t}")
            dve.wait_ge(aux_.ready.sem, st.at(aux_.ready, nth))
            copy(hT[:, 0:4, t * P:(t + 1) * P], b.rearrange("p (k t) -> p k t", t=P)).then_inc(st.up(aux_.saved), 1)
        dve.wait_ge(wide_.saved.sem, st.at(wide_.saved, wide_.nth_save("glu1")))
        tsc(ge, ge, 1.0, ALU.add).then_inc(st.up(dve_step), 1)
        dve.wait_ge(st.last.sem, st.reached())
        dve.reciprocal(ge, ge).then_inc(st.up(dve_step), 1)
        dve.wait_ge(st.last.sem, st.reached())
        tt(y1, y1, ge, ALU.mult).then_inc(st.up(y_ready), 1)
        dve_split(st, dve, TILES2, "A.ff1.0")
        add_projected([f"A.out{n}" for n in range(4)])
        layer_norm(1)
        split_turned([f"A.n{n}" for n in range(4)])
        dve_mlp(st, dve, "A.", TILES2)
        add_mlp(0)
        dve.memset(part(4096, 1024), 0.0).then_inc(st.up(kiz_zero), 1)
        layer_norm(2)
        save_turned([f"B.x{n}" for n in range(4)])

        def top_keys(t):
            keys = (t + 1) * P
            v = slice(0, P) if t == 0 else slice(P, 384)
            s, r, a = isc[:, v], irep[:, v], iadd[:, v]
            dve.wait_ge(idx_relu.sem, st.at(idx_relu, t + 1))
            rl = relu_[:, 0:IDX_HEADS * keys].rearrange("p (h n) -> p h n", n=keys)
            tsc(s, rl[:, 0, :], wi[:, 8 * t:8 * t + 1], ALU.mult).then_inc(st.up(dve_step), 1)
            for h in range(1, IDX_HEADS):
                dve.wait_ge(st.last.sem, st.reached())
                stt(s, rl[:, h, :], wi[:, 8 * t + h:8 * t + h + 1], s, ALU.mult, ALU.add) \
                    .then_inc(st.up(idx_summed if h == IDX_HEADS - 1 else dve_step), 1)
            dve.wait_ge(st.last.sem, st.reached())
            d = s[:, t * P:(t + 1) * P]
            tt(d, d, K["causal"], ALU.add).then_inc(st.up(dve_step), 1)
            for n in range(TOPK // 8):
                dve.wait_ge(st.last.sem, st.reached())
                dve.max(m8, r if n else s).then_inc(st.up(dve_step), 1)
                dve.wait_ge(st.last.sem, st.reached())
                dve.match_replace(r, m8, r if n else s, TAKEN).then_inc(st.up(dve_step), 1)
            dve.wait_ge(st.last.sem, st.reached())
            tsc(a, r, TAKEN, ALU.is_equal, -MASKED, ALU.mult).then_inc(st.up(dve_step), 1)
            dve.wait_ge(st.last.sem, st.reached())
            tsc(a, a, MASKED, ALU.add).then_inc(st.up(dve_step), 1)
            dve.wait_ge(st.last.sem, st.reached())
            d = a[:, t * P:(t + 1) * P]
            tt(d, d, K["causal"], ALU.add).then_inc(st.up(dve_step), 1)

        top_keys(0)
        top_keys(1)

        def logits(b):
            t, _, nh = DSA_BATCHES[b]
            view, keys = dsa_view(b)
            dve.wait_ge(dsc_ready.sem, st.at(dsc_ready, b + 1))
            if b:
                dve.wait_ge(aux_.saved.sem, st.at(aux_.saved, aux_.nth_save(f"pt{b - 1}.3")))
            e = rows[:, :].rearrange("p (i n) -> p i n", n=keys)
            hs = slots(b)
            for n, h in enumerate(hs):
                slope = float(np.float32(2.0 ** (-8.0 * (h + 1) / DSA_HEADS)))
                stt(e[:, n, :], K["rel"][:, S - keys:S], slope, view[:, n, :], ALU.mult, ALU.add) \
                    .then_inc(st.up(dsc_read if n == nh - 1 else dve_step), 1)
            dve.wait_ge(st.last.sem, st.reached())
            tt(e, e, bc(iadd[:, 0:P] if t == 0 else iadd[:, P:384], 1, nh), ALU.add).then_inc(st.up(dve_step), 1)
            dve.wait_ge(st.last.sem, st.reached())
            dve.tensor_reduce(mx[:, 0:nh], e, AX_X, ALU.max, negate=True).then_inc(st.up(dmax_ready), 1)

        def probabilities(b):
            _, _, nh = DSA_BATCHES[b]
            _, keys = dsa_view(b)
            dve.wait_ge(dexp_ready.sem, st.at(dexp_ready, b + 1))
            dve.reciprocal(wts[:, 0:nh], sums[:, 0:nh]).then_inc(st.up(dve_step), 1)
            dve.wait_ge(st.last.sem, st.reached())
            e = rows[:, :].rearrange("p (i n) -> p i n", n=keys)
            tt(e, e, bc(wts[:, 0:nh], 2, keys), ALU.mult).then_inc(st.up(dprobs_ready), 1)

        for b in range(3):
            logits(b)
            probabilities(b)
            if b:
                dve.wait_ge(wide_.saved.sem, st.at(wide_.saved, wide_.nth_save(f"do{b}")))
            for n in range(4):
                bk, nth = aux_.next(f"pt{b}.{n}")
                dve.wait_ge(aux_.ready.sem, st.at(aux_.ready, nth))
                copy(scr[:, n * BANK:(n + 1) * BANK], bk).then_inc(st.up(aux_.saved), 1)
        save_turned([f"do{n}" for n in range(4)])
        dve_split(st, dve, TILES2, "B.ff1.0")
        add_projected([f"B.out{n}" for n in range(4)])
        layer_norm(3)
        split_turned([f"B.n{n}" for n in range(4)])
        dve_mlp(st, dve, "B.", TILES2)
        add_mlp(4)
        layer_norm(4)

    def pool_tail(pool, st):
        for j in range(SJ):
            pool.wait_ge(scan_ready.sem, st.at(scan_ready, j + 1))
            w, o = (v[j % 2].rearrange("p (r t) -> p r t", r=2) for v in (wst, xst))
            v1, v2 = (v.rearrange("p (r t) -> p r t", r=2) for v in (pu1, pu2))
            if j >= 2:
                q, jl = divmod(j - 2, 4)
                if jl == 3:
                    pool.wait_ge(wide.again(WIDE2).saved.sem, st.at(wide.again(WIDE2).saved, wide.again(WIDE2).nth_save(f"y{q}")))
                else:
                    pool.wait_ge(state_used.sem, st.at(state_used, j - 2 - q + 1))
            if j == 0:
                pool.wait_ge(aux.again(AUX2).saved.sem, st.at(aux.again(AUX2).saved, aux.again(AUX2).nth_save("bt1")))
            if j:
                pool.wait_ge(st.last.sem, st.reached())
            pool.tensor_tensor(v1, w, bc(ctab[:, j, :], 1, 2), ALU.mult).then_inc(st.up(pool_step), 1)
            pool.tensor_tensor(v2, w, bc(stab[:, j, :], 1, 2), ALU.mult).then_inc(st.up(pool_step), 1)
            pool.wait_ge(st.last.sem, st.reached())
            pool.tensor_tensor(o[:, 0], v1[:, 0], v2[:, 1], ALU.subtract).then_inc(st.up(pool_step), 1)
            pool.tensor_tensor(o[:, 1], v1[:, 1], v2[:, 0], ALU.add).then_inc(st.up(state_ready), 1)

    @block.sync
    def _(sp):
        sp.dma_start(x[:, :, :], I["x"][0].rearrange("(t p) n -> p t n", p=P)).then_inc(x_in.sem, 16)
        sp.dma_start(const[:, :], I["const"]).then_inc(const_in.sem, 16)
        with sp.Fori(0, DEPTH) as i:
            where = Where(i)

            def src(name):
                return I[name][bass.ds(i, 1)].rearrange("o a b -> (o a) b")

            def vec(name):
                return I[name][bass.ds(i, 1)]

            sp.wait_ge(small_used.sem, i * small_used.per_layer + 1)
            small = [(vec_rows[8 * n:8 * n + 8, :], vec(v).rearrange("o (k p) -> (o k) p", p=P))
                     for n, v in enumerate(("norm_mix", "norm_mlp", "norm_ple"))]
            for n, v in ((C_Q, "nsa_q_norm"), (C_K, "nsa_k_norm")):
                for u in range(2):
                    small.append((vec_rows[n:n + 1, u * DH:(u + 1) * DH], vec(v)))
            for n, v in enumerate(("cmp_pos_k", "cmp_pos_v")):
                small.append((vec_rows[C_POS + 16 * n:C_POS + 16 * n + 16, :],
                              src(v).rearrange("(j l) d -> j (l d)", l=2)))
            for n, v in enumerate(("cmp_w2_k", "cmp_w2_v")):
                small.append((w2[:, n], src(v).rearrange("(h p) d -> p h d", p=P)))
            for dst, s in small[:9]:
                sp.dma_start(dst, s).then_inc(small_in.sem, 16)
            for n, name in enumerate(TILES):
                if n == RING:
                    for dst, s in small[9:]:
                        sp.dma_start(dst, s).then_inc(late_in.sem, 16)
                    sp.dma_start(p_sb[:, :, :], I["p"][bass.ds(i, 1)].rearrange("o b s n -> (o b s) n")
                                 .rearrange("(t p) n -> p t n", p=P)).then_inc(late_in.sem, 16)
                sp.wait_ge(tile_used.sem, where.value(tile_used, n + 1))
                kind, _, num = name.partition(".")
                if name.startswith("in"):
                    c = int(name[2:])
                    m = min(BANK, D_IN - c * BANK)
                    s, k = src("w_in")[:, c * BANK:c * BANK + m], KT
                elif name in ("w1k", "w1v"):
                    s, k, m = src("cmp_w1_" + name[2]), 16, CMP_HID
                elif name in ("up_nsa", "up_ret"):
                    s, k, m = src("w_" + name), 4, D
                elif kind == "ff1":
                    s, k, m = src("w_ff1")[:, int(num) * BANK:(int(num) + 1) * BANK], KT, BANK
                elif kind == "ff2":
                    s, k, m = src("w_ff2")[int(num) * BANK:(int(num) + 1) * BANK, :], 4, D
                elif name == "ple":
                    s, k, m = src("w_ple"), 2, D
                else:
                    c = int(name[-1])
                    s = src("w_out" if name.startswith("out") else "w_ple_gate")[:, c * BANK:(c + 1) * BANK]
                    k, m = KT, BANK
                sp.dma_start(w_tile(n, (k, m)), s.rearrange("(k p) n -> p k n", p=P)) \
                    .then_inc(tile_in[n % RING].sem, 16)
        sp_tail(sp)

    @block.tensor
    def _(pe):
        pe.sem_inc(tile_used.sem, RING)
        pe.wait_ge(const_in.sem, 16)
        with pe.Fori(0, DEPTH) as i:
            st = Steps(Where(i))
            pe_layer(pe, st)
            st.check()
        pe_tail(pe, Steps(Where()))

    @block.scalar
    def _(act):
        act.sem_inc(wide.saved.sem, 2)
        act.wait_ge(eps_set.sem, 3)
        act.wait_ge(x_in.sem, 16)
        with act.Fori(0, DEPTH) as i:
            st = Steps(Where(i))
            act_layer(act, st)
            st.check()
        act_tail(act, Steps(Where()))

    @block.vector
    def _(dve):
        dve.sem_inc(aux.saved.sem, 2)
        dve.memset(part(10784, 64), 0.0).then_inc(zero_set.sem, 1)
        dve.wait_ge(zero_set.sem, 1)
        dve.memset(vec_rows, 0.0).then_inc(small_used.sem, 1)
        for n, v in enumerate((EPS, LN_EPS, np.pi / 2)):
            dve.memset(eps_tile[:, n:n + 1], float(v)).then_inc(eps_set.sem, 1)
        dve.wait_ge(const_in.sem, 16)
        dve.wait_ge(x_in.sem, 16)
        with dve.Fori(0, DEPTH) as i:
            st = Steps(Where(i))
            dve_layer(dve, st)
            st.check()
        dve_tail(dve, Steps(Where()))

    @block.gpsimd
    def _(pool):
        pool.wait_ge(const_in.sem, 16)
        with pool.Fori(0, DEPTH) as i:
            st = Steps(Where(i))
            pool_layer(pool, st)
            st.check()
        pool_tail(pool, Steps(Where()))


NAMES = ["x", "p", "norm_mix", "w_in", "nsa_q_norm", "nsa_k_norm", "cmp_pos_k", "cmp_pos_v", "cmp_w1_k", "cmp_w2_k",
         "cmp_w1_v", "cmp_w2_v", "w_up_nsa", "w_up_ret", "w_out", "norm_mlp", "w_ff1", "w_ff2", "norm_ple", "w_ple",
         "w_ple_gate", "sb_ssm_w_in_2", "ssm_log_dt_2", "ssm_lam_re_2", "ssm_lam_im_2", "ssm_b_re_2", "ssm_b_im_2",
         "ssm_c_re_2", "ssm_c_im_2", "ssm_d_2", "ssm_w_glu_2", "ssm_b_glu_2", "sb_ssm_w_out_2", "dsa_w_in_2",
         "dsa_w_out_2", "ln_mix_g_2", "ln_mix_b_2", "ln_ffn_g_2", "ln_ffn_b_2", "mlp_w1_2", "mlp_w2_2"]


def kernel(**inputs):
    import concourse.bacc as bacc
    from concourse.bass_utils import run_bass_kernel_spmd

    nc = bacc.Bacc("TRN2", target_bir_lowering=False, num_devices=1)
    arrays = {f"in_{name}": np.ascontiguousarray(inputs[name]) for name in NAMES}
    arrays["in_const"] = constants()
    I = {name[3:]: nc.dram_tensor(name, a.shape, mybir.dt.from_np(a.dtype), kind="ExternalInput").ap()
         for name, a in arrays.items()}
    out = nc.dram_tensor("out", (1, S, D), F32, kind="ExternalOutput").ap()
    build(nc, I, out)
    return run_bass_kernel_spmd(nc, [arrays], core_ids=[0]).results[0]["out"]
```

```python
from contextlib import ExitStack

import numpy as np

import concourse.bass as bass
from concourse import mybir

F32 = mybir.dt.float32
F32R = mybir.dt.float32r
ALU = mybir.AluOpType
ACT = mybir.ActivationFunctionType
AX_X = mybir.AxisListType.X

P = 128
S = 256
TT = S // P
D = 1024
KT = D // P
DEPTH = 2
DFF = 4 * D
FB = DFF // P
BANK = 512
SLOT = 4096
RING = 3
EPS = 1e-6
MASKED = -1e30

HEADS, DH, GROUPS = 8, 64, 2
NCMP, CMP_STRIDE, CMP_LEN, CMP_HID = 16, 16, 32, 256
Z_Q, Z_KC, Z_VC, Z_KS, Z_VS, Z_KW, Z_VW, Z_GATE = 0, 512, 640, 768, 896, 1024, 1152, 1280
Z_RQ, Z_RK, Z_RV, Z_RG, Z_MA, Z_MB, D_IN = 1304, 1816, 2328, 2840, 3352, 4376, 5400
N_IN = -(-D_IN // BANK)
RH, RD = 4, 128
PLE = 256

ALPHA = (2 * DEPTH) ** 0.25
LN_EPS = 1e-5
SB_W, SB_HEADS = 512, 8
SSM_G, SSM_C, SSM_N = 32, 16, 64
SJ = SSM_G * SSM_N // P
DSA_HEADS, DSA_KV = 16, 4
IDX_HEADS, IDX_DIM, TOPK = 8, 32, min(256, S // 4)
I_Q, I_K, I_V, I_QI, I_KI, I_WI, DSA_IN = 0, 1024, 1280, 1536, 1792, 1824, 1832
TAKEN = -3e38
TWO_PI = 2 * np.pi
TURN = [6.28125]
TURN.append(np.floor((TWO_PI - TURN[0]) * 2.0 ** 21) / 2.0 ** 21)
TURN.append(TWO_PI - TURN[0] - TURN[1])
ROUND = 1.5 * 2.0 ** 23

CONST_PARTS = [("ident", P), ("causal", P), ("cmp_add", 128), ("cmp_keep", 128), ("decay", RH * 384),
               ("cos", TT * 64), ("sin", TT * 64), ("own_rows", 4), ("suffix", P), ("ones", P),
               ("strict_keep", P), ("strict_add", P), ("rel", S)]
CONST_AT = {}
_n = 0
for _name, _w in CONST_PARTS:
    CONST_AT[_name] = (_n, _n + _w)
    _n += _w
CONST_W = _n


def constants():
    f = np.float32
    c = np.zeros((P, CONST_W), f)

    def put(name, a):
        lo, hi = CONST_AT[name]
        c[:, lo:hi] = np.asarray(a, f).reshape(P, hi - lo)

    i = np.arange(P)
    put("ident", np.eye(P))
    put("causal", np.where(i[None, :] <= i[:, None], 0.0, MASKED))
    t = np.arange(S).reshape(TT, P).T[:, :, None, None]
    own = np.arange(GROUPS)[:, None] == np.arange(GROUPS * NCMP)[None, :] // NCMP
    ends = (np.arange(GROUPS * NCMP) % NCMP) * CMP_STRIDE + CMP_LEN - 1
    keep = (ends[None, None, None, :] <= t) & own[None, None]
    put("cmp_add", np.where(keep, 0.0, MASKED))
    put("cmp_keep", keep)
    gamma = (f(1.0) - f(2.0) ** (f(-5.0) - np.arange(RH, dtype=f))).astype(f)
    lg = np.log(gamma).astype(np.float64)
    diff = (i[None, :] - i[:, None]).astype(np.float64)
    near = np.where(diff[:, None] >= 0, np.exp(lg[None, :, None] * np.maximum(diff[:, None], 0)), 0.0)
    far = np.exp(lg[None, :, None] * (diff[:, None] + P))
    put("decay", np.concatenate([near, far, near], -1) * RD ** -0.5)
    inv = (f(10000.0) ** (-np.arange(64, dtype=f) / f(64))).astype(f)
    ang = (np.arange(S, dtype=f)[:, None] * inv[None]).astype(f).reshape(TT, P, 64).transpose(1, 0, 2)
    put("cos", np.cos(ang.astype(np.float64)))
    put("sin", np.sin(ang.astype(np.float64)))
    put("own_rows", i[:, None] // 32 == np.arange(4)[None])
    put("suffix", i[:, None] >= i[None, :])
    put("ones", np.ones((P, P)))
    put("strict_keep", i[:, None] < i[None, :])
    put("strict_add", np.where(i[:, None] < i[None, :], 0.0, MASKED))
    put("rel", np.arange(S)[None, :] - P - i[:, None])
    return c


WIDE = [f"c{c}t{t}" for c in range(5) for t in range(TT)] + ["hk", "hv"]
WIDE += [f"c{c}t{t}" for c in (5, 6, 7) for t in range(TT)] + ["o0"]
WIDE += [f"c8t{t}" for t in range(TT)] + ["o1"] + [f"c9t{t}" for t in range(TT)] + ["yr0", "yr1"]
WIDE += [f"c10t{t}" for t in range(TT)] + [f"f{n}" for n in range(FB // 2)] + [f"g{n}" for n in range(4)]
AUX = ["cols"] + [f"n{n}" for n in range(4)] + ["q0", "q1", "k", "zc", "hidT", "w2", "kcT", "cmp0", "cmp1"]
AUX += [f"pt0.{n}" for n in range(4)] + ["pcT"] + [f"pt1.{n}" for n in range(4)] + [f"pt2.{n}" for n in range(4)]
AUX += [f"rot{n}" for n in range(4)] + ["pT", "ya0", "ya1", "yr0", "yr1"]
AUX += [f"upa{n}" for n in range(4)] + [f"upb{n}" for n in range(4)] + [f"m{n}" for n in range(4)]
AUX += [f"out{n}" for n in range(4)] + [f"nm{n}" for n in range(4)] + [f"np{n}" for n in range(4)]
AUX += [f"ple{n}" for n in range(4)]
assert len(WIDE) % 2 == 0 and len(AUX) % 2 == 0, (len(WIDE), len(AUX))

TILES = [f"in{c}" for c in range(5)] + ["w1k", "w1v"] + [f"in{c}" for c in range(5, N_IN)]
TILES += ["up_nsa", "up_ret", "out0", "out1"] + [f"ff1.{n}" for n in range(8)] + [f"ff2.{n}" for n in range(8)]
TILES += ["gate0", "gate1", "ple"]
assert len(TILES) % RING == 0
MLP_TILES = 16


def _mlp_names(pre, n, kind):
    return [f"{pre}{kind}{i}" for i in range(n)]


WIDE2 = ["u0", "u1", "sq0", "sq1", "sk0", "sk1", "sv0", "sv1", "y0", "y1", "sA0", "sA1", "y2", "sB0", "sB1", "y3"]
WIDE2 += ["glu0", "glu1"] + _mlp_names("A.", FB // 2, "f")
WIDE2 += ["qi", "kiw", "dk", "dv", "dq0", "dq1", "dq2", "dq3", "do0", "do1", "do2", "do3"] + _mlp_names("B.", FB // 2, "f")
AUX2 = _mlp_names("A.", 4, "x") + ["ct0", "ct1", "par", "bt0", "bt1"] + [f"bu{j}" for j in range(4)]
AUX2 += [f"cs{h}" for h in range(4)]
AUX2 += [f"bu{j}" for j in range(4, 9)] + [f"cs{h}" for h in range(4, 8)] + [f"bu{j}" for j in range(9, 16)]
AUX2 += ["ao0", "ao1"] + _mlp_names("A.", 4, "out") + _mlp_names("A.", 4, "n")
AUX2 += _mlp_names("B.", 4, "x") + [f"pt{b}.{n}" for b in range(3) for n in range(4)] + [f"do{n}" for n in range(4)]
AUX2 += _mlp_names("B.", 4, "out") + _mlp_names("B.", 4, "n")
TILES2 = ["sb3", "sb0", "sb1", "sb2", "glu", "sbo0", "sbo1"]
TILES2 += [f"A.ff1.{n}" for n in range(8)] + [f"A.ff2.{n}" for n in range(8)]
TILES2 += ["ds3", "ds2", "ds0", "ds1", "dso0", "dso1"]
TILES2 += [f"B.ff1.{n}" for n in range(8)] + [f"B.ff2.{n}" for n in range(8)]


def _mlp_tiles(pre):
    return [f"{pre}ff1.{n}" for n in range(8)] + [f"{pre}ff2.{n}" for n in range(8)]


SPLITS = [f"in{c}" for c in range(N_IN)] + ["out0", "out1"] + _mlp_tiles("") + ["gate0", "gate1"]
SPLITS2 = ["sbo0", "sbo1"] + _mlp_tiles("A.") + ["dso0", "dso1"] + _mlp_tiles("B.")


def _places(splits):
    pairs = (("work", "big"), ("tmp", "rows"))
    late = {"in4": ("hT", "work"), "in5": ("hT", "work"), "in6": ("zb", "hT"), "in7": ("work", "zb"),
            "in8": ("hT", "work"), "in9": ("hT", "work"), "in10": ("hT", "work")}
    turn = [name for name in splits if name not in late]
    return {name: late[name] if name in late else pairs[turn.index(name) % 2] for name in splits}


PLACES, PLACES2 = _places(SPLITS), _places(SPLITS2)


def split_halves(name):
    return KT * (D_IN - (N_IN - 1) * BANK) // 2 if name == f"in{N_IN - 1}" else SLOT // 2


POOL_SPLITS = [f"in{c}" for c in range(N_IN)] + ["out0", "out1", "sbo0", "sbo1", "dso0", "dso1"]


class Signal:

    def __init__(self, sem, per_layer, start=0):
        self.sem, self.per_layer, self.start = sem, per_layer, start


class Where:

    def __init__(self, layer=None):
        self.layer = layer

    def value(self, signal, n):
        if self.layer is None:
            return DEPTH * signal.per_layer + n
        return self.layer * signal.per_layer + n


class Steps:

    def __init__(self, where):
        self.where, self.count, self.last = where, {}, None

    def up(self, signal, by=1):
        self.count[signal] = self.count.get(signal, 0) + by
        self.last = signal
        return signal.sem

    def at(self, signal, n):
        return self.where.value(signal, n)

    def reached(self):
        return self.at(self.last, self.last.start + self.count[self.last])

    def check(self):
        bad = {s.sem.name: (n, s.per_layer) for s, n in self.count.items() if n != s.per_layer}
        assert not bad, bad


class Line:

    def __init__(self, banks, names, ready, saved):
        self.banks, self.names, self.ready, self.saved, self.at = banks, names, ready, saved, 0

    def next(self, name):
        assert self.names[self.at] == name, (self.names[self.at], name)
        self.at += 1
        return self.banks[(self.at - 1) % 2], self.at

    def nth_save(self, name):
        return self.names.index(name) + 3

    def again(self, names):
        return Line(self.banks, names, self.ready, self.saved)


class Kit:

    def __init__(self, mm, tp, next_tile, tile_done, turn_rows, rows_by_tile, units_by_tile, rows_by_split, mlp, finish):
        self.mm, self.tp, self.next_tile, self.tile_done = mm, tp, next_tile, tile_done
        self.turn_rows, self.rows_by_tile, self.units_by_tile = turn_rows, rows_by_tile, units_by_tile
        self.rows_by_split, self.mlp, self.finish = rows_by_split, mlp, finish


def bc(ap, axis, n):
    ap = ap.unsqueeze(axis)
    shape = list(ap.shape)
    shape[axis] = n
    return ap.broadcast_to(shape)


def build(nc, I, out):
    with ExitStack() as ctx:
        program(nc, ctx, I, out)


def program(nc, ctx, I, out):
    address = {}

    def sb(name, shape):
        address[name] = -(-nc.sbuf_base // 32) * 32
        return ctx.enter_context(nc.sbuf_tensor(name, shape, F32))

    def digits(name, buffer, lo, width):
        return nc.alloc_sbuf_tensor_at(name, [P, width], F32R, offset=address[buffer] + 4 * lo)

    def sig(name, per_layer=0, start=0):
        return Signal(ctx.enter_context(nc.semaphore(name)), per_layer, start)

    ring = [sb(f"ring{i}", [P, SLOT]) for i in range(RING)]
    x = sb("x", [P, TT, D])
    hT = sb("hT", [P, KT, S])
    big = sb("big", [P, TT * D_IN])
    scr = sb("scr", [P, 2304])
    rows = sb("rows", [P, 2048])
    tmp = sb("tmp", [P, 2048])
    const = sb("const", [P, CONST_W])
    work = sb("work", [P, 10848])
    tiny = sb("tiny", [P, 512])
    p_sb = sb("p_sb", [P, TT, PLE])
    pT = sb("pT", [P, 2, S])
    psum = ctx.enter_context(nc.psum_tensor("psum", [P, 8 * BANK], F32))
    bank = [psum[:, b * BANK:(b + 1) * BANK] for b in range(8)]
    scores = psum[:, 4 * BANK:8 * BANK]

    K = {name: const[:, lo:hi] for name, (lo, hi) in CONST_AT.items()}
    ident = K["ident"]
    z = big[:, :].rearrange("p (t n) -> p t n", t=TT)
    hid_f = work[:, 0:FB * S].rearrange("p (f t) -> p f t", t=S)
    hid_hi = digits("hid_hi", "big", 0, FB * S)[:, :].rearrange("p (f t) -> p f t", t=S)
    hid_lo = digits("hid_lo", "work", 0, FB * S)[:, :].rearrange("p (f t) -> p f t", t=S)
    ht_hi, ht_lo = (ctx.enter_context(nc.sbuf_tensor(name, [P, KT, S], F32R)) for name in ("ht_hi", "ht_lo"))
    HALF = SLOT // 2
    w_hi = {name: digits(f"w_hi_{name}", buffer, lo, HALF)
            for name, buffer, lo in (("work", "work", FB * S), ("big", "big", FB * S), ("tmp", "tmp", 0),
                                     ("rows", "rows", 0), ("hT", "hT", 0), ("zb", "work", 1536))}
    w_lo = [digits(f"w_lo{i}", f"ring{i}", 0, SLOT) for i in range(RING)]
    rows_t = rows[:, :].rearrange("p (t n) -> p t n", t=TT)

    gate_t = scr[:, 0:TT * D].rearrange("p (t n) -> p t n", t=TT)

    def part(lo, width, pattern=None, **sizes):
        ap = work[:, lo:lo + width]
        return ap.rearrange(pattern, **sizes) if pattern else ap

    qT = part(0, 1024, "p (b t) -> p b t", t=S)
    yaT = qT
    kT = part(1024, 512, "p (k t) -> p k t", t=S)
    zT2 = part(1536, 1088, "p (k g t) -> p k g t", k=2, g=2)
    zb2 = part(2624, 1024, "p (k j g n) -> p k j g n", k=2, j=16, g=2)
    hc, hu, he = (work[0:32, lo:lo + 512] for lo in (3648, 4160, 4672))
    hidT = part(5184, 512, "p (k h m) -> p k h m", k=2, h=2)
    kvc = part(5696, 128)
    kcd = part(5824, 128, "p (u d) -> p u d", u=2)
    vz = part(5952, 256, "p (h d) -> p h d", d=DH)
    kcT = part(10784, 64, "p (g n) -> p g n", g=GROUPS)
    qn = part(6240, 1024, "p (t n) -> p t n", t=TT)
    pc = part(6240, 512, "p (t h n) -> p t h n", t=2, n=32)
    pcT = part(6752, 512, "p (b t) -> p b t", t=P)
    qkT = part(1536, 2048, "p (a h t) -> p a h t", a=2, t=S)
    yrT = part(6240, 1024, "p (b t) -> p b t", t=S)
    w2 = part(10336, 256, "p (k h d) -> p k h d", k=2, h=2)
    vec_rows = work[0:64, 10592:10720]
    cols = part(10720, 64)
    inner = scr[:, 0:RH * 384].rearrange("p (h n) -> p h n", h=RH)
    ptb = scr[:, 0:2048].rearrange("p (b t) -> p b t", t=P)
    sq = scr[:, :].rearrange("p (t n) -> p t n", t=TT)
    C_MIX, C_MLP, C_PLE, C_Q, C_K, C_POS = 0, 8, 16, 24, 25, 32
    ss36, rr36 = tiny[:, 0:36], tiny[:, 36:72]
    gates = tiny[:, 72:120].rearrange("p (t n) -> p t n", t=TT)
    mx, sums, wts = tiny[:, 120:136], tiny[:, 136:152], tiny[:, 152:168]
    nss, nrr = tiny[:, 168:170], tiny[:, 170:172]
    kss, krr = tiny[:, 172:173], tiny[:, 173:174]
    cmx, csum = tiny[:, 176:192], tiny[:, 192:208]
    yss, yrr = tiny[:, 208:216], tiny[:, 216:224]

    const_in, x_in = sig("const_in"), sig("x_in")
    small_in = sig("small_in", 16 * 9)
    late_in = sig("late_in", 16 * 3)
    small_used = sig("small_used", 1, 1)
    tile_in = [sig(f"tile_in{r}", 16 * len(TILES) // RING) for r in range(RING)]
    tile_used = sig("tile_used", len(TILES))
    wide = Line(bank[0:2], WIDE, sig("wide_ready", len(WIDE)), sig("wide_saved", len(WIDE), 2))
    aux = Line(bank[2:4], AUX, sig("aux_ready", len(AUX)), sig("aux_saved", len(AUX), 2))
    act_step, dve_step, pool_step = sig("act_step", 59), sig("dve_step", 60), sig("pool_step", 23)
    norm_ready = sig("norm_ready", 1)
    sq_ready, ss_ready, rr_ready = sig("sq_ready", 1), sig("ss_ready", 1), sig("rr_ready", 1)
    heads_ready = sig("heads_ready", 1)
    gates_ready = sig("gates_ready", 1)
    zb_ready = sig("zb_ready", 1)
    gelu_arg, gelu_gate, gelu_ready = sig("gelu_arg", 1), sig("gelu_gate", 1), sig("gelu_ready", 1)
    kc_ss, kc_rr, kc_ready = sig("kc_ss", 1), sig("kc_rr", 1), sig("kc_ready", 1)
    cmp_arg, cmp_exp, cmp_ready = sig("cmp_arg", 1), sig("cmp_exp", 1), sig("cmp_ready", 1)
    scores_ready = sig("scores_ready", 4)
    max_ready, exp_ready, probs_ready = sig("max_ready", 3), sig("exp_ready", 3), sig("probs_ready", 3)
    inner_saved = sig("inner_saved", 1)
    rope_ready = sig("rope_ready", 1)
    silu_ready = sig("silu_ready", 1)
    yr_sq, yr_ss, yr_rr, yr_ready = sig("yr_sq", 1), sig("yr_ss", 1), sig("yr_rr", 1), sig("yr_ready", 1)
    merge_ready = sig("merge_ready", 2)
    mix_ready = sig("mix_ready", 4)
    ht_split = sig("ht_split", 12)
    w_hi_ready = sig("w_hi_ready", 2 * len(SPLITS))
    pool_share = sum(name in POOL_SPLITS for name in SPLITS)
    w_lo_ready = sig("w_lo_ready", 2 * (len(SPLITS) - pool_share))
    w_lo_pool = sig("w_lo_pool", 2 * pool_share)
    hid_hi_ready, hid_lo_ready = sig("hid_hi_ready", FB // 2), sig("hid_lo_ready", FB // 2)
    ff2_ready, ff2_saved = sig("ff2_ready", 4), sig("ff2_saved", 4)
    stored = sig("stored")
    zero_set = sig("zero_set")

    BATCHES = [(0, 0, 8), (1, 0, 4), (1, 4, 4)]

    def batch_view(b):
        keys = (BATCHES[b][0] + 1) * P
        return scores.rearrange("p (i n) -> p i n", n=keys), keys

    def mlp_nth(pre):
        return 1 if pre == "B." else 0

    def w_tile(n, shape):
        k, m = shape
        return ring[n % RING][:, 0:k * m].rearrange("p (k n) -> p k n", k=k)

    block = ctx.enter_context(nc.Block())

    def pe_kit(pe, st, wide_, aux_, tiles, splits, places):
        tile = {"at": 0, "owed": 0}

        def mm(o, lhsT, rhs, start, stop, signal=None):
            ins = pe.matmul(o, lhsT, rhs, start=start, stop=stop)
            if signal:
                ins.then_inc(st.up(signal), 1)
            elif tile["owed"]:
                ins.then_inc(st.up(tile_used, tile["owed"]), tile["owed"])
                tile["owed"] = 0

        def tp(o, in_, n=P, signal=None):
            ins = pe.transpose(o, in_, ident[0:n, 0:n])
            if signal:
                ins.then_inc(st.up(signal), 1)
            elif tile["owed"]:
                ins.then_inc(st.up(tile_used, tile["owed"]), tile["owed"])
                tile["owed"] = 0

        def next_tile(name, k, m):
            n = tile["at"]
            assert tiles[n] == name
            pe.wait_ge(tile_in[n % RING].sem, st.at(tile_in[n % RING], 16 * (n // RING + 1)))
            tile["at"] += 1
            return w_tile(n, (k, m))

        def tile_done():
            tile["owed"] += 1

        def turn_rows(names, source, ready=None, counts=(0, 0)):
            for n, name in enumerate(names):
                t, half = divmod(n, 2)
                if ready and half == 0:
                    pe.wait_ge(ready.sem, st.at(ready, counts[t]))
                b, nth = aux_.next(name)
                pe.wait_ge(aux_.saved.sem, st.at(aux_.saved, nth))
                for k in range(4):
                    lo = (4 * half + k) * P
                    tp(b[:, k * P:(k + 1) * P], source[:, t, lo:lo + P],
                       signal=aux_.ready if k == 3 else None)

        def rows_by_tile(line, names, xT, w, k, c0=0, m=BANK):
            for t, name in enumerate(names):
                b, nth = line.next(name)
                pe.wait_ge(line.saved.sem, st.at(line.saved, nth))
                for j in range(k):
                    mm(b[:, 0:m], xT[:, j, t * P:(t + 1) * P], w[:, j, c0:c0 + m], j == 0, j == k - 1,
                       line.ready if j == k - 1 else None)

        def units_by_tile(line, names, w, col=0):
            for n, name in enumerate(names):
                b, nth = line.next(name)
                pe.wait_ge(line.saved.sem, st.at(line.saved, nth))
                for u in range(2):
                    lo = col + (2 * n + u) * P
                    for k in range(KT):
                        mm(b[:, u * S:(u + 1) * S], w[:, k, lo:lo + P], hT[:, k, :], k == 0, k == KT - 1,
                           line.ready if u == 1 and k == KT - 1 else None)

        def wait_split(name, half):
            signal, n = lower_digits(name, splits)
            pe.wait_ge(signal.sem, st.at(signal, 2 * n + half + 1))

        def next_split(name, k, m):
            next_tile(name, k, m)
            halves = [w_hi[place][:, 0:k * m // 2].rearrange("p (k n) -> p k n", k=k // 2) for place in places[name]]
            lo = w_lo[(tile["at"] - 1) % RING][:, 0:k * m].rearrange("p (k n) -> p k n", k=k)
            return lo, lambda kk, cols_: halves[kk // (k // 2)][:, kk % (k // 2), cols_]

        def products(o, a_hi, a_lo, b_hi, b_lo, start, stop, signal):
            mm(o, a_lo, b_hi, start, False)
            mm(o, a_hi, b_lo, False, False)
            mm(o, a_hi, b_hi, False, stop, signal)

        def rows_by_split(line, names, name, turned=None, counts=(0, 0), m=BANK):
            lo, hi = next_split(name, KT, m)
            for t, fill in enumerate(names):
                b, nth = line.next(fill)
                pe.wait_ge(line.saved.sem, st.at(line.saved, nth))
                if turned:
                    pe.wait_ge(turned.sem, st.at(turned, counts[t]))
                tok = slice(t * P, (t + 1) * P)
                for k in range(KT):
                    last = k == KT - 1
                    if t == 0 and k % (KT // 2) == 0:
                        wait_split(name, k // (KT // 2))
                    products(b[:, 0:m], ht_hi[:, k, tok], ht_lo[:, k, tok], hi(k, slice(0, m)), lo[:, k, :], k == 0, last,
                             line.ready if last else None)
            tile_done()

        def mlp(pre):
            for n in range(8):
                lo, hi = next_split(f"{pre}ff1.{n}", KT, BANK)
                wait_split(f"{pre}ff1.{n}", 1)
                for q in range(2):
                    b, nth = wide_.next(f"{pre}f{2 * n + q}")
                    pe.wait_ge(wide_.saved.sem, st.at(wide_.saved, nth))
                    for u in range(2):
                        c = slice((2 * q + u) * P, (2 * q + u + 1) * P)
                        for k in range(KT):
                            last = k == KT - 1
                            products(b[:, u * S:(u + 1) * S], hi(k, c), lo[:, k, c], ht_hi[:, k, :], ht_lo[:, k, :],
                                     k == 0, last, wide_.ready if last and u == 1 else None)
                tile_done()
            for n in range(8):
                lo, hi = next_split(f"{pre}ff2.{n}", 4, D)
                wait_split(f"{pre}ff2.{n}", 1)
                pe.wait_ge(hid_lo_ready.sem, st.at(hid_lo_ready, FB // 2 * mlp_nth(pre) + 2 * n + 2))
                for q in range(4):
                    t, c = divmod(q, 2)
                    for k in range(4):
                        last = n == 7 and k == 3
                        tok, col = slice(t * P, (t + 1) * P), slice(c * BANK, (c + 1) * BANK)
                        products(scores[:, q * BANK:(q + 1) * BANK], hid_hi[:, 4 * n + k, tok],
                                 hid_lo[:, 4 * n + k, tok], hi(k, col), lo[:, k, col], n == 0 and k == 0, last,
                                 ff2_ready if last else None)
                tile_done()

        def finish():
            pe.drain().then_inc(st.up(tile_used, tile["owed"]), tile["owed"])
            assert tile["at"] == len(tiles)

        return Kit(mm, tp, next_tile, tile_done, turn_rows, rows_by_tile, units_by_tile, rows_by_split, mlp, finish)

    def pe_layer(pe, st):
        wide_, aux_ = wide.again(WIDE), aux.again(AUX)
        kit = pe_kit(pe, st, wide_, aux_, TILES, SPLITS, PLACES)
        mm, tp, next_tile, tile_done = kit.mm, kit.tp, kit.next_tile, kit.tile_done
        turn_rows, rows_by_tile = kit.turn_rows, kit.rows_by_tile

        def chunk(c):
            kit.rows_by_split(wide_, [f"c{c}t{t}" for t in range(TT)], f"in{c}", ht_split, (2, 4),
                              min(BANK, D_IN - c * BANK))

        def score_batch(b):
            t, h0, nh = BATCHES[b]
            view, keys = batch_view(b)
            if b:
                pe.wait_ge(exp_ready.sem, st.at(exp_ready, b))
            for h in range(h0, h0 + nh):
                g, hg = divmod(h, 4)
                for kind in range(2):
                    last = h == h0 + nh - 1 and kind == 1
                    mm(view[:, (h - h0) * 2 + kind, :], qT[64 * g:64 * g + 64, hg, t * P:(t + 1) * P],
                       kT[64 * g:64 * g + 64, kind, 0:keys], True, True, scores_ready if last else None)

        def turn_probs(b):
            pe.wait_ge(probs_ready.sem, st.at(probs_ready, b + 1))
            for n in range(4):
                bk, nth = aux_.next(f"pt{b}.{n}")
                pe.wait_ge(aux_.saved.sem, st.at(aux_.saved, nth))
                for k in range(4):
                    lo = (4 * n + k) * P
                    tp(bk[:, k * P:(k + 1) * P], rows[:, lo:lo + P], signal=aux_.ready if k == 3 else None)

        def weigh_values(b, o, last_signal):
            t, h0, nh = BATCHES[b]
            pe.wait_ge(aux_.saved.sem, st.at(aux_.saved, aux_.nth_save(f"pt{b}.3")))
            for h in range(h0, h0 + nh):
                g = h // 4
                terms = [(pcT[:, 2 * t + h // 4, :], vz[:, h % 4, :])]
                for kind, col in enumerate((Z_VS, Z_VW)):
                    for kt in range(t + 1):
                        blk = ((h - h0) * 2 + kind) * (t + 1) + kt
                        terms.append((ptb[:, blk, :], z[:, kt, col + g * DH:col + (g + 1) * DH]))
                for n, (a, v) in enumerate(terms):
                    last = n == len(terms) - 1
                    mm(o[:, h * DH:(h + 1) * DH], a, v, n == 0, last,
                       last_signal if last and h == h0 + nh - 1 else None)

        pe.wait_ge(small_in.sem, st.at(small_in, 16 * 9))
        b, nth = aux_.next("cols")
        pe.wait_ge(aux_.saved.sem, st.at(aux_.saved, nth))
        mm(b[:, 0:64], vec_rows, ident[0:64, 0:64], True, True, aux_.ready)
        pe.wait_ge(aux_.saved.sem, st.at(aux_.saved, 2))
        turn_rows([f"n{n}" for n in range(4)], x)
        for c in range(4):
            chunk(c)
        pe.wait_ge(heads_ready.sem, st.at(heads_ready, 1))
        for t in range(TT):
            b, nth = aux_.next(f"q{t}")
            pe.wait_ge(aux_.saved.sem, st.at(aux_.saved, nth))
            for hg in range(4):
                tp(b[:, hg * P:(hg + 1) * P], qn[:, t, hg * P:(hg + 1) * P], signal=aux_.ready if hg == 3 else None)
        for name, pair in (("k", (Z_KS, Z_KW)), ("zc", (Z_KC, Z_VC))):
            b, nth = aux_.next(name)
            pe.wait_ge(aux_.saved.sem, st.at(aux_.saved, nth))
            for n, col in enumerate(pair):
                for t in range(TT):
                    tp(b[:, n * S + t * P:n * S + (t + 1) * P], z[:, t, col:col + P],
                       signal=aux_.ready if n == t == 1 else None)
        chunk(4)
        pe.wait_ge(zb_ready.sem, st.at(zb_ready, 1))
        for kind, name in enumerate(("hk", "hv")):
            w = next_tile("w1" + name[1], 16, CMP_HID)
            b, nth = wide_.next(name)
            pe.wait_ge(wide_.saved.sem, st.at(wide_.saved, nth))
            for j in range(16):
                mm(b[0:32, 0:CMP_HID], zb2[:, kind, j].rearrange("p g n -> p (g n)"), w[:, j, :], j == 0, j == 15,
                   wide_.ready if j == 15 else None)
            tile_done()
        score_batch(0)
        chunk(5)
        pe.wait_ge(gelu_ready.sem, st.at(gelu_ready, 1))
        b, nth = aux_.next("hidT")
        pe.wait_ge(aux_.saved.sem, st.at(aux_.saved, nth))
        for kind in range(2):
            for half in range(2):
                n = kind * 2 + half
                mm(b[:, n * 32:n * 32 + 32], hc[:, n * P:(n + 1) * P], ident[0:32, 0:32], True, True,
                   aux_.ready if n == 3 else None)
        pe.wait_ge(aux_.saved.sem, st.at(aux_.saved, aux_.nth_save("hidT")))
        pe.wait_ge(late_in.sem, st.at(late_in, 16 * 3))
        b, nth = aux_.next("w2")
        pe.wait_ge(aux_.saved.sem, st.at(aux_.saved, nth))
        for kind in range(2):
            for half in range(2):
                mm(b[:, kind * DH:(kind + 1) * DH], hidT[:, kind, half, :], w2[:, kind, half, :],
                   half == 0, half == 1, aux_.ready if kind == half == 1 else None)
        chunk(6)
        pe.wait_ge(kc_ready.sem, st.at(kc_ready, 1))
        b, nth = aux_.next("kcT")
        pe.wait_ge(aux_.saved.sem, st.at(aux_.saved, nth))
        tp(b[:, 0:P], kcd.rearrange("p u d -> p (u d)"), signal=aux_.ready)
        pe.wait_ge(aux_.saved.sem, st.at(aux_.saved, aux_.nth_save("kcT")))
        for t in range(TT):
            b, nth = aux_.next(f"cmp{t}")
            pe.wait_ge(aux_.saved.sem, st.at(aux_.saved, nth))
            for h in range(HEADS):
                g, hg = divmod(h, 4)
                mm(b[:, h * 32:h * 32 + 32], qT[:, hg, t * P:(t + 1) * P], kcT[:, g, :], True,
                   True, aux_.ready if h == HEADS - 1 else None)
        turn_probs(0)
        score_batch(1)
        chunk(7)
        pe.wait_ge(cmp_ready.sem, st.at(cmp_ready, 1))
        b, nth = aux_.next("pcT")
        pe.wait_ge(aux_.saved.sem, st.at(aux_.saved, nth))
        for n in range(4):
            tp(b[:, n * P:(n + 1) * P], pc[:, n // 2, 4 * (n % 2):4 * (n % 2) + 4, :].rearrange("p h n -> p (h n)"),
               signal=aux_.ready if n == 3 else None)
        pe.wait_ge(aux_.saved.sem, st.at(aux_.saved, aux_.nth_save("pcT")))
        o, nth = wide_.next("o0")
        pe.wait_ge(wide_.saved.sem, st.at(wide_.saved, nth))
        weigh_values(0, o, wide_.ready)
        turn_probs(1)
        score_batch(2)
        chunk(8)
        o, nth = wide_.next("o1")
        pe.wait_ge(wide_.saved.sem, st.at(wide_.saved, nth))
        weigh_values(1, o, None)
        turn_probs(2)
        weigh_values(2, o, wide_.ready)
        pe.wait_ge(rope_ready.sem, st.at(rope_ready, 1))
        for n in range(4):
            a, t = divmod(n, 2)
            b, nth = aux_.next(f"rot{n}")
            pe.wait_ge(aux_.saved.sem, st.at(aux_.saved, nth))
            for h in range(RH):
                lo = (Z_RQ, Z_RK)[a] + h * RD
                tp(b[:, h * P:(h + 1) * P], z[:, t, lo:lo + RD], signal=aux_.ready if h == 3 else None)
        pe.wait_ge(aux_.saved.sem, st.at(aux_.saved, aux_.nth_save("rot3")))
        pe.wait_ge(exp_ready.sem, st.at(exp_ready, 3))
        for h in range(RH):
            o = scores[:, h * BANK:h * BANK + 384]
            mm(o[:, 0:S], qkT[:, 1, h, 0:P], qkT[:, 0, h, :], True, True)
            mm(o[:, S:384], qkT[:, 1, h, P:S], qkT[:, 0, h, P:S], True, True, scores_ready if h == RH - 1 else None)
        chunk(9)
        pe.wait_ge(inner_saved.sem, st.at(inner_saved, 1))
        for t in range(TT):
            o, nth = wide_.next(f"yr{t}")
            pe.wait_ge(wide_.saved.sem, st.at(wide_.saved, nth))
            for h in range(RH):
                v = [z[:, m, Z_RV + h * RD:Z_RV + (h + 1) * RD] for m in range(TT)]
                terms = [(inner[:, h, 0:P], v[0])] if t == 0 else [(inner[:, h, P:S], v[0]), (inner[:, h, S:384], v[1])]
                for n, (a, vv) in enumerate(terms):
                    last = n == len(terms) - 1
                    mm(o[:, h * RD:(h + 1) * RD], a, vv, n == 0, last,
                       wide_.ready if last and h == RH - 1 else None)
        pe.wait_ge(late_in.sem, st.at(late_in, 16 * 3))
        b, nth = aux_.next("pT")
        pe.wait_ge(aux_.saved.sem, st.at(aux_.saved, nth))
        for k in range(2):
            for t in range(TT):
                tp(b[:, k * S + t * P:k * S + (t + 1) * P], p_sb[:, t, k * P:(k + 1) * P],
                   signal=aux_.ready if k == t == 1 else None)
        pe.wait_ge(wide_.saved.sem, st.at(wide_.saved, wide_.nth_save("o1")))
        for t in range(TT):
            b, nth = aux_.next(f"ya{t}")
            pe.wait_ge(aux_.saved.sem, st.at(aux_.saved, nth))
            for k in range(4):
                tp(b[:, k * P:(k + 1) * P], z[:, t, Z_Q + k * P:Z_Q + (k + 1) * P],
                   signal=aux_.ready if k == 3 else None)
        chunk(10)
        pe.wait_ge(yr_ready.sem, st.at(yr_ready, 1))
        for t in range(TT):
            b, nth = aux_.next(f"yr{t}")
            pe.wait_ge(aux_.saved.sem, st.at(aux_.saved, nth))
            for k in range(4):
                tp(b[:, k * P:(k + 1) * P], z[:, t, Z_RQ + k * P:Z_RQ + (k + 1) * P],
                   signal=aux_.ready if k == 3 else None)
        pe.wait_ge(aux_.saved.sem, st.at(aux_.saved, aux_.nth_save("ya1")))
        w = next_tile("up_nsa", 4, D)
        for c in range(2):
            rows_by_tile(aux_, [f"upa{2 * c + t}" for t in range(TT)], yaT, w, 4, c * BANK)
        tile_done()
        pe.wait_ge(aux_.saved.sem, st.at(aux_.saved, aux_.nth_save("yr1")))
        w = next_tile("up_ret", 4, D)
        for c in range(2):
            rows_by_tile(aux_, [f"upb{2 * c + t}" for t in range(TT)], yrT, w, 4, c * BANK)
        tile_done()
        for n in range(4):
            c, t = divmod(n, 2)
            pe.wait_ge(mix_ready.sem, st.at(mix_ready, n + 1))
            b, nth = aux_.next(f"m{n}")
            pe.wait_ge(aux_.saved.sem, st.at(aux_.saved, nth))
            for k in range(4):
                lo = (4 * c + k) * P
                tp(b[:, k * P:(k + 1) * P], rows_t[:, t, lo:lo + P], signal=aux_.ready if k == 3 else None)
        mix_turned = aux_.nth_save("m2"), aux_.nth_save("m3")
        for c in range(2):
            kit.rows_by_split(aux_, [f"out{2 * c + t}" for t in range(TT)], f"out{c}", aux_.saved, mix_turned)
        turn_rows([f"nm{n}" for n in range(4)], x, aux_.saved, (aux_.nth_save("out2"), aux_.nth_save("out3")))
        pe.wait_ge(ht_split.sem, st.at(ht_split, 8))
        kit.mlp("")
        turn_rows([f"np{n}" for n in range(4)], x, ff2_saved, (2, 4))
        for c in range(2):
            kit.rows_by_split(wide_, [f"g{2 * c + t}" for t in range(TT)], f"gate{c}", ht_split, (10, 12))
        w = next_tile("ple", 2, D)
        for c in range(2):
            rows_by_tile(aux_, [f"ple{2 * c + t}" for t in range(TT)], pT, w, 2, c * BANK)
        tile_done()
        kit.finish()

    def act_rsqrt(st, act, dst, src, scale, eps, signal=None, power=-0.5):
        act.activation(dst, src, ACT.Ln, bias=eps_col[eps], scale=scale).then_inc(st.up(act_step), 1)
        act.wait_ge(st.last.sem, st.reached())
        act.activation(dst, dst, ACT.Exp, scale=power).then_inc(st.up(signal or act_step), 1)

    eps_tile = sb("eps_tile", [P, 3])
    eps_col = {EPS: eps_tile[:, 0:1], LN_EPS: eps_tile[:, 1:2]}
    half_pi = eps_tile[:, 2:3]
    eps_set = sig("eps_set")

    def act_norm(st, act, signal=None, power=-0.5):
        for t in range(TT):
            act.activation(gate_t[:, t, :], x[:, t, :], ACT.Square, accum_out=nss[:, t:t + 1]).then_inc(st.up(act_step), 1)
        act.wait_ge(st.last.sem, st.reached())
        act_rsqrt(st, act, nrr, nss, 1.0 / D, EPS, signal, power)

    def act_split(st, act, tiles, splits, name, halves=(0, 1)):
        n = tiles.index(name)
        act.wait_ge(tile_in[n % RING].sem, st.at(tile_in[n % RING], 16 * (n // RING + 1)))
        places, width = PLACES if splits is SPLITS else PLACES2, split_halves(name)
        for h in halves:
            place = places[name][h]
            earlier = [tiles.index(o) for o in splits[:splits.index(name)] if place in places[o]]
            before = [TILES.index(o) - len(TILES) for o in SPLITS if place in PLACES[o]]
            n_used = (before + earlier)[-1] + 1 + RING
            if n_used > 0:
                act.wait_ge(tile_used.sem, st.at(tile_used, n_used))
            act.activation(w_hi[place][:, 0:width], ring[n % RING][:, h * width:(h + 1) * width], ACT.Copy) \
                .then_inc(st.up(w_hi_ready), 1)

    def lower_digits(name, splits):
        mine = [n for n in splits if (n in POOL_SPLITS) == (name in POOL_SPLITS)]
        return (w_lo_pool if name in POOL_SPLITS else w_lo_ready), mine.index(name)

    def lower_split(st, eng, tiles, splits, name):
        n, nth = tiles.index(name), splits.index(name)
        signal, _ = lower_digits(name, splits)
        places, width = PLACES if splits is SPLITS else PLACES2, split_halves(name)
        for h in range(2):
            c = slice(h * width, (h + 1) * width)
            eng.wait_ge(w_hi_ready.sem, st.at(w_hi_ready, 2 * nth + h + 1))
            upper = w_hi[places[name][h]][:, 0:width].bitcast(F32)
            eng.tensor_tensor(w_lo[n % RING][:, c], ring[n % RING][:, c], upper, ALU.subtract) \
                .then_inc(st.up(signal), 1)

    def mlp_tile(pre, n):
        return f"{pre}ff{n // 8 + 1}.{n % 8}"

    def act_mlp(st, act, wide_, pre, tiles, splits):
        for n in range(1, MLP_TILES):
            act_split(st, act, tiles, splits, mlp_tile(pre, n))
            for f in ((2 * n - 2, 2 * n - 1) if n <= FB // 4 else ()):
                b, nth = wide_.next(f"{pre}f{f}")
                act.wait_ge(wide_.ready.sem, st.at(wide_.ready, nth))
                hi, h = (v[:, 2 * f:2 * f + 2, :].rearrange("p f t -> p (f t)") for v in (hid_hi, hid_f))
                act.activation(h, b, ACT.Relu).then_inc(st.up(wide_.saved), 1)
                act.wait_ge(st.last.sem, st.reached())
                act.activation(h, h, ACT.Square).then_inc(st.up(act_step), 1)
                act.wait_ge(st.last.sem, st.reached())
                act.activation(hi, h, ACT.Copy).then_inc(st.up(hid_hi_ready), 1)

    def dve_mlp(st, dve, pre, tiles, splits):
        for n in range(1, MLP_TILES):
            lower_split(st, dve, tiles, splits, mlp_tile(pre, n))
            for f in ((2 * n - 2, 2 * n - 1) if n <= FB // 4 else ()):
                hi, lo, h = (v[:, 2 * f:2 * f + 2, :] for v in (hid_hi, hid_lo, hid_f))
                dve.wait_ge(hid_hi_ready.sem, st.at(hid_hi_ready, FB // 2 * mlp_nth(pre) + f + 1))
                dve.tensor_tensor(lo, h, hi.bitcast(F32), ALU.subtract).then_inc(st.up(hid_lo_ready), 1)

    def act_layer(act, st):
        wide_, aux_ = wide.again(WIDE), aux.again(AUX)

        def save_chunk(c):
            m = min(BANK, D_IN - c * BANK)
            for t in range(TT):
                b, nth = wide_.next(f"c{c}t{t}")
                act.wait_ge(wide_.ready.sem, st.at(wide_.ready, nth))
                act.activation(z[:, t, c * BANK:c * BANK + m], b[:, 0:m], ACT.Copy, scale=nrr[:, t:t + 1]) \
                    .then_inc(st.up(wide_.saved), 1)

        def exps(b):
            _, _, nh = BATCHES[b]
            view, keys = batch_view(b)
            act.wait_ge(max_ready.sem, st.at(max_ready, b + 1))
            e = rows[:, :].rearrange("p (i n) -> p i n", n=keys)
            for n in range(2 * nh):
                act.activation(e[:, n, :], view[:, n, :], ACT.Exp, bias=mx[:, n:n + 1],
                                     accum_out=sums[:, n:n + 1]) \
                    .then_inc(st.up(exp_ready if n == 2 * nh - 1 else act_step), 1)

        act_split(st, act, TILES, SPLITS, "in0")
        act.wait_ge(aux.saved.sem, st.at(aux.saved, 2))
        act_norm(st, act)
        act.wait_ge(st.last.sem, st.reached())
        for c in range(3):
            act_split(st, act, TILES, SPLITS, f"in{c + 1}")
            save_chunk(c)
        act_split(st, act, TILES, SPLITS, "in4")
        act.wait_ge(st.last.sem, st.reached())
        act.activation(sq, z[:, :, 0:1152], ACT.Square).then_inc(st.up(sq_ready), 1)
        act.activation(gates, z[:, :, Z_GATE:Z_GATE + 24], ACT.Sigmoid).then_inc(st.up(gates_ready), 1)
        act.wait_ge(ss_ready.sem, st.at(ss_ready, 1))
        act_rsqrt(st, act, rr36, ss36, 1.0 / DH, EPS, rr_ready)
        save_chunk(3)
        save_chunk(4)
        act_split(st, act, TILES, SPLITS, "in5")
        for n, name in enumerate(("hk", "hv")):
            b, nth = wide_.next(name)
            act.wait_ge(wide_.ready.sem, st.at(wide_.ready, nth))
            act.activation(hc[:, n * CMP_HID:(n + 1) * CMP_HID], b[0:32, 0:CMP_HID], ACT.Copy) \
                .then_inc(st.up(wide_.saved), 1)
        act_split(st, act, TILES, SPLITS, "in6", (0,))
        exps(0)
        act.wait_ge(gelu_arg.sem, st.at(gelu_arg, 1))
        act.activation(he, hu, ACT.Sigmoid, scale=2.0 * (2.0 / np.pi) ** 0.5).then_inc(st.up(gelu_gate), 1)
        save_chunk(5)
        act_split(st, act, TILES, SPLITS, "in6", (1,))
        act_split(st, act, TILES, SPLITS, "in7", (0,))
        act.wait_ge(kc_ss.sem, st.at(kc_ss, 1))
        act_rsqrt(st, act, krr, kss, 1.0 / DH, EPS, kc_rr)
        save_chunk(6)
        act_split(st, act, TILES, SPLITS, "in7", (1,))
        act_split(st, act, TILES, SPLITS, "in8", (0,))
        act.wait_ge(cmp_arg.sem, st.at(cmp_arg, 1))
        act.activation(pc.rearrange("p t h n -> p (t h n)"), pc.rearrange("p t h n -> p (t h n)"), ACT.Exp) \
            .then_inc(st.up(cmp_exp), 1)
        exps(1)
        save_chunk(7)
        act_split(st, act, TILES, SPLITS, "in8", (1,))
        b, nth = wide_.next("o0")
        act.wait_ge(wide_.ready.sem, st.at(wide_.ready, nth))
        act.activation(z[:, 0, Z_Q:Z_Q + 512], b, ACT.Copy).then_inc(st.up(wide_.saved), 1)
        exps(2)
        save_chunk(8)
        act_split(st, act, TILES, SPLITS, "in9")
        act.wait_ge(st.last.sem, st.reached())
        act.activation(z[:, :, Z_MA:Z_MB], z[:, :, Z_MA:Z_MB], ACT.Sigmoid).then_inc(st.up(merge_ready), 1)
        b, nth = wide_.next("o1")
        act.wait_ge(wide_.ready.sem, st.at(wide_.ready, nth))
        act.activation(z[:, 1, Z_Q:Z_Q + 512], b, ACT.Copy).then_inc(st.up(wide_.saved), 1)
        save_chunk(9)
        act_split(st, act, TILES, SPLITS, "in10")
        for t in range(TT):
            b, nth = wide_.next(f"yr{t}")
            act.wait_ge(wide_.ready.sem, st.at(wide_.ready, nth))
            act.activation(z[:, t, Z_RQ:Z_RQ + 512], b, ACT.Copy).then_inc(st.up(wide_.saved), 1)
        act.wait_ge(st.last.sem, st.reached())
        act.activation(sq[:, :, 0:512], z[:, :, Z_RQ:Z_RQ + 512], ACT.Square).then_inc(st.up(yr_sq), 1)
        act.activation(tmp[:, 0:1024].rearrange("p (t n) -> p t n", t=TT), z[:, :, Z_RG:Z_RG + 512], ACT.Sigmoid) \
            .then_inc(st.up(silu_ready), 1)
        act.wait_ge(yr_ss.sem, st.at(yr_ss, 1))
        act_rsqrt(st, act, yrr, yss, 1.0 / RD, EPS, yr_rr)
        save_chunk(10)
        act.wait_ge(st.last.sem, st.reached())
        act.activation(z[:, :, Z_MB:D_IN], z[:, :, Z_MB:D_IN], ACT.Sigmoid).then_inc(st.up(merge_ready), 1)
        act_split(st, act, TILES, SPLITS, "out0", (0,))
        act.wait_ge(mix_ready.sem, st.at(mix_ready, 4))
        act_split(st, act, TILES, SPLITS, "out0", (1,))
        act.wait_ge(aux_.saved.sem, st.at(aux_.saved, aux_.nth_save("m3")))
        act_split(st, act, TILES, SPLITS, "out1")
        act_split(st, act, TILES, SPLITS, "ff1.0")
        act.wait_ge(aux_.saved.sem, st.at(aux_.saved, aux_.nth_save("out3")))
        act_norm(st, act, norm_ready, -1.0)
        act_mlp(st, act, wide_, "", TILES, SPLITS)
        act_split(st, act, TILES, SPLITS, "gate0")
        act.wait_ge(ff2_saved.sem, st.at(ff2_saved, 4))
        act_norm(st, act)
        act.wait_ge(st.last.sem, st.reached())
        act_split(st, act, TILES, SPLITS, "gate1")
        for n in range(4):
            c, t = divmod(n, 2)
            b, nth = wide_.next(f"g{n}")
            act.wait_ge(wide_.ready.sem, st.at(wide_.ready, nth))
            act.activation(gate_t[:, t, c * BANK:(c + 1) * BANK], b, ACT.Sigmoid, scale=nrr[:, t:t + 1]) \
                .then_inc(st.up(wide_.saved), 1)

    def dve_layer(dve, st):
        wide_, aux_ = wide.again(WIDE), aux.again(AUX)

        def tt(o, a, b, op):
            return dve.tensor_tensor(o, a, b, op)

        def tsc(o, a, s1, op0, s2=None, op1=None):
            return dve.tensor_scalar(o, a, s1, s2, op0, op1) if op1 else dve.tensor_scalar(o, a, s1, None, op0)

        def copy(o, a):
            return dve.tensor_copy(o, a)

        def split_turned(names, gain):
            for n, name in enumerate(names):
                t, half = divmod(n, 2)
                b, nth = aux_.next(name)
                dve.wait_ge(aux_.ready.sem, st.at(aux_.ready, nth))
                h, hi, lo = (v[:, 4 * half:4 * half + 4, t * P:(t + 1) * P] for v in (hT, ht_hi, ht_lo))
                tt(h, b.rearrange("p (k t) -> p k t", t=P), bc(cols[:, gain + 4 * half:gain + 4 * half + 4], 2, P),
                   ALU.mult).then_inc(st.up(aux_.saved), 1)
                dve.wait_ge(st.last.sem, st.reached())
                copy(hi, h).then_inc(st.up(dve_step), 1)
                dve.wait_ge(st.last.sem, st.reached())
                tt(lo, h, hi.bitcast(F32), ALU.subtract).then_inc(st.up(ht_split), 1)

        def maxima(b):
            t, _, nh = BATCHES[b]
            view, keys = batch_view(b)
            dve.wait_ge(scores_ready.sem, st.at(scores_ready, b + 1))
            diag = view[:, :, t * P:(t + 1) * P]
            tt(diag, diag, bc(K["causal"], 1, 2 * nh), ALU.add).then_inc(st.up(dve_step), 1)
            dve.wait_ge(st.last.sem, st.reached())
            dve.tensor_reduce(mx[:, 0:2 * nh], view, AX_X, ALU.max, negate=True).then_inc(st.up(max_ready), 1)

        def probabilities(b):
            t, h0, nh = BATCHES[b]
            _, keys = batch_view(b)
            dve.wait_ge(exp_ready.sem, st.at(exp_ready, b + 1))
            dve.reciprocal(wts[:, 0:2 * nh], sums[:, 0:2 * nh]).then_inc(st.up(dve_step), 1)
            dve.wait_ge(st.last.sem, st.reached())
            w = wts[:, 0:2 * nh].rearrange("p (h k) -> p h k", k=2)
            tt(w, w, gates[:, t, 8:24].rearrange("p (k h) -> p h k", k=2)[:, h0:h0 + nh, :], ALU.mult) \
                .then_inc(st.up(dve_step), 1)
            dve.wait_ge(st.last.sem, st.reached())
            e = rows[:, :].rearrange("p (i n) -> p i n", n=keys)
            tt(e, e, bc(wts[:, 0:2 * nh], 2, keys), ALU.mult).then_inc(st.up(probs_ready), 1)

        def save_probs(b):
            for n in range(4):
                bk, nth = aux_.next(f"pt{b}.{n}")
                dve.wait_ge(aux_.ready.sem, st.at(aux_.ready, nth))
                copy(scr[:, n * BANK:(n + 1) * BANK], bk).then_inc(st.up(aux_.saved), 1)

        b, nth = aux_.next("cols")
        dve.wait_ge(aux_.ready.sem, st.at(aux_.ready, nth))
        copy(cols, b[:, 0:64]).then_inc(st.up(aux_.saved), 1)
        dve.wait_ge(st.last.sem, st.reached())
        split_turned([f"n{n}" for n in range(4)], C_MIX)
        dve.wait_ge(sq_ready.sem, st.at(sq_ready, 1))
        dve.tensor_reduce(ss36.rearrange("p (t n) -> p t n", t=TT), sq.rearrange("p t (n d) -> p t n d", d=DH),
                                AX_X, ALU.add).then_inc(st.up(ss_ready), 1)
        dve.wait_ge(gates_ready.sem, st.at(gates_ready, 1))
        dve.wait_ge(rr_ready.sem, st.at(rr_ready, 1))
        rr = rr36.rearrange("p (t n) -> p t n", t=TT)
        for t in range(TT):
            tt(qn[:, t, :].rearrange("p (h g d) -> p g h d", g=GROUPS, d=DH),
               z[:, t, Z_Q:Z_Q + 512].rearrange("p (g h d) -> p g h d", g=GROUPS, d=DH),
               bc(rr[:, t, 0:8].rearrange("p (g h) -> p g h", g=GROUPS), 3, DH), ALU.mult) \
                .then_inc(st.up(dve_step if t else small_used), 1)
        for n, (col, r0, nh) in enumerate(((Z_KS, 12, 2), (Z_KW, 16, 2))):
            v = z[:, :, col:col + nh * DH].rearrange("p t (h d) -> p t h d", d=DH)
            tt(v, v, bc(rr[:, :, r0:r0 + nh], 3, DH), ALU.mult).then_inc(st.up(heads_ready if n == 1 else dve_step), 1)
        for t in range(TT):
            b, nth = aux_.next(f"q{t}")
            dve.wait_ge(aux_.ready.sem, st.at(aux_.ready, nth))
            tsc(qT[:, :, t * P:(t + 1) * P], b.rearrange("p (k t) -> p k t", t=P), cols[:, C_Q:C_Q + 1], ALU.mult,
                DH ** -0.5, ALU.mult).then_inc(st.up(aux_.saved), 1)
        b, nth = aux_.next("k")
        dve.wait_ge(aux_.ready.sem, st.at(aux_.ready, nth))
        tsc(kT.rearrange("p k t -> p (k t)"), b, cols[:, C_K:C_K + 1], ALU.mult).then_inc(st.up(aux_.saved), 1)
        b, nth = aux_.next("zc")
        dve.wait_ge(aux_.ready.sem, st.at(aux_.ready, nth))
        bz = b.rearrange("p (k t) -> p k t", k=2)
        for g in range(GROUPS):
            src = bz[64 * g:64 * g + 64]
            copy(zT2[0:64, :, g, 0:S], src).then_inc(st.up(dve_step), 1)
            copy(zT2[64:128, :, g, 0:S - 1], src[:, :, 1:S]).then_inc(st.up(dve_step), 1)
            copy(zT2[0:64, :, g, S:272], src[:, :, S - 1:S].broadcast_to([64, 2, 16])).then_inc(st.up(dve_step), 1)
            copy(zT2[64:128, :, g, S - 1:272], src[:, :, S - 1:S].broadcast_to([64, 2, 17])) \
                .then_inc(st.up(aux_.saved if g == 1 else dve_step), 1)
        dve.wait_ge(st.last.sem, st.reached())
        for kind in range(2):
            for g in range(GROUPS):
                for jh in range(2):
                    src = zT2[:, kind, g, 16 * jh:16 * jh + S].rearrange("p (n j l) -> p j n l", j=8, l=2)[:, :, :, 0]
                    pos = cols[:, C_POS + 16 * kind + 8 * jh:C_POS + 16 * kind + 8 * jh + 8]
                    tt(zb2[:, kind, 8 * jh:8 * jh + 8, g, :], src, bc(pos, 2, NCMP), ALU.add) \
                        .then_inc(st.up(zb_ready if kind == g == jh == 1 else dve_step), 1)
        maxima(0)
        dve.wait_ge(wide_.saved.sem, st.at(wide_.saved, wide_.nth_save("hv")))
        tt(hu, hc, hc, ALU.mult).then_inc(st.up(dve_step), 1)
        dve.wait_ge(st.last.sem, st.reached())
        tsc(hu, hu, 0.044715, ALU.mult, 1.0, ALU.add).then_inc(st.up(dve_step), 1)
        dve.wait_ge(st.last.sem, st.reached())
        tt(hu, hu, hc, ALU.mult).then_inc(st.up(gelu_arg), 1)
        dve.wait_ge(gelu_gate.sem, st.at(gelu_gate, 1))
        tt(hc, hc, he, ALU.mult).then_inc(st.up(gelu_ready), 1)
        probabilities(0)
        b, nth = aux_.next("hidT")
        dve.wait_ge(aux_.ready.sem, st.at(aux_.ready, nth))
        copy(hidT.rearrange("p k h (r m) -> p (k h) r m", r=4),
             bc(b[:, 0:P].rearrange("p (n m) -> p n m", m=32), 2, 4)).then_inc(st.up(aux_.saved), 1)
        b, nth = aux_.next("w2")
        dve.wait_ge(aux_.ready.sem, st.at(aux_.ready, nth))
        copy(kvc, b[:, 0:P]).then_inc(st.up(aux_.saved), 1)
        dve.wait_ge(st.last.sem, st.reached())
        tt(kcd[:, 0, :], kvc[:, 0:DH], kvc[:, 0:DH], ALU.mult).then_inc(st.up(dve_step), 1)
        dve.wait_ge(st.last.sem, st.reached())
        dve.tensor_reduce(kss, kcd[:, 0, :], AX_X, ALU.add).then_inc(st.up(kc_ss), 1)
        dve.wait_ge(kc_rr.sem, st.at(kc_rr, 1))
        for u in range(2):
            tsc(kcd[:, u, :], kvc[:, 0:DH], krr, ALU.mult).then_inc(st.up(dve_step), 1)
        tt(vz, bc(kvc[:, DH:2 * DH], 1, 4), bc(K["own_rows"], 2, DH), ALU.mult).then_inc(st.up(kc_ready), 1)
        b, nth = aux_.next("kcT")
        dve.wait_ge(aux_.ready.sem, st.at(aux_.ready, nth))
        for g in range(GROUPS):
            r = slice(64 * g, 64 * g + 64)
            tsc(kcT[r, g, :], b[r, 0:32], cols[r, C_K:C_K + 1], ALU.mult) \
                .then_inc(st.up(aux_.saved if g else dve_step), 1)
        for t in range(TT):
            b, nth = aux_.next(f"cmp{t}")
            dve.wait_ge(aux_.ready.sem, st.at(aux_.ready, nth))
            m = K["cmp_add"].rearrange("p (t g n) -> p t g n", t=TT, g=GROUPS)[:, t]
            tt(pc[:, t].rearrange("p (g h) n -> p g h n", g=GROUPS),
               b[:, 0:S].rearrange("p (g h n) -> p g h n", g=GROUPS, n=32), bc(m, 2, 4), ALU.add) \
                .then_inc(st.up(aux_.saved), 1)
        dve.wait_ge(st.last.sem, st.reached())
        pc2 = pc.rearrange("p t h n -> p (t h) n")
        dve.tensor_reduce(cmx, pc2, AX_X, ALU.max).then_inc(st.up(dve_step), 1)
        dve.wait_ge(st.last.sem, st.reached())
        tt(pc2, pc2, bc(cmx, 2, 32), ALU.subtract).then_inc(st.up(cmp_arg), 1)
        save_probs(0)
        dve.wait_ge(cmp_exp.sem, st.at(cmp_exp, 1))
        for t in range(TT):
            m = K["cmp_keep"].rearrange("p (t g n) -> p t g n", t=TT, g=GROUPS)[:, t]
            v = pc[:, t].rearrange("p (g h) n -> p g h n", g=GROUPS)
            tt(v, v, bc(m, 2, 4), ALU.mult).then_inc(st.up(dve_step), 1)
        dve.wait_ge(st.last.sem, st.reached())
        dve.tensor_reduce(csum, pc2, AX_X, ALU.add).then_inc(st.up(dve_step), 1)
        dve.wait_ge(st.last.sem, st.reached())
        tsc(csum, csum, 1e-30, ALU.max).then_inc(st.up(dve_step), 1)
        dve.wait_ge(st.last.sem, st.reached())
        dve.reciprocal(csum, csum).then_inc(st.up(dve_step), 1)
        dve.wait_ge(st.last.sem, st.reached())
        cs2 = csum.rearrange("p (t h) -> p t h", t=TT)
        tt(cs2, cs2, gates[:, :, 0:8], ALU.mult).then_inc(st.up(dve_step), 1)
        dve.wait_ge(st.last.sem, st.reached())
        tt(pc2, pc2, bc(csum, 2, 32), ALU.mult).then_inc(st.up(cmp_ready), 1)
        maxima(1)
        b, nth = aux_.next("pcT")
        dve.wait_ge(aux_.ready.sem, st.at(aux_.ready, nth))
        copy(pcT.rearrange("p b t -> p (b t)"), b).then_inc(st.up(aux_.saved), 1)
        probabilities(1)
        dve.wait_ge(wide_.saved.sem, st.at(wide_.saved, wide_.nth_save("o0")))
        save_probs(1)
        maxima(2)
        probabilities(2)
        aux_names = [f"pt2.{n}" for n in range(4)]
        for n in range(4):
            bk, nth = aux_.next(aux_names[n])
            dve.wait_ge(aux_.ready.sem, st.at(aux_.ready, nth))
            copy(scr[:, n * BANK:(n + 1) * BANK], bk).then_inc(st.up(aux_.saved), 1)
        for n in range(4):
            a, t = divmod(n, 2)
            b, nth = aux_.next(f"rot{n}")
            dve.wait_ge(aux_.ready.sem, st.at(aux_.ready, nth))
            copy(qkT[:, a, :, t * P:(t + 1) * P], b.rearrange("p (h t) -> p h t", t=P)).then_inc(st.up(aux_.saved), 1)
        dve.wait_ge(scores_ready.sem, st.at(scores_ready, 4))
        tt(inner, scores.rearrange("p (h n) -> p h n", n=BANK)[:, :, 0:384],
           K["decay"].rearrange("p (h n) -> p h n", h=RH), ALU.mult).then_inc(st.up(inner_saved), 1)
        b, nth = aux_.next("pT")
        dve.wait_ge(aux_.ready.sem, st.at(aux_.ready, nth))
        copy(pT.rearrange("p k t -> p (k t)"), b).then_inc(st.up(aux_.saved), 1)
        for t in range(TT):
            b, nth = aux_.next(f"ya{t}")
            dve.wait_ge(aux_.ready.sem, st.at(aux_.ready, nth))
            copy(yaT[:, :, t * P:(t + 1) * P], b.rearrange("p (h t) -> p h t", t=P)).then_inc(st.up(aux_.saved), 1)
        dve.wait_ge(yr_sq.sem, st.at(yr_sq, 1))
        dve.tensor_reduce(yss.rearrange("p (t h) -> p t h", t=TT),
                                sq[:, :, 0:512].rearrange("p t (h d) -> p t h d", d=RD), AX_X, ALU.add) \
            .then_inc(st.up(yr_ss), 1)
        dve.wait_ge(silu_ready.sem, st.at(silu_ready, 1))
        sg = tmp[:, 0:1024].rearrange("p (t n) -> p t n", t=TT)
        tt(sg, sg, z[:, :, Z_RG:Z_RG + 512], ALU.mult).then_inc(st.up(dve_step), 1)
        dve.wait_ge(yr_rr.sem, st.at(yr_rr, 1))
        yv = z[:, :, Z_RQ:Z_RQ + 512].rearrange("p t (h d) -> p t h d", d=RD)
        tt(yv, yv, bc(yrr.rearrange("p (t h) -> p t h", t=TT), 3, RD), ALU.mult).then_inc(st.up(dve_step), 1)
        dve.wait_ge(st.last.sem, st.reached())
        yv = z[:, :, Z_RQ:Z_RQ + 512]
        tt(yv, yv, sg, ALU.mult).then_inc(st.up(yr_ready), 1)
        for t in range(TT):
            b, nth = aux_.next(f"yr{t}")
            dve.wait_ge(aux_.ready.sem, st.at(aux_.ready, nth))
            copy(yrT[:, :, t * P:(t + 1) * P], b.rearrange("p (h t) -> p h t", t=P)).then_inc(st.up(aux_.saved), 1)
        dve.wait_ge(merge_ready.sem, st.at(merge_ready, 1))
        for n in range(4):
            c, t = divmod(n, 2)
            b, nth = aux_.next(f"upa{n}")
            dve.wait_ge(aux_.ready.sem, st.at(aux_.ready, nth))
            tt(rows_t[:, t, c * BANK:(c + 1) * BANK], b, z[:, t, Z_MA + c * BANK:Z_MA + (c + 1) * BANK],
               ALU.mult).then_inc(st.up(aux_.saved), 1)
        dve.wait_ge(merge_ready.sem, st.at(merge_ready, 2))
        for n in range(4):
            c, t = divmod(n, 2)
            b, nth = aux_.next(f"upb{n}")
            dve.wait_ge(aux_.ready.sem, st.at(aux_.ready, nth))
            u = tmp[:, n * BANK:(n + 1) * BANK]
            tt(u, b, z[:, t, Z_MB + c * BANK:Z_MB + (c + 1) * BANK], ALU.mult).then_inc(st.up(aux_.saved), 1)
            dve.wait_ge(st.last.sem, st.reached())
            r = rows_t[:, t, c * BANK:(c + 1) * BANK]
            tt(r, r, u, ALU.add).then_inc(st.up(mix_ready), 1)
        for n in range(4):
            c, t = divmod(n, 2)
            b, nth = aux_.next(f"m{n}")
            dve.wait_ge(aux_.ready.sem, st.at(aux_.ready, nth))
            hi, lo = (v[:, 4 * c:4 * c + 4, t * P:(t + 1) * P] for v in (ht_hi, ht_lo))
            b4 = b.rearrange("p (k t) -> p k t", t=P)
            copy(hi, b4).then_inc(st.up(dve_step), 1)
            dve.wait_ge(st.last.sem, st.reached())
            tt(lo, b4, hi.bitcast(F32), ALU.subtract).then_inc(st.up(aux_.saved), 1)
        for n in range(4):
            if n == 2:
                lower_split(st, dve, TILES, SPLITS, "ff1.0")
            c, t = divmod(n, 2)
            b, nth = aux_.next(f"out{n}")
            dve.wait_ge(aux_.ready.sem, st.at(aux_.ready, nth))
            xv = x[:, t, c * BANK:(c + 1) * BANK]
            tt(xv, xv, b, ALU.add).then_inc(st.up(aux_.saved), 1)
        split_turned([f"nm{n}" for n in range(4)], C_MLP)
        dve_mlp(st, dve, "", TILES, SPLITS)
        lower_split(st, dve, TILES, SPLITS, "gate0")
        dve.wait_ge(norm_ready.sem, st.at(norm_ready, 1))
        for n in range(4):
            t, c = divmod(n, 2)
            dve.wait_ge(ff2_ready.sem, st.at(ff2_ready, n + 1))
            xv = x[:, t, c * BANK:(c + 1) * BANK]
            dve.scalar_tensor_tensor(out=xv, in0=scores[:, n * BANK:(n + 1) * BANK], scalar=nrr[:, t:t + 1], in1=xv,
                                     op0=ALU.mult, op1=ALU.add).then_inc(st.up(ff2_saved), 1)
        split_turned([f"np{n}" for n in range(4)], C_PLE)
        lower_split(st, dve, TILES, SPLITS, "gate1")
        dve.wait_ge(st.last.sem, st.reached())
        for n in range(4):
            c, t = divmod(n, 2)
            dve.wait_ge(wide_.saved.sem, st.at(wide_.saved, wide_.nth_save(f"g{n}")))
            b, nth = aux_.next(f"ple{n}")
            dve.wait_ge(aux_.ready.sem, st.at(aux_.ready, nth))
            u = tmp[:, n * BANK:(n + 1) * BANK]
            tt(u, b, gate_t[:, t, c * BANK:(c + 1) * BANK], ALU.mult).then_inc(st.up(dve_step), 1)
            dve.wait_ge(st.last.sem, st.reached())
            xv = x[:, t, c * BANK:(c + 1) * BANK]
            tt(xv, xv, u, ALU.add).then_inc(st.up(aux_.saved), 1)

    def pool_layer(pool, st):
        for c in range(6):
            lower_split(st, pool, TILES, SPLITS, f"in{c}")
        pool.wait_ge(wide.again(WIDE).saved.sem, st.at(wide.again(WIDE).saved, wide.again(WIDE).nth_save("c4t1")))
        t4 = [tmp[:, n * 512:(n + 1) * 512].rearrange("p (t h d) -> p t h d", t=TT, d=64) for n in range(4)]
        cos, sin = (bc(K[n].rearrange("p (t d) -> p t d", t=TT), 2, RH) for n in ("cos", "sin"))
        for a, col in enumerate((Z_RQ, Z_RK)):
            v = z[:, :, col:col + 512].rearrange("p t (h u d) -> p t h u d", u=2, d=64)
            x1, x2 = ([v[:, t, :, u, :] for t in range(TT)] for u in range(2))
            for t in range(TT):
                for n, (xx, tab) in enumerate(((x1, cos), (x2, sin), (x1, sin), (x2, cos))):
                    pool.tensor_tensor(t4[n][:, t], xx[t], tab[:, t], ALU.mult).then_inc(st.up(pool_step), 1)
            pool.wait_ge(st.last.sem, st.reached())
            for t in range(TT):
                pool.tensor_tensor(x1[t], t4[0][:, t], t4[1][:, t], ALU.subtract).then_inc(st.up(pool_step), 1)
                pool.tensor_tensor(x2[t], t4[2][:, t], t4[3][:, t], ALU.add) \
                    .then_inc(st.up(rope_ready if a == t == 1 else pool_step), 1)
            if a == 0:
                pool.wait_ge(st.last.sem, st.reached())
        for name in [f"in{c}" for c in range(6, N_IN)] + ["out0", "out1"]:
            lower_split(st, pool, TILES, SPLITS, name)

    uT = part(0, 1024, "p (b t) -> p b t", t=S)
    sqT = part(1024, 1024, "p (b t) -> p b t", t=S)
    ao = part(1024, 1024, "p (t n) -> p t n", t=TT)
    skT = part(2048, 1024, "p (b t) -> p b t", t=S)
    sv = part(3072, 1024, "p (t n) -> p t n", t=TT)
    BD = part(4096, 1024, "p (r j u c) -> p r j u c", r=2, j=SJ, u=2)
    BT = part(5120, 1024, "p (r q n) -> p r q n", r=2, q=4)
    CT = part(6144, 1024, "p (r i m) -> p r i m", r=2, i=4)
    cin = part(7168, 1024, "p (r i u n) -> p r i u n", r=2, i=4, u=2)
    bin_ = big[:, 4096:4608].rearrange("p (r j c) -> p r j c", r=2, j=SJ)
    t1, t2 = part(8704, 512), part(9216, 512)
    wst = [part(9728 + 512 * n, 512) for n in range(2)]
    pu1, pu2 = part(4096, 512), part(4608, 512)
    xst = [part(7168 + 512 * n, 512) for n in range(3)]
    ctab, stab = (big[:, n * 4096:(n + 1) * 4096].rearrange("p (j t) -> p j t", t=S) for n in range(2))
    ln_lo = CONST_AT["cmp_add"][0]
    assert CONST_AT["sin"][1] - ln_lo == 2 * D
    ln_g, ln_b = const[:, ln_lo:ln_lo + D], const[:, ln_lo + D:ln_lo + 2 * D]
    prow = big[0:16, 0:18 * P].rearrange("p (r n) -> p r n", n=P)
    log_dt, dt = tiny[0:16, 340:342], tiny[0:16, 342:344]
    pcol = tiny[:, 240:320].rearrange("p (r j) -> p r j", j=SJ)
    cm, sm, cn, sn2 = (tiny[:, 400 + 16 * n:416 + 16 * n] for n in range(4))
    b_col, d_col = tiny[:, 330:334], tiny[:, 334:338]
    zs = rows[:, 0:1536].rearrange("p (h n) -> p h n", h=4)
    sp_ = tmp[:, 0:1536].rearrange("p (h n) -> p h n", h=4)
    sw = scr[:, 0:1536].rearrange("p (h n) -> p h n", h=4)
    yT = hT[:, 4:8, :]
    ge = part(2048, 1024)
    lsum, lmu, lss, lrr = (tiny[:, 350 + 2 * n:352 + 2 * n] for n in range(4))
    dqT = part(0, 2048, "p (b t) -> p b t", t=S)
    dkT = part(2048, 1024, "p (v t) -> p v t", t=S)
    dv = part(3072, 512, "p (t n) -> p t n", t=TT)
    qiT = part(3584, 512, "p (b t) -> p b t", t=S)
    kiz = part(4096, 1024, "p (h t) -> p h t", t=S)
    relu_ = part(5120, 2048)
    isc, irep, iadd = part(7168, 384), part(7552, 384), part(7936, 384)
    m8 = tiny[:, 470:478]
    wi = tiny[:, 480:496]
    dob = big[:, 0:2048].rearrange("p (t n) -> p t n", t=TT)
    (P_LR, P_LI, P_Y, P_TH, P_W, P_E, P_KQ, P_RED, P_HA, P_SN, P_CS, P_SIN, P_CM1, P_COS, P_MAG, P_NR, P_T1,
     P_T2) = range(18)
    P_CR, P_CI, P_ABI, P_DEN = P_Y, P_W, P_SN, P_KQ

    par_in, b_in, c_in, ln_in = sig("par_in"), sig("b_in"), sig("c_in"), sig("ln_in")
    dt_ready, sin_arg, sin_ready, par_ready = sig("dt_ready"), sig("sin_arg"), sig("sin_ready"), sig("par_ready")
    bd_ready = sig("bd_ready")
    sbz_ready, ln1p_ready, sp_ready, sw_arg, sw_ready = (sig(n) for n in (
        "sbz_ready", "ln1p_ready", "sp_ready", "sw_arg", "sw_ready"))
    scan_ready, state_used = sig("scan_ready"), sig("state_used")
    state_pool, state_dve = sig("state_pool"), sig("state_dve")
    TURNED_BY_DVE = range(2, SJ, 3)

    def states(j):
        mine = [n for n in range(j + 1) if (n in TURNED_BY_DVE) == (j in TURNED_BY_DVE)]
        return (state_dve if j in TURNED_BY_DVE else state_pool), len(mine)

    def place_free(wide_, j):
        q, jl = divmod(j - len(xst), 4)
        return (wide_.saved, wide_.nth_save(f"y{q}")) if jl == 3 else (state_used, j - len(xst) - q + 1)
    ygelu_arg, ygelu_gate, ygelu_ready, y_ready = (sig(n) for n in ("ygelu_arg", "ygelu_gate", "ygelu_ready", "y_ready"))
    ln_stats, ln_done = sig("ln_stats"), sig("ln_done")
    idx_ready, idx_relu, idx_summed = sig("idx_ready"), sig("idx_relu"), sig("idx_summed")
    kiz_zero = sig("kiz_zero")
    dsc_ready, dsc_read, dmax_ready, dexp_ready, dprobs_ready = (sig(n) for n in (
        "dsc_ready", "dsc_read", "dmax_ready", "dexp_ready", "dprobs_ready"))

    DSA_BATCHES = [(0, 0, 16), (1, 0, 8), (1, 8, 8)]

    def dsa_view(b):
        keys = (DSA_BATCHES[b][0] + 1) * P
        return scores.rearrange("p (i n) -> p i n", n=keys), keys

    def slots(b):
        _, h0, nh = DSA_BATCHES[b]
        return [h0 + 2 * n for n in range(nh // 2)] + [h0 + 2 * n + 1 for n in range(nh // 2)]

    def flat(ap):
        return ap.rearrange("p a b -> p (a b)")

    def sp_tail(sp):
        where = Where()
        sp.wait_ge(ff2_saved.sem, DEPTH * ff2_saved.per_layer)

        def load(dst, src, signal):
            sp.dma_start(dst, src).then_inc(signal.sem, 16)

        def load_ln(which, n):
            for dst, v in ((ln_g, "g"), (ln_b, "b")):
                load(dst, I[f"ln_{which}_{v}_2"][n:n + 1, :].broadcast_to([P, D]), ln_in)

        for r, name in ((P_LR, "ssm_lam_re_2"), (P_LI, "ssm_lam_im_2")):
            load(prow[:, r, :], I[name][0].rearrange("(j u) n -> j (u n)", u=2), par_in)
        load(log_dt, I["ssm_log_dt_2"][0].rearrange("(j u) -> j u", u=2), par_in)
        load(vec_rows[0:4, :], I["ssm_d_2"][0].rearrange("(r g) c -> r (g c)", r=4), par_in)
        load(vec_rows[4:8, :], I["ssm_b_glu_2"][0].rearrange("(r n) -> r n", r=4), par_in)
        for r, name in enumerate(("ssm_c_re_2", "ssm_c_im_2")):
            for u in range(2):
                load(cin[:, r, :, u, :], I[name][0].rearrange("(i g) c n -> (g c) i n", i=4), c_in)
        for r, name in enumerate(("ssm_b_re_2", "ssm_b_im_2")):
            load(bin_[:, r], I[name][0].rearrange("(j u) n c -> (u n) j c", u=2), b_in)
        load_ln("mix", 0)
        for n, name in enumerate(TILES2):
            sp.wait_ge(tile_used.sem, where.value(tile_used, n + 1))
            kind, _, num = name.rpartition(".")
            layer = "AB".find(name[0])
            if kind.endswith("ff1"):
                s, k, m = I["mlp_w1_2"][layer][:, int(num) * BANK:(int(num) + 1) * BANK], KT, BANK
            elif kind.endswith("ff2"):
                s, k, m = I["mlp_w2_2"][layer][int(num) * BANK:(int(num) + 1) * BANK, :], 4, D
            elif name == "glu":
                s, k, m = I["ssm_w_glu_2"][0], 4, SB_W
            else:
                w = I[{"sb": "sb_ssm_w_in_2", "sbo": "sb_ssm_w_out_2", "ds": "dsa_w_in_2",
                       "dso": "dsa_w_out_2"}[name[:-1]]][0]
                c = int(name[-1])
                k, m = KT, min(BANK, w.shape[1] - c * BANK)
                s = w[:, c * BANK:c * BANK + m]
            sp.dma_start(w_tile(n, (k, m)), s.rearrange("(k p) n -> p k n", p=P)) \
                .then_inc(tile_in[n % RING].sem, 16)
            if name in ("A.ff1.0", "ds3", "B.ff1.0"):
                done = {"A.ff1.0": 1, "ds3": 2, "B.ff1.0": 3}[name]
                sp.wait_ge(ln_done.sem, TT * done)
                load_ln(*{1: ("ffn", 0), 2: ("mix", 1), 3: ("ffn", 1)}[done])
        for t in range(TT):
            sp.wait_ge(ln_done.sem, TT * 3 + t + 1)
            sp.dma_start(out[0][t * P:(t + 1) * P, :], x[:, t, :]).then_inc(stored.sem, 16)
        sp.wait_ge(stored.sem, TT * 16)

    def pe_tail(pe, st):
        wide_, aux_ = wide.again(WIDE2), aux.again(AUX2)
        kit = pe_kit(pe, st, wide_, aux_, TILES2, SPLITS2, PLACES2)
        mm, tp, next_tile, tile_done = kit.mm, kit.tp, kit.next_tile, kit.tile_done

        def sb_scores(batch):
            for hl in range(4):
                blk, r = (4 * batch + hl) // 2, slice(64 * (hl % 2), 64 * (hl % 2) + 64)
                o = scores[:, hl * BANK:hl * BANK + 384]
                mm(o[:, 0:S], skT[r, blk, 0:P], sqT[r, blk, :], True, True)
                mm(o[:, S:384], skT[r, blk, P:S], sqT[r, blk, P:S], True, True, sbz_ready if hl == 3 else None)

        def suffix_sums(batch):
            pe.wait_ge(sp_ready.sem, st.at(sp_ready, batch + 1))
            for hl in range(4):
                b, nth = aux_.next(f"cs{4 * batch + hl}")
                pe.wait_ge(aux_.saved.sem, st.at(aux_.saved, nth))
                mm(b[:, 0:384], K["suffix"], sp_[:, hl, :], True, False)
                mm(b[:, P:S], K["ones"], sp_[:, hl, S:384], False, True, aux_.ready)

        def sb_values(batch):
            pe.wait_ge(sw_ready.sem, st.at(sw_ready, batch + 1))
            for t in range(TT):
                o, nth = wide_.next(f"s{'AB'[batch]}{t}")
                pe.wait_ge(wide_.saved.sem, st.at(wide_.saved, nth))
                for hl in range(4):
                    h = 4 * batch + hl
                    v = [sv[:, m, h * DH:(h + 1) * DH] for m in range(TT)]
                    terms = [(sw[:, hl, 0:P], v[0])] if t == 0 else [(sw[:, hl, P:S], v[0]), (sw[:, hl, S:384], v[1])]
                    for n, (a, vv) in enumerate(terms):
                        last = n == len(terms) - 1
                        mm(o[:, hl * DH:(hl + 1) * DH], a, vv, n == 0, last, wide_.ready if last and hl == 3 else None)

        def ssm_in(j):
            q, jl = divmod(j, 4)
            r = slice(32 * jl, 32 * jl + 32)
            b, nth = aux_.next(f"bu{j}")
            pe.wait_ge(aux_.saved.sem, st.at(aux_.saved, nth))
            for ri in range(2):
                mm(b[:, ri * S:(ri + 1) * S], BT[r, ri, q, :], uT[r, q, :], True, True, aux_.ready if ri else None)

        y_bank = [None]

        def ssm_out(j):
            q, jl = divmod(j, 4)
            if jl == 0:
                y_bank[0], nth = wide_.next(f"y{q}")
                pe.wait_ge(wide_.saved.sem, st.at(wide_.saved, nth))
            signal, n = states(j)
            pe.wait_ge(signal.sem, st.at(signal, n))
            r = slice(32 * jl, 32 * jl + 32)
            for ri in range(2):
                ins = pe.matmul(y_bank[0][r, 0:S], CT[:, ri, q, r], xst[j % len(xst)][:, ri * S:(ri + 1) * S],
                                start=ri == 0, stop=ri == 1)
            ins.then_inc(st.up(wide_.ready if jl == 3 else state_used), 1)

        pe.wait_ge(aux_.saved.sem, st.at(aux_.saved, 2))
        kit.turn_rows([f"A.x{n}" for n in range(4)], x)
        pe.wait_ge(c_in.sem, st.at(c_in, 64))
        for ri in range(2):
            b, nth = aux_.next(f"ct{ri}")
            pe.wait_ge(aux_.saved.sem, st.at(aux_.saved, nth))
            for i in range(4):
                tp(b[:, i * P:(i + 1) * P], cin[:, ri, i].rearrange("p u n -> p (u n)"),
                   signal=aux_.ready if i == 3 else None)
        pe.wait_ge(aux_.saved.sem, st.at(aux_.saved, aux_.nth_save("A.x3")))
        w = next_tile("sb3", KT, BANK)
        kit.units_by_tile(wide_, ["u0", "u1"], w)
        tile_done()
        pe.wait_ge(par_ready.sem, st.at(par_ready, 1))
        b, nth = aux_.next("par")
        pe.wait_ge(aux_.saved.sem, st.at(aux_.saved, nth))
        for n, r in enumerate((P_CR, P_CI, P_MAG, P_COS, P_SIN)):
            tp(b[:, n * SJ:(n + 1) * SJ], prow[:, r, :], 16)
        tp(b[:, 80:144], vec_rows, 64, aux_.ready)
        w = next_tile("sb0", KT, BANK)
        kit.units_by_tile(wide_, ["sq0", "sq1"], w)
        tile_done()
        w = next_tile("sb1", KT, BANK)
        kit.units_by_tile(wide_, ["sk0", "sk1"], w)
        tile_done()
        w = next_tile("sb2", KT, BANK)
        kit.rows_by_tile(wide_, ["sv0", "sv1"], hT, w, KT)
        tile_done()
        pe.wait_ge(bd_ready.sem, st.at(bd_ready, 1))
        for ri in range(2):
            b, nth = aux_.next(f"bt{ri}")
            pe.wait_ge(aux_.saved.sem, st.at(aux_.saved, nth))
            for q in range(4):
                tp(b[:, q * P:(q + 1) * P], BD[:, ri, 4 * q:4 * q + 4].rearrange("p j u c -> p (j u c)"),
                   signal=aux_.ready if q == 3 else None)
        pe.wait_ge(wide_.saved.sem, st.at(wide_.saved, wide_.nth_save("sk1")))
        pe.wait_ge(aux_.saved.sem, st.at(aux_.saved, aux_.nth_save("bt1")))
        for j in range(SJ + 2):
            if j < SJ:
                ssm_in(j)
            if j == 1:
                sb_scores(0)
            if j == 3:
                suffix_sums(0)
                sb_scores(1)
            if j == 8:
                suffix_sums(1)
            if j >= 2:
                ssm_out(j - 2)
            if j in (9, 13):
                sb_values(j // 13)
        pe.wait_ge(ygelu_ready.sem, st.at(ygelu_ready, 1))
        w = next_tile("glu", 4, SB_W)
        for n in range(2):
            b, nth = wide_.next(f"glu{n}")
            pe.wait_ge(wide_.saved.sem, st.at(wide_.saved, nth))
            for u in range(2):
                lo = (2 * n + u) * P
                for k in range(4):
                    mm(b[:, u * S:(u + 1) * S], w[:, k, lo:lo + P], yT[:, k, :], k == 0, k == 3,
                       wide_.ready if u == 1 and k == 3 else None)
        tile_done()
        pe.wait_ge(wide_.saved.sem, st.at(wide_.saved, wide_.nth_save("sB1")))
        for t in range(TT):
            b, nth = aux_.next(f"ao{t}")
            pe.wait_ge(aux_.saved.sem, st.at(aux_.saved, nth))
            for k in range(4):
                tp(b[:, k * P:(k + 1) * P], ao[:, t, k * P:(k + 1) * P], signal=aux_.ready if k == 3 else None)
        pe.wait_ge(aux_.saved.sem, st.at(aux_.saved, aux_.nth_save("ao1")))
        pe.wait_ge(y_ready.sem, st.at(y_ready, 1))

        def project_and_mlp(pre, name, norm):
            for c in range(2):
                kit.rows_by_split(aux_, [f"{pre}out{2 * c + t}" for t in range(TT)], f"{name}{c}")
            kit.turn_rows([f"{pre}n{n}" for n in range(4)], x, ln_done, (2 * norm - 1, 2 * norm))
            pe.wait_ge(aux_.saved.sem, st.at(aux_.saved, aux_.nth_save(f"{pre}n3")))
            kit.mlp(pre)

        project_and_mlp("A.", "sbo", 1)
        kit.turn_rows([f"B.x{n}" for n in range(4)], x, ln_done, (3, 4))
        pe.wait_ge(aux_.saved.sem, st.at(aux_.saved, aux_.nth_save("B.x3")))
        w = next_tile("ds3", KT, DSA_IN - I_QI)
        kit.units_by_tile(wide_, ["qi"], w)
        b, nth = wide_.next("kiw")
        pe.wait_ge(wide_.saved.sem, st.at(wide_.saved, nth))
        for k in range(KT):
            mm(b[0:32, 0:S], w[:, k, I_KI - I_QI:I_WI - I_QI], hT[:, k, :], k == 0, k == KT - 1)
        for t in range(TT):
            for k in range(KT):
                mm(b[:, S + 8 * t:S + 8 * t + 8], hT[:, k, t * P:(t + 1) * P], w[:, k, I_WI - I_QI:DSA_IN - I_QI],
                   k == 0, k == KT - 1, wide_.ready if t == 1 and k == KT - 1 else None)
        tile_done()

        def index_scores(t):
            if t == 0:
                pe.wait_ge(wide_.saved.sem, st.at(wide_.saved, wide_.nth_save("kiw")))
            else:
                pe.wait_ge(idx_relu.sem, st.at(idx_relu, 1))
            keys = (t + 1) * P
            for h in range(IDX_HEADS):
                mm(scores[:, h * keys:(h + 1) * keys], qiT[:, h // 4, t * P:(t + 1) * P], kiz[:, h % 4, 0:keys],
                   True, True, idx_ready if h == IDX_HEADS - 1 else None)

        pe.wait_ge(ff2_saved.sem, st.at(ff2_saved, 4))
        index_scores(0)
        w = next_tile("ds2", KT, BANK)
        kit.units_by_tile(wide_, ["dk"], w)
        b, nth = wide_.next("dv")
        pe.wait_ge(wide_.saved.sem, st.at(wide_.saved, nth))
        for t in range(TT):
            for k in range(KT):
                mm(b[:, t * S:(t + 1) * S], hT[:, k, t * P:(t + 1) * P], w[:, k, S:2 * S], k == 0, k == KT - 1,
                   wide_.ready if t == 1 and k == KT - 1 else None)
        tile_done()
        index_scores(1)
        for c in range(2):
            w = next_tile(f"ds{c}", KT, BANK)
            kit.units_by_tile(wide_, [f"dq{2 * c}", f"dq{2 * c + 1}"], w)
            tile_done()

        def dsa_scores(b):
            t, _, _ = DSA_BATCHES[b]
            view, keys = dsa_view(b)
            if b == 0:
                pe.wait_ge(idx_relu.sem, st.at(idx_relu, 2))
                pe.wait_ge(wide_.saved.sem, st.at(wide_.saved, wide_.nth_save("dq3")))
            else:
                pe.wait_ge(dsc_read.sem, st.at(dsc_read, b))
            hs = slots(b)
            for n, h in enumerate(hs):
                r = slice(64 * (h % 2), 64 * (h % 2) + 64)
                mm(view[:, n, :], dqT[r, h // 2, t * P:(t + 1) * P], dkT[r, h // 4, 0:keys], True, True,
                   dsc_ready if n == len(hs) - 1 else None)

        def dsa_probs(b):
            pe.wait_ge(dprobs_ready.sem, st.at(dprobs_ready, b + 1))
            for n in range(4):
                bk, nth = aux_.next(f"pt{b}.{n}")
                pe.wait_ge(aux_.saved.sem, st.at(aux_.saved, nth))
                for k in range(4):
                    lo = (4 * n + k) * P
                    tp(bk[:, k * P:(k + 1) * P], rows[:, lo:lo + P], signal=aux_.ready if k == 3 else None)

        def dsa_values(b):
            t, h0, nh = DSA_BATCHES[b]
            pe.wait_ge(aux_.saved.sem, st.at(aux_.saved, aux_.nth_save(f"pt{b}.3")))
            place = {h: n for n, h in enumerate(slots(b))}
            for half in range(nh // 8):
                o, nth = wide_.next(f"do{b + 1 if b else half}")
                pe.wait_ge(wide_.saved.sem, st.at(wide_.saved, nth))
                for hl in range(8):
                    h = h0 + 8 * half + hl
                    for kt in range(t + 1):
                        last = kt == t
                        mm(o[:, hl * DH:(hl + 1) * DH], ptb[:, place[h] * (t + 1) + kt, :],
                           dv[:, kt, (h // 4) * DH:(h // 4 + 1) * DH], kt == 0, last,
                           wide_.ready if last and hl == 7 else None)

        dsa_scores(0)
        dsa_scores(1)
        dsa_probs(0)
        dsa_values(0)
        dsa_scores(2)
        dsa_probs(1)
        dsa_values(1)
        dsa_probs(2)
        dsa_values(2)
        pe.wait_ge(wide_.saved.sem, st.at(wide_.saved, wide_.nth_save("do3")))
        kit.turn_rows([f"do{n}" for n in range(4)], dob)
        pe.wait_ge(aux_.saved.sem, st.at(aux_.saved, aux_.nth_save("do3")))
        project_and_mlp("B.", "dso", 3)

    def act_tail(act, st):
        wide_, aux_ = wide.again(WIDE2), aux.again(AUX2)
        norm = [0]

        def save(name, dst, lo=0, hi=BANK, scale=1.0, rows_=slice(0, P), last=True):
            b, nth = wide_.next(name)
            act.wait_ge(wide_.ready.sem, st.at(wide_.ready, nth))
            act.activation(dst, b[rows_, lo:hi], ACT.Copy, scale=scale) \
                .then_inc(st.up(wide_.saved if last else act_step), 1)
            return b

        def ln_statistics(ready, counts):
            for t in range(TT):
                act.wait_ge(ready.sem, st.at(ready, counts[t]))
                one = slice(t, t + 1)
                act.activation(gate_t[:, t, :], x[:, t, :], ACT.Copy, accum_out=lsum[:, one]).then_inc(st.up(act_step), 1)
                act.wait_ge(st.last.sem, st.reached())
                act.activation(lmu[:, one], lsum[:, one], ACT.Copy, scale=-1.0 / D).then_inc(st.up(act_step), 1)
                act.wait_ge(st.last.sem, st.reached())
                act.activation(gate_t[:, t, :], x[:, t, :], ACT.Square, bias=lmu[:, one], accum_out=lss[:, one]) \
                    .then_inc(st.up(act_step), 1)
                act.wait_ge(st.last.sem, st.reached())
                act_rsqrt(st, act, lrr[:, one], lss[:, one], 1.0 / D, LN_EPS, ln_stats)

        act.wait_ge(par_in.sem, st.at(par_in, 16 * 5))
        act.activation(dt, log_dt, ACT.Exp).then_inc(st.up(dt_ready), 1)
        act.wait_ge(sin_arg.sem, st.at(sin_arg, 1))
        act.activation(prow[:, P_SN, :], prow[:, P_RED, :], ACT.Sin).then_inc(st.up(act_step), 1)
        act.activation(prow[:, P_CS, :], prow[:, P_HA, :], ACT.Sin, bias=half_pi[0:16, :], scale=-1.0) \
            .then_inc(st.up(sin_ready), 1)
        for n in range(2):
            save(f"u{n}", flat(uT[:, 2 * n:2 * n + 2, :]))
        for n in range(2):
            save(f"sq{n}", flat(sqT[:, 2 * n:2 * n + 2, :]), scale=DH ** -0.5)
        for n in range(2):
            save(f"sk{n}", flat(skT[:, 2 * n:2 * n + 2, :]))
        for t in range(TT):
            save(f"sv{t}", sv[:, t, :])

        def softplus_parts(batch):
            act.wait_ge(sbz_ready.sem, st.at(sbz_ready, batch + 1))
            v = scores.rearrange("p (h n) -> p h n", n=BANK)[:, :, 0:384]
            if batch:
                act.wait_ge(st.last.sem, st.reached())
            act.activation(sp_, v, ACT.Abs).then_inc(st.up(act_step), 1)
            act.activation(zs, v, ACT.Copy).then_inc(st.up(act_step), 1)
            act.wait_ge(st.last.sem, st.reached())
            act.activation(sp_, sp_, ACT.Exp, scale=-1.0).then_inc(st.up(act_step), 1)
            act.wait_ge(st.last.sem, st.reached())
            act.activation(sp_, sp_, ACT.Ln, bias=1.0).then_inc(st.up(ln1p_ready), 1)

        def weights(batch):
            act.wait_ge(sw_arg.sem, st.at(sw_arg, batch + 1))
            act.activation(sw, zs, ACT.Exp).then_inc(st.up(sw_ready), 1)

        def save_sb(batch):
            for t in range(TT):
                save(f"s{'AB'[batch]}{t}", ao[:, t, batch * S:(batch + 1) * S], 0, S)

        softplus_parts(0)
        weights(0)
        softplus_parts(1)
        save("y0", yT[:, 0, :], 0, S)
        save("y1", yT[:, 1, :], 0, S)
        save_sb(0)
        weights(1)
        save("y2", yT[:, 2, :], 0, S)
        save_sb(1)
        save("y3", yT[:, 3, :], 0, S)
        act_split(st, act, TILES2, SPLITS2, "sbo0")
        act.wait_ge(ygelu_arg.sem, st.at(ygelu_arg, 1))
        act.activation(ge, ge, ACT.Sigmoid, scale=2.0 * (2.0 / np.pi) ** 0.5).then_inc(st.up(ygelu_gate), 1)
        for n in range(2):
            b, nth = wide_.next(f"glu{n}")
            act.wait_ge(wide_.ready.sem, st.at(wide_.ready, nth))
            for u in range(2):
                blk = 2 * n + u
                if blk == 0:
                    act.wait_ge(ygelu_ready.sem, st.at(ygelu_ready, 1))
                act.activation(ge[:, blk * S:(blk + 1) * S], b[:, u * S:(u + 1) * S], ACT.Sigmoid,
                               bias=b_col[:, blk:blk + 1]) \
                    .then_inc(st.up(wide_.saved if u else act_step), 1)
        act_split(st, act, TILES2, SPLITS2, "sbo1")
        act_split(st, act, TILES2, SPLITS2, "A.ff1.0")
        ln_statistics(aux_.saved, (aux_.nth_save("A.out2"), aux_.nth_save("A.out3")))
        act_mlp(st, act, wide_, "A.", TILES2, SPLITS2)
        ln_statistics(ff2_saved, (2, 4))
        save("qi", flat(qiT))
        b, nth = wide_.next("kiw")
        act.wait_ge(wide_.ready.sem, st.at(wide_.ready, nth))
        act.wait_ge(kiz_zero.sem, st.at(kiz_zero, 1))
        for hl in range(4):
            act.activation(kiz[32 * hl:32 * hl + 32, hl, :], b[0:32, 0:S], ACT.Copy).then_inc(st.up(act_step), 1)
        act.activation(wi, b[:, S:S + 16], ACT.Copy, scale=IDX_DIM ** -0.5 * IDX_HEADS ** -0.5) \
            .then_inc(st.up(wide_.saved), 1)

        def index_relu(t):
            act.wait_ge(idx_ready.sem, st.at(idx_ready, t + 1))
            if t:
                act.wait_ge(idx_summed.sem, st.at(idx_summed, 1))
            n = IDX_HEADS * (t + 1) * P
            act.activation(relu_[:, 0:n], scores[:, 0:n], ACT.Relu).then_inc(st.up(idx_relu), 1)

        index_relu(0)
        b, nth = wide_.next("dk")
        act.wait_ge(wide_.ready.sem, st.at(wide_.ready, nth))
        for f in range(2):
            src = b[64 * f:64 * f + 64, :].rearrange("p (u t) -> p u t", t=S)
            for r in range(2):
                act.activation(dkT[64 * r:64 * r + 64].rearrange("p (u f) t -> p f u t", f=2)[:, f], src, ACT.Copy) \
                    .then_inc(st.up(wide_.saved if f == r == 1 else act_step), 1)
        save("dv", flat(dv))
        index_relu(1)
        for n in range(4):
            save(f"dq{n}", flat(dqT[:, 2 * n:2 * n + 2, :]), scale=DH ** -0.5)

        def dsa_exp(b):
            nh = DSA_BATCHES[b][2]
            act.wait_ge(dmax_ready.sem, st.at(dmax_ready, b + 1))
            e = rows[:, :].rearrange("p (i n) -> p i n", i=nh)
            for n in range(nh):
                act.activation(e[:, n, :], e[:, n, :], ACT.Exp, bias=mx[:, n:n + 1],
                                     accum_out=sums[:, n:n + 1]) \
                    .then_inc(st.up(dexp_ready if n == nh - 1 else act_step), 1)

        dsa_exp(0)
        dsa_o = [dob[:, 0, 0:512], dob[:, 0, 512:1024], dob[:, 1, 0:512], dob[:, 1, 512:1024]]
        save("do0", dsa_o[0])
        save("do1", dsa_o[1])
        dsa_exp(1)
        save("do2", dsa_o[2])
        dsa_exp(2)
        act_split(st, act, TILES2, SPLITS2, "dso0")
        save("do3", dsa_o[3])
        act_split(st, act, TILES2, SPLITS2, "dso1")
        act_split(st, act, TILES2, SPLITS2, "B.ff1.0")
        ln_statistics(aux_.saved, (aux_.nth_save("B.out2"), aux_.nth_save("B.out3")))
        act_mlp(st, act, wide_, "B.", TILES2, SPLITS2)
        ln_statistics(ff2_saved, (6, 8))

    def dve_tail(dve, st):
        wide_, aux_ = wide.again(WIDE2), aux.again(AUX2)

        def tt(o, a, b, op):
            return dve.tensor_tensor(o, a, b, op)

        def tsc(o, a, s1, op0, s2=None, op1=None):
            return dve.tensor_scalar(o, a, s1, s2, op0, op1) if op1 else dve.tensor_scalar(o, a, s1, None, op0)

        def stt(o, a, s1, b, op0, op1):
            return dve.scalar_tensor_tensor(out=o, in0=a, scalar=s1, in1=b, op0=op0, op1=op1)

        def copy(o, a):
            return dve.tensor_copy(o, a)

        def save_turned(names):
            for n, name in enumerate(names):
                t, half = divmod(n, 2)
                b, nth = aux_.next(name)
                dve.wait_ge(aux_.ready.sem, st.at(aux_.ready, nth))
                copy(hT[:, 4 * half:4 * half + 4, t * P:(t + 1) * P], b.rearrange("p (k t) -> p k t", t=P)) \
                    .then_inc(st.up(aux_.saved), 1)

        def split_turned(names):
            for n, name in enumerate(names):
                t, half = divmod(n, 2)
                b, nth = aux_.next(name)
                dve.wait_ge(aux_.ready.sem, st.at(aux_.ready, nth))
                hi, lo = (v[:, 4 * half:4 * half + 4, t * P:(t + 1) * P] for v in (ht_hi, ht_lo))
                b4 = b.rearrange("p (k t) -> p k t", t=P)
                copy(hi, b4).then_inc(st.up(dve_step), 1)
                dve.wait_ge(st.last.sem, st.reached())
                tt(lo, b4, hi.bitcast(F32), ALU.subtract).then_inc(st.up(aux_.saved), 1)

        def add_projected(names):
            for name in names:
                c, t = divmod(int(name[-1]), 2)
                b, nth = aux_.next(name)
                dve.wait_ge(aux_.ready.sem, st.at(aux_.ready, nth))
                xv = x[:, t, c * BANK:(c + 1) * BANK]
                stt(xv, xv, ALPHA, b, ALU.mult, ALU.add).then_inc(st.up(aux_.saved), 1)

        def add_mlp(first):
            for n in range(4):
                t, c = divmod(n, 2)
                dve.wait_ge(ff2_ready.sem, st.at(ff2_ready, first + n + 1))
                xv = x[:, t, c * BANK:(c + 1) * BANK]
                stt(xv, xv, ALPHA, scores[:, n * BANK:(n + 1) * BANK], ALU.mult, ALU.add).then_inc(st.up(ff2_saved), 1)

        def layer_norm(n):
            dve.wait_ge(ln_in.sem, st.at(ln_in, 32 * n))
            for t in range(TT):
                xt = x[:, t, :]
                dve.wait_ge(ln_stats.sem, st.at(ln_stats, 2 * n - 1 + t))
                tsc(xt, xt, lmu[:, t:t + 1], ALU.add, lrr[:, t:t + 1], ALU.mult).then_inc(st.up(dve_step), 1)
                dve.wait_ge(st.last.sem, st.reached())
                tt(xt, xt, ln_g, ALU.mult).then_inc(st.up(dve_step), 1)
                dve.wait_ge(st.last.sem, st.reached())
                tt(xt, xt, ln_b, ALU.add).then_inc(st.up(ln_done), 1)

        save_turned([f"A.x{n}" for n in range(4)])
        dve.memset(part(4096, 1024), 0.0).then_inc(st.up(dve_step), 1)
        dve.memset(part(6144, 1024), 0.0).then_inc(st.up(dve_step), 1)
        dve.wait_ge(st.last.sem, st.reached())
        for ri in range(2):
            b, nth = aux_.next(f"ct{ri}")
            dve.wait_ge(aux_.ready.sem, st.at(aux_.ready, nth))
            for u in range(2):
                r = slice(64 * u, 64 * u + 64)
                o = CT[r, ri].rearrange("p i (j u c) -> p (i j) u c", u=2, c=SSM_C)[:, :, u, :]
                v = b[r, :].rearrange("p (j u c) -> p j u c", u=2, c=SSM_C)[:, :, u, :]
                tsc(o, v, -1.0 if ri else 1.0, ALU.mult).then_inc(st.up(aux_.saved if u else dve_step), 1)
        R = [prow[:, n, :] for n in range(18)]
        dve.wait_ge(dt_ready.sem, st.at(dt_ready, 1))
        for o, a in ((P_Y, P_LR), (P_TH, P_LI)):
            tt(R[o].rearrange("p (u n) -> p u n", u=2), R[a].rearrange("p (u n) -> p u n", u=2), bc(dt, 2, SSM_N), ALU.mult) \
                .then_inc(st.up(dve_step), 1)
        dve.wait_ge(st.last.sem, st.reached())
        tsc(R[P_Y], R[P_Y], -80.0, ALU.max, 80.0, ALU.min).then_inc(st.up(dve_step), 1)
        dve.wait_ge(st.last.sem, st.reached())
        tsc(R[P_W], R[P_Y], 1.0 / 256, ALU.mult).then_inc(st.up(dve_step), 1)
        dve.wait_ge(st.last.sem, st.reached())
        tsc(R[P_E], R[P_W], 1.0 / 7, ALU.mult, 1.0, ALU.add).then_inc(st.up(dve_step), 1)
        for n in range(6, 1, -1):
            dve.wait_ge(st.last.sem, st.reached())
            tt(R[P_E], R[P_E], R[P_W], ALU.mult).then_inc(st.up(dve_step), 1)
            dve.wait_ge(st.last.sem, st.reached())
            tsc(R[P_E], R[P_E], 1.0 / n, ALU.mult, 1.0, ALU.add).then_inc(st.up(dve_step), 1)
        dve.wait_ge(st.last.sem, st.reached())
        tt(R[P_E], R[P_E], R[P_W], ALU.mult).then_inc(st.up(dve_step), 1)
        for _ in range(8):
            dve.wait_ge(st.last.sem, st.reached())
            stt(R[P_E], R[P_E], 2.0, R[P_E], ALU.add, ALU.mult).then_inc(st.up(dve_step), 1)
        tsc(R[P_KQ], R[P_TH], 1.0 / TWO_PI, ALU.mult, ROUND, ALU.add).then_inc(st.up(dve_step), 1)
        dve.wait_ge(st.last.sem, st.reached())
        tsc(R[P_KQ], R[P_KQ], ROUND, ALU.subtract).then_inc(st.up(dve_step), 1)
        dve.wait_ge(st.last.sem, st.reached())
        stt(R[P_RED], R[P_KQ], -TURN[0], R[P_TH], ALU.mult, ALU.add).then_inc(st.up(dve_step), 1)
        for c in TURN[1:]:
            dve.wait_ge(st.last.sem, st.reached())
            stt(R[P_RED], R[P_KQ], -c, R[P_RED], ALU.mult, ALU.add).then_inc(st.up(dve_step), 1)
        dve.wait_ge(st.last.sem, st.reached())
        tsc(R[P_RED], R[P_RED], 0.5, ALU.mult).then_inc(st.up(dve_step), 1)
        dve.wait_ge(st.last.sem, st.reached())
        stt(R[P_HA], R[P_RED], -1.0, R[P_RED], ALU.mult, ALU.max).then_inc(st.up(sin_arg), 1)
        tsc(R[P_MAG], R[P_E], 1.0, ALU.add).then_inc(st.up(dve_step), 1)
        tt(R[P_DEN], R[P_LR], R[P_LR], ALU.mult).then_inc(st.up(dve_step), 1)
        tt(R[P_T1], R[P_LI], R[P_LI], ALU.mult).then_inc(st.up(dve_step), 1)
        dve.wait_ge(st.last.sem, st.reached())
        tt(R[P_DEN], R[P_DEN], R[P_T1], ALU.add).then_inc(st.up(dve_step), 1)
        dve.wait_ge(st.last.sem, st.reached())
        dve.reciprocal(R[P_DEN], R[P_DEN]).then_inc(st.up(dve_step), 1)
        dve.wait_ge(sin_ready.sem, st.at(sin_ready, 1))
        stt(R[P_SIN], R[P_SN], 2.0, R[P_CS], ALU.mult, ALU.mult).then_inc(st.up(dve_step), 1)
        stt(R[P_CM1], R[P_SN], -2.0, R[P_SN], ALU.mult, ALU.mult).then_inc(st.up(dve_step), 1)
        dve.wait_ge(st.last.sem, st.reached())
        tsc(R[P_COS], R[P_CM1], 1.0, ALU.add).then_inc(st.up(dve_step), 1)
        tt(R[P_ABI], R[P_MAG], R[P_SIN], ALU.mult).then_inc(st.up(dve_step), 1)
        dve.wait_ge(st.last.sem, st.reached())
        tt(R[P_NR], R[P_E], R[P_COS], ALU.mult).then_inc(st.up(dve_step), 1)
        dve.wait_ge(st.last.sem, st.reached())
        tt(R[P_NR], R[P_NR], R[P_CM1], ALU.add).then_inc(st.up(dve_step), 1)
        dve.wait_ge(st.last.sem, st.reached())
        for o, a, c, op in ((P_CR, P_LR, P_LI, ALU.add), (P_CI, P_LI, P_LR, ALU.subtract)):
            dve.wait_ge(st.last.sem, st.reached())
            tt(R[P_T1], R[P_NR], R[a], ALU.mult).then_inc(st.up(dve_step), 1)
            tt(R[P_T2], R[P_ABI], R[c], ALU.mult).then_inc(st.up(dve_step), 1)
            dve.wait_ge(st.last.sem, st.reached())
            if o == P_CR:
                tt(R[P_T1], R[P_T1], R[P_T2], op).then_inc(st.up(dve_step), 1)
            else:
                tt(R[P_T1], R[P_T2], R[P_T1], op).then_inc(st.up(dve_step), 1)
            dve.wait_ge(st.last.sem, st.reached())
            tt(R[o], R[P_T1], R[P_DEN], ALU.mult).then_inc(st.up(par_ready if o == P_CI else dve_step), 1)
        b, nth = aux_.next("par")
        dve.wait_ge(aux_.ready.sem, st.at(aux_.ready, nth))
        copy(tiny[:, 240:320], b[:, 0:80]).then_inc(st.up(dve_step), 1)
        copy(d_col, b[:, 80:84]).then_inc(st.up(dve_step), 1)
        copy(b_col, b[:, 84:88]).then_inc(st.up(aux_.saved), 1)
        dve.wait_ge(st.last.sem, st.reached())
        cr, ci, mag, cost, sint = (pcol[:, n, :] for n in range(5))
        dve.wait_ge(b_in.sem, st.at(b_in, 32))
        v1, v2 = (v[:, 0:256].rearrange("p (j c) -> p j c", c=SSM_C) for v in (t1, t2))
        for ri, (a, c, op) in enumerate(((cr, ci, ALU.subtract), (ci, cr, ALU.add))):
            dve.wait_ge(st.last.sem, st.reached())
            tt(v1, bin_[:, 0], bc(a, 2, SSM_C), ALU.mult).then_inc(st.up(dve_step), 1)
            tt(v2, bin_[:, 1], bc(c, 2, SSM_C), ALU.mult).then_inc(st.up(dve_step), 1)
            dve.wait_ge(st.last.sem, st.reached())
            for u in range(2):
                r = slice(64 * u, 64 * u + 64)
                tt(BD[r, ri, :, u, :], v1[r], v2[r], op).then_inc(st.up(bd_ready if ri == u == 1 else dve_step), 1)
        dve.wait_ge(st.last.sem, st.reached())
        dve.memset(ctab[:, :, 0:1], 1.0).then_inc(st.up(dve_step), 1)
        dve.memset(stab[:, :, 0:1], 0.0).then_inc(st.up(dve_step), 1)
        copy(cm, cost).then_inc(st.up(dve_step), 1)
        copy(sm, sint).then_inc(st.up(dve_step), 1)
        m = 1
        while m < S:
            a = scr[:, 0:SJ * m].rearrange("p (j t) -> p j t", t=m)
            c = part(8704, SJ * m, "p (j t) -> p j t", t=m)
            for o, p, q, op in ((ctab, cm, sm, ALU.subtract), (stab, sm, cm, ALU.add)):
                dve.wait_ge(st.last.sem, st.reached())
                tt(a, ctab[:, :, 0:m], bc(p, 2, m), ALU.mult).then_inc(st.up(dve_step), 1)
                tt(c, stab[:, :, 0:m], bc(q, 2, m), ALU.mult).then_inc(st.up(dve_step), 1)
                dve.wait_ge(st.last.sem, st.reached())
                tt(o[:, :, m:2 * m], a, c, op).then_inc(st.up(dve_step), 1)
            tt(cn, cm, cm, ALU.mult).then_inc(st.up(dve_step), 1)
            tt(sn2, sm, sm, ALU.mult).then_inc(st.up(dve_step), 1)
            dve.wait_ge(st.last.sem, st.reached())
            stt(sm, sm, 2.0, cm, ALU.mult, ALU.mult).then_inc(st.up(dve_step), 1)
            dve.wait_ge(st.last.sem, st.reached())
            tt(cm, cn, sn2, ALU.subtract).then_inc(st.up(dve_step), 1)
            m *= 2
        for ri in range(2):
            b, nth = aux_.next(f"bt{ri}")
            dve.wait_ge(aux_.ready.sem, st.at(aux_.ready, nth))
            copy(flat(BT[:, ri]), b).then_inc(st.up(aux_.saved), 1)

        def softplus(batch):
            dve.wait_ge(ln1p_ready.sem, st.at(ln1p_ready, batch + 1))
            v = scores.rearrange("p (h n) -> p h n", n=BANK)[:, :, 0:384]
            stt(sp_, v, 0.0, sp_, ALU.max, ALU.add).then_inc(st.up(dve_step), 1)
            dve.wait_ge(st.last.sem, st.reached())
            d = sp_.rearrange("p h (b t) -> p h b t", t=P)
            for n in (0, 2):
                tt(d[:, :, n, :], d[:, :, n, :], bc(K["strict_keep"], 1, 4), ALU.mult) \
                    .then_inc(st.up(sp_ready if n else dve_step), 1)

        def log_weights(batch):
            for hl in range(4):
                b, nth = aux_.next(f"cs{4 * batch + hl}")
                dve.wait_ge(aux_.ready.sem, st.at(aux_.ready, nth))
                tt(zs[:, hl, :], zs[:, hl, :], b[:, 0:384], ALU.subtract).then_inc(st.up(aux_.saved), 1)
            dve.wait_ge(st.last.sem, st.reached())
            d = zs.rearrange("p h (b t) -> p h b t", t=P)
            for n in (0, 2):
                tt(d[:, :, n, :], d[:, :, n, :], bc(K["strict_add"], 1, 4), ALU.add) \
                    .then_inc(st.up(sw_arg if n else dve_step), 1)

        def scan(j):
            b, nth = aux_.next(f"bu{j}")
            dve.wait_ge(aux_.ready.sem, st.at(aux_.ready, nth))
            b2 = b.rearrange("p (r t) -> p r t", r=2)
            if j >= 2 and j - 2 not in TURNED_BY_DVE:
                signal, n = states(j - 2)
                dve.wait_ge(signal.sem, st.at(signal, n))
            v1, v2 = (v.rearrange("p (r t) -> p r t", r=2) for v in (t1, t2))
            dve.wait_ge(st.last.sem, st.reached())
            tt(v1, b2, bc(ctab[:, j, :], 1, 2), ALU.mult).then_inc(st.up(dve_step), 1)
            tt(v2, b2, bc(stab[:, j, :], 1, 2), ALU.mult).then_inc(st.up(aux_.saved), 1)
            dve.wait_ge(st.last.sem, st.reached())
            tt(v1[:, 0], v1[:, 0], v2[:, 1], ALU.add).then_inc(st.up(dve_step), 1)
            tt(v1[:, 1], v1[:, 1], v2[:, 0], ALU.subtract).then_inc(st.up(dve_step), 1)
            dve.wait_ge(st.last.sem, st.reached())
            for ri in range(2):
                dve.tensor_tensor_scan(wst[j % 2][:, ri * S:(ri + 1) * S], mag[:, j:j + 1].broadcast_to([P, S]),
                                             v1[:, ri], 0.0, ALU.mult, ALU.add) \
                    .then_inc(st.up(scan_ready if ri else dve_step), 1)
            if j in TURNED_BY_DVE:
                w, o = (v.rearrange("p (r t) -> p r t", r=2) for v in (wst[j % 2], xst[j % len(xst)]))
                dve.wait_ge(st.last.sem, st.reached())
                tt(v1, w, bc(ctab[:, j, :], 1, 2), ALU.mult).then_inc(st.up(dve_step), 1)
                tt(v2, w, bc(stab[:, j, :], 1, 2), ALU.mult).then_inc(st.up(dve_step), 1)
                dve.wait_ge(st.last.sem, st.reached())
                if j >= len(xst):
                    signal, n = place_free(wide_, j)
                    dve.wait_ge(signal.sem, st.at(signal, n))
                tt(o[:, 0], v1[:, 0], v2[:, 1], ALU.subtract).then_inc(st.up(dve_step), 1)
                tt(o[:, 1], v1[:, 1], v2[:, 0], ALU.add).then_inc(st.up(state_dve), 1)

        for j in range(SJ):
            scan(j)
            if j == 1:
                softplus(0)
            if j == 3:
                log_weights(0)
            if j == 5:
                softplus(1)
            if j == 8:
                log_weights(1)
        dve.wait_ge(wide_.saved.sem, st.at(wide_.saved, wide_.nth_save("y3")))
        for k in range(4):
            stt(yT[:, k, :], uT[:, k, :], d_col[:, k:k + 1], yT[:, k, :], ALU.mult, ALU.add).then_inc(st.up(dve_step), 1)
        dve.wait_ge(st.last.sem, st.reached())
        y1 = yT.rearrange("p b t -> p (b t)")
        tt(ge, y1, y1, ALU.mult).then_inc(st.up(dve_step), 1)
        dve.wait_ge(st.last.sem, st.reached())
        tsc(ge, ge, 0.044715, ALU.mult, 1.0, ALU.add).then_inc(st.up(dve_step), 1)
        dve.wait_ge(st.last.sem, st.reached())
        tt(ge, ge, y1, ALU.mult).then_inc(st.up(ygelu_arg), 1)
        dve.wait_ge(ygelu_gate.sem, st.at(ygelu_gate, 1))
        tt(y1, y1, ge, ALU.mult).then_inc(st.up(ygelu_ready), 1)
        for t in range(TT):
            b, nth = aux_.next(f"ao{t}")
            dve.wait_ge(aux_.ready.sem, st.at(aux_.ready, nth))
            hi, lo = (v[:, 0:4, t * P:(t + 1) * P] for v in (ht_hi, ht_lo))
            b4 = b.rearrange("p (k t) -> p k t", t=P)
            copy(hi, b4).then_inc(st.up(dve_step), 1)
            dve.wait_ge(st.last.sem, st.reached())
            tt(lo, b4, hi.bitcast(F32), ALU.subtract).then_inc(st.up(aux_.saved), 1)
        dve.wait_ge(wide_.saved.sem, st.at(wide_.saved, wide_.nth_save("glu1")))
        tt(y1, y1, ge, ALU.mult).then_inc(st.up(dve_step), 1)
        dve.wait_ge(st.last.sem, st.reached())
        copy(ht_hi[:, 4:8, :], yT).then_inc(st.up(dve_step), 1)
        dve.wait_ge(st.last.sem, st.reached())
        tt(ht_lo[:, 4:8, :], yT, ht_hi[:, 4:8, :].bitcast(F32), ALU.subtract).then_inc(st.up(y_ready), 1)
        add_projected([f"A.out{n}" for n in range(2)])
        lower_split(st, dve, TILES2, SPLITS2, "A.ff1.0")
        add_projected([f"A.out{n}" for n in range(2, 4)])
        layer_norm(1)
        split_turned([f"A.n{n}" for n in range(4)])
        dve_mlp(st, dve, "A.", TILES2, SPLITS2)
        add_mlp(0)
        dve.memset(part(4096, 1024), 0.0).then_inc(st.up(kiz_zero), 1)
        layer_norm(2)
        save_turned([f"B.x{n}" for n in range(4)])

        def top_keys(t):
            keys = (t + 1) * P
            v = slice(0, P) if t == 0 else slice(P, 384)
            s, r, a = isc[:, v], irep[:, v], iadd[:, v]
            dve.wait_ge(idx_relu.sem, st.at(idx_relu, t + 1))
            rl = relu_[:, 0:IDX_HEADS * keys].rearrange("p (h n) -> p h n", n=keys)
            tsc(s, rl[:, 0, :], wi[:, 8 * t:8 * t + 1], ALU.mult).then_inc(st.up(dve_step), 1)
            for h in range(1, IDX_HEADS):
                dve.wait_ge(st.last.sem, st.reached())
                stt(s, rl[:, h, :], wi[:, 8 * t + h:8 * t + h + 1], s, ALU.mult, ALU.add) \
                    .then_inc(st.up(idx_summed if h == IDX_HEADS - 1 else dve_step), 1)
            dve.wait_ge(st.last.sem, st.reached())
            d = s[:, t * P:(t + 1) * P]
            tt(d, d, K["causal"], ALU.add).then_inc(st.up(dve_step), 1)
            for n in range(TOPK // 8):
                dve.wait_ge(st.last.sem, st.reached())
                dve.max(m8, r if n else s).then_inc(st.up(dve_step), 1)
                dve.wait_ge(st.last.sem, st.reached())
                dve.match_replace(r, m8, r if n else s, TAKEN).then_inc(st.up(dve_step), 1)
            dve.wait_ge(st.last.sem, st.reached())
            tsc(a, r, TAKEN, ALU.is_equal, -MASKED, ALU.mult).then_inc(st.up(dve_step), 1)
            dve.wait_ge(st.last.sem, st.reached())
            tsc(a, a, MASKED, ALU.add).then_inc(st.up(dve_step), 1)
            dve.wait_ge(st.last.sem, st.reached())
            d = a[:, t * P:(t + 1) * P]
            tt(d, d, K["causal"], ALU.add).then_inc(st.up(dve_step), 1)

        top_keys(0)
        top_keys(1)

        def logits(b):
            t, _, nh = DSA_BATCHES[b]
            view, keys = dsa_view(b)
            dve.wait_ge(dsc_ready.sem, st.at(dsc_ready, b + 1))
            if b:
                dve.wait_ge(aux_.saved.sem, st.at(aux_.saved, aux_.nth_save(f"pt{b - 1}.3")))
            e = rows[:, :].rearrange("p (i n) -> p i n", n=keys)
            hs = slots(b)
            for n, h in enumerate(hs):
                slope = float(np.float32(2.0 ** (-8.0 * (h + 1) / DSA_HEADS)))
                stt(e[:, n, :], K["rel"][:, S - keys:S], slope, view[:, n, :], ALU.mult, ALU.add) \
                    .then_inc(st.up(dsc_read if n == nh - 1 else dve_step), 1)
            dve.wait_ge(st.last.sem, st.reached())
            tt(e, e, bc(iadd[:, 0:P] if t == 0 else iadd[:, P:384], 1, nh), ALU.add).then_inc(st.up(dve_step), 1)
            dve.wait_ge(st.last.sem, st.reached())
            dve.tensor_reduce(mx[:, 0:nh], e, AX_X, ALU.max, negate=True).then_inc(st.up(dmax_ready), 1)

        def probabilities(b):
            _, _, nh = DSA_BATCHES[b]
            _, keys = dsa_view(b)
            dve.wait_ge(dexp_ready.sem, st.at(dexp_ready, b + 1))
            dve.reciprocal(wts[:, 0:nh], sums[:, 0:nh]).then_inc(st.up(dve_step), 1)
            dve.wait_ge(st.last.sem, st.reached())
            e = rows[:, :].rearrange("p (i n) -> p i n", n=keys)
            tt(e, e, bc(wts[:, 0:nh], 2, keys), ALU.mult).then_inc(st.up(dprobs_ready), 1)

        for b in range(3):
            logits(b)
            probabilities(b)
            if b:
                dve.wait_ge(wide_.saved.sem, st.at(wide_.saved, wide_.nth_save(f"do{b}")))
            for n in range(4):
                bk, nth = aux_.next(f"pt{b}.{n}")
                dve.wait_ge(aux_.ready.sem, st.at(aux_.ready, nth))
                copy(scr[:, n * BANK:(n + 1) * BANK], bk).then_inc(st.up(aux_.saved), 1)
        split_turned([f"do{n}" for n in range(4)])
        add_projected([f"B.out{n}" for n in range(2)])
        lower_split(st, dve, TILES2, SPLITS2, "B.ff1.0")
        add_projected([f"B.out{n}" for n in range(2, 4)])
        layer_norm(3)
        split_turned([f"B.n{n}" for n in range(4)])
        dve_mlp(st, dve, "B.", TILES2, SPLITS2)
        add_mlp(4)
        layer_norm(4)

    def pool_tail(pool, st):
        wide_, aux_ = wide.again(WIDE2), aux.again(AUX2)
        pool.wait_ge(aux_.saved.sem, st.at(aux_.saved, aux_.nth_save("bt1")))
        for j in range(SJ):
            if j in TURNED_BY_DVE:
                continue
            pool.wait_ge(scan_ready.sem, st.at(scan_ready, j + 1))
            w, o = (v.rearrange("p (r t) -> p r t", r=2) for v in (wst[j % 2], xst[j % len(xst)]))
            v1, v2 = (v.rearrange("p (r t) -> p r t", r=2) for v in (pu1, pu2))
            if j:
                pool.wait_ge(st.last.sem, st.reached())
            pool.tensor_tensor(v1, w, bc(ctab[:, j, :], 1, 2), ALU.mult).then_inc(st.up(pool_step), 1)
            pool.tensor_tensor(v2, w, bc(stab[:, j, :], 1, 2), ALU.mult).then_inc(st.up(pool_step), 1)
            pool.wait_ge(st.last.sem, st.reached())
            if j >= len(xst):
                signal, n = place_free(wide_, j)
                pool.wait_ge(signal.sem, st.at(signal, n))
            pool.tensor_tensor(o[:, 0], v1[:, 0], v2[:, 1], ALU.subtract).then_inc(st.up(pool_step), 1)
            pool.tensor_tensor(o[:, 1], v1[:, 1], v2[:, 0], ALU.add).then_inc(st.up(state_pool), 1)
        for name in ("sbo0", "sbo1", "dso0", "dso1"):
            lower_split(st, pool, TILES2, SPLITS2, name)

    @block.sync
    def _(sp):
        sp.dma_start(x[:, :, :], I["x"][0].rearrange("(t p) n -> p t n", p=P)).then_inc(x_in.sem, 16)
        sp.dma_start(const[:, :], I["const"]).then_inc(const_in.sem, 16)
        with sp.Fori(0, DEPTH) as i:
            where = Where(i)

            def src(name):
                return I[name][bass.ds(i, 1)].rearrange("o a b -> (o a) b")

            def vec(name):
                return I[name][bass.ds(i, 1)]

            sp.wait_ge(small_used.sem, i * small_used.per_layer + 1)
            small = [(vec_rows[8 * n:8 * n + 8, :], vec(v).rearrange("o (k p) -> (o k) p", p=P))
                     for n, v in enumerate(("norm_mix", "norm_mlp", "norm_ple"))]
            for n, v in ((C_Q, "nsa_q_norm"), (C_K, "nsa_k_norm")):
                for u in range(2):
                    small.append((vec_rows[n:n + 1, u * DH:(u + 1) * DH], vec(v)))
            for n, v in enumerate(("cmp_pos_k", "cmp_pos_v")):
                small.append((vec_rows[C_POS + 16 * n:C_POS + 16 * n + 16, :],
                              src(v).rearrange("(j l) d -> j (l d)", l=2)))
            for n, v in enumerate(("cmp_w2_k", "cmp_w2_v")):
                small.append((w2[:, n], src(v).rearrange("(h p) d -> p h d", p=P)))
            for dst, s in small[:9]:
                sp.dma_start(dst, s).then_inc(small_in.sem, 16)
            for n, name in enumerate(TILES):
                if n == RING:
                    for dst, s in small[9:]:
                        sp.dma_start(dst, s).then_inc(late_in.sem, 16)
                    sp.dma_start(p_sb[:, :, :], I["p"][bass.ds(i, 1)].rearrange("o b s n -> (o b s) n")
                                 .rearrange("(t p) n -> p t n", p=P)).then_inc(late_in.sem, 16)
                sp.wait_ge(tile_used.sem, where.value(tile_used, n + 1))
                kind, _, num = name.partition(".")
                if name.startswith("in"):
                    c = int(name[2:])
                    m = min(BANK, D_IN - c * BANK)
                    s, k = src("w_in")[:, c * BANK:c * BANK + m], KT
                elif name in ("w1k", "w1v"):
                    s, k, m = src("cmp_w1_" + name[2]), 16, CMP_HID
                elif name in ("up_nsa", "up_ret"):
                    s, k, m = src("w_" + name), 4, D
                elif kind == "ff1":
                    s, k, m = src("w_ff1")[:, int(num) * BANK:(int(num) + 1) * BANK], KT, BANK
                elif kind == "ff2":
                    s, k, m = src("w_ff2")[int(num) * BANK:(int(num) + 1) * BANK, :], 4, D
                elif name == "ple":
                    s, k, m = src("w_ple"), 2, D
                else:
                    c = int(name[-1])
                    s = src("w_out" if name.startswith("out") else "w_ple_gate")[:, c * BANK:(c + 1) * BANK]
                    k, m = KT, BANK
                sp.dma_start(w_tile(n, (k, m)), s.rearrange("(k p) n -> p k n", p=P)) \
                    .then_inc(tile_in[n % RING].sem, 16)
        sp_tail(sp)

    @block.tensor
    def _(pe):
        pe.sem_inc(tile_used.sem, RING)
        pe.wait_ge(const_in.sem, 16)
        pe.wait_ge(x_in.sem, 16)
        with pe.Fori(0, DEPTH) as i:
            st = Steps(Where(i))
            pe_layer(pe, st)
            st.check()
        pe_tail(pe, Steps(Where()))

    @block.scalar
    def _(act):
        act.sem_inc(wide.saved.sem, 2)
        act.wait_ge(eps_set.sem, 3)
        act.wait_ge(x_in.sem, 16)
        with act.Fori(0, DEPTH) as i:
            st = Steps(Where(i))
            act_layer(act, st)
            st.check()
        act_tail(act, Steps(Where()))

    @block.vector
    def _(dve):
        dve.sem_inc(aux.saved.sem, 2)
        dve.memset(part(10784, 64), 0.0).then_inc(zero_set.sem, 1)
        dve.wait_ge(zero_set.sem, 1)
        dve.memset(vec_rows, 0.0).then_inc(small_used.sem, 1)
        for n, v in enumerate((EPS, LN_EPS, np.pi / 2)):
            dve.memset(eps_tile[:, n:n + 1], float(v)).then_inc(eps_set.sem, 1)
        dve.wait_ge(const_in.sem, 16)
        dve.wait_ge(x_in.sem, 16)
        with dve.Fori(0, DEPTH) as i:
            st = Steps(Where(i))
            dve_layer(dve, st)
            st.check()
        dve_tail(dve, Steps(Where()))

    @block.gpsimd
    def _(pool):
        pool.wait_ge(const_in.sem, 16)
        with pool.Fori(0, DEPTH) as i:
            st = Steps(Where(i))
            pool_layer(pool, st)
            st.check()
        pool_tail(pool, Steps(Where()))


NAMES = ["x", "p", "norm_mix", "w_in", "nsa_q_norm", "nsa_k_norm", "cmp_pos_k", "cmp_pos_v", "cmp_w1_k", "cmp_w2_k",
         "cmp_w1_v", "cmp_w2_v", "w_up_nsa", "w_up_ret", "w_out", "norm_mlp", "w_ff1", "w_ff2", "norm_ple", "w_ple",
         "w_ple_gate", "sb_ssm_w_in_2", "ssm_log_dt_2", "ssm_lam_re_2", "ssm_lam_im_2", "ssm_b_re_2", "ssm_b_im_2",
         "ssm_c_re_2", "ssm_c_im_2", "ssm_d_2", "ssm_w_glu_2", "ssm_b_glu_2", "sb_ssm_w_out_2", "dsa_w_in_2",
         "dsa_w_out_2", "ln_mix_g_2", "ln_mix_b_2", "ln_ffn_g_2", "ln_ffn_b_2", "mlp_w1_2", "mlp_w2_2"]


def kernel(**inputs):
    import concourse.bacc as bacc
    from concourse.bass_utils import run_bass_kernel_spmd

    nc = bacc.Bacc("TRN2", target_bir_lowering=False, num_devices=1)
    arrays = {f"in_{name}": np.ascontiguousarray(inputs[name]) for name in NAMES}
    arrays["in_const"] = constants()
    I = {name[3:]: nc.dram_tensor(name, a.shape, mybir.dt.from_np(a.dtype), kind="ExternalInput").ap()
         for name, a in arrays.items()}
    out = nc.dram_tensor("out", (1, S, D), F32, kind="ExternalOutput").ap()
    build(nc, I, out)
    return run_bass_kernel_spmd(nc, [arrays], core_ids=[0]).results[0]["out"]
```
